# Optimizing a Trainium2 kernel written in Bass

```python
import math
import jax, jax.numpy as jnp
from jax import lax
import numpy as np

D_MODEL = 1024
BATCH = 1
SEQ = 512
DEPTH = 1

CHUNK = 64
EPS = 1e-6
FOX_HEADS = 8
FOX_DH = 64
Q_BLOCK = 128
GDN_HEADS = 4
GDN_DK = 128
GDN_DV = 128
CONV_W = 4
PEER_HEADS = 8
N_KEYS = 128
N_EXPERTS = N_KEYS * N_KEYS
PEER_DQ = 256
PEER_TOPK = 16
PEER_BLOCK = 128

FOX_W = FOX_HEADS * FOX_DH
GDN_KW = GDN_HEADS * GDN_DK
GDN_VW = GDN_HEADS * GDN_DV
SPLITS = (FOX_W, FOX_W, FOX_W, FOX_HEADS, GDN_KW, GDN_KW, GDN_VW, GDN_VW, GDN_HEADS, GDN_HEADS, D_MODEL, D_MODEL)
IN_W = sum(SPLITS)

kernel_name = "hybrid_fox_gdn_peer_block"

def rms_norm(x, g):
    xf = x.astype(jnp.float32)
    y = xf * lax.rsqrt(jnp.mean(xf * xf, axis=-1, keepdims=True) + EPS)
    return (y * g.astype(jnp.float32)).astype(x.dtype)

def l2_norm(t):
    tf = t.astype(jnp.float32)
    return tf * lax.rsqrt(jnp.sum(tf * tf, axis=-1, keepdims=True) + EPS)

def forgetting_attention(q, k, v, log_f):
    B, S, H, dh = q.shape
    nb = S // Q_BLOCK
    cum = jnp.cumsum(log_f.astype(jnp.float32), axis=1).transpose(0, 2, 1)
    kh = k.transpose(0, 2, 1, 3)
    vh = v.transpose(0, 2, 1, 3)
    qb = q.reshape(B, nb, Q_BLOCK, H, dh).transpose(1, 0, 3, 2, 4)
    cq = cum.reshape(B, H, nb, Q_BLOCK).transpose(2, 0, 1, 3)
    pos_k = jnp.arange(S)
    scale = dh ** -0.5

    def block(args):
        i, qi, ci = args
        s = jnp.einsum('bhqd,bhkd->bhqk', qi, kh).astype(jnp.float32) * scale
        s = s + ci[..., :, None] - cum[..., None, :]
        pos_q = i * Q_BLOCK + jnp.arange(Q_BLOCK)
        mask = pos_k[None, :] <= pos_q[:, None]
        s = jnp.where(mask, s, -jnp.inf)
        p = jax.nn.softmax(s, axis=-1).astype(vh.dtype)
        return jnp.einsum('bhqk,bhkd->bhqd', p, vh)

    o = lax.map(block, (jnp.arange(nb), qb, cq))
    return o.transpose(1, 0, 3, 2, 4).reshape(B, S, H * dh)

def causal_short_conv(x, w):
    S = x.shape[1]
    xp = jnp.pad(x, ((0, 0), (CONV_W - 1, 0), (0, 0)))
    y = sum(w[i] * xp[:, i:i + S] for i in range(CONV_W))
    return jax.nn.silu(y)

def gated_delta_rule(q, k, v, g, beta):
    B, S, H, dk = q.shape
    dv = v.shape[-1]
    nc = S // CHUNK
    f32 = jnp.float32

    def chunked(t):
        t = t.reshape((B, nc, CHUNK, H) + t.shape[3:])
        return jnp.moveaxis(t, 3, 1)

    q = chunked(q.astype(f32)) * (dk ** -0.5)
    k = chunked(k.astype(f32))
    v = chunked(v.astype(f32))
    g = jnp.cumsum(chunked(g.astype(f32)), axis=-1)
    beta = chunked(beta.astype(f32))
    idx = jnp.arange(CHUNK)
    causal = idx[:, None] >= idx[None, :]
    strict = idx[:, None] > idx[None, :]
    diff = g[..., :, None] - g[..., None, :]
    decay = jnp.where(causal, jnp.exp(jnp.where(causal, diff, 0.0)), 0.0)
    kb = k * beta[..., None]
    L = jnp.where(strict, jnp.einsum('bhnid,bhnjd->bhnij', kb, k) * decay, 0.0)
    A = L + jnp.eye(CHUNK, dtype=f32)
    rhs = jnp.concatenate([v * beta[..., None], kb * jnp.exp(g)[..., None]], axis=-1)
    sol = lax.linalg.triangular_solve(A, rhs, left_side=True, lower=True, unit_diagonal=True)
    u, w = sol[..., :dv], sol[..., dv:]
    attn_intra = jnp.einsum('bhnid,bhnjd->bhnij', q, k) * decay
    q_dec = q * jnp.exp(g)[..., None]
    g_last = g[..., -1]
    k_dec = k * jnp.exp(g_last[..., None] - g)[..., None]
    xs = tuple(jnp.moveaxis(t, 2, 0) for t in (u, w, attn_intra, q_dec, k_dec, g_last))

    def step(state, inp):
        u_c, w_c, a_c, qd_c, kd_c, gl_c = inp
        v_new = u_c - jnp.einsum('bhcd,bhde->bhce', w_c, state)
        o_c = jnp.einsum('bhcd,bhde->bhce', qd_c, state) + jnp.einsum('bhij,bhje->bhie', a_c, v_new)
        state = state * jnp.exp(gl_c)[..., None, None] + jnp.einsum('bhcd,bhce->bhde', kd_c, v_new)
        return state, o_c

    s0 = jnp.zeros((B, H, dk, dv), f32)
    _, o = lax.scan(step, s0, xs)
    o = jnp.moveaxis(o, 0, 2)
    return jnp.moveaxis(o, 1, 3).reshape(B, S, H, dv)

def peer(h, w_query, keys1, keys2, expert_down, expert_up):
    B, S, D = h.shape
    nb = (B * S) // PEER_BLOCK
    xt = h.reshape(nb, PEER_BLOCK, D)

    def block(xb):
        qy = (xb @ w_query).reshape(PEER_BLOCK, PEER_HEADS, 2, PEER_DQ // 2)
        s1 = jnp.einsum('thd,kd->thk', qy[:, :, 0], keys1).astype(jnp.float32)
        s2 = jnp.einsum('thd,kd->thk', qy[:, :, 1], keys2).astype(jnp.float32)
        v1, i1 = lax.top_k(s1, PEER_TOPK)
        v2, i2 = lax.top_k(s2, PEER_TOPK)
        cand = (v1[..., :, None] + v2[..., None, :]).reshape(PEER_BLOCK, PEER_HEADS, PEER_TOPK * PEER_TOPK)
        cidx = (i1[..., :, None] * N_KEYS + i2[..., None, :]).reshape(PEER_BLOCK, PEER_HEADS, PEER_TOPK * PEER_TOPK)
        top_s, pos = lax.top_k(cand, PEER_TOPK)
        eidx = jnp.take_along_axis(cidx, pos, axis=-1)
        gates = jax.nn.softmax(top_s, axis=-1)
        u = expert_down[eidx]
        act = jax.nn.gelu(jnp.einsum('td,thkd->thk', xb, u).astype(jnp.float32), approximate=False)
        ve = expert_up[eidx]
        return jnp.einsum('thk,thkd->td', (gates * act).astype(xb.dtype), ve)

    return lax.map(block, xt).reshape(B, S, D)

def setup_inputs(seed: int = 0) -> dict:
    key = jax.random.key(seed)
    ks = jax.random.split(key, 24)
    f32 = jnp.float32
    D = D_MODEL

    def nrm(k, shape, scale):
        return jax.random.normal(k, shape, f32) * scale

    def gain(k, shape):
        return 1.0 + 0.01 * jax.random.normal(k, shape, f32)

    dt = jnp.exp(jax.random.uniform(ks[9], (DEPTH, GDN_HEADS), f32, math.log(1e-3), math.log(0.1)))
    return {
        "x": nrm(ks[0], (BATCH, SEQ, D), 1.0),
        "c": nrm(ks[1], (BATCH, D), 1.0),
        "w_ada": nrm(ks[2], (DEPTH, D, 6 * D), 0.5 * D ** -0.5),
        "b_ada": nrm(ks[3], (DEPTH, 6 * D), 0.02),
        "g_pre_mix": gain(ks[4], (DEPTH, D)),
        "g_post_mix": gain(ks[5], (DEPTH, D)),
        "w_in": nrm(ks[6], (DEPTH, D, IN_W), D ** -0.5),
        "b_fgate": 3.0 + 0.1 * jax.random.normal(ks[7], (DEPTH, FOX_HEADS), f32),
        "fox_w_o": nrm(ks[8], (DEPTH, FOX_W, D), FOX_W ** -0.5),
        "conv_w": nrm(ks[10], (DEPTH, CONV_W, 2 * GDN_KW + GDN_VW), CONV_W ** -0.5),
        "a_log": jnp.log(jax.random.uniform(ks[11], (DEPTH, GDN_HEADS), f32, 1.0, 16.0)),
        "dt_bias": dt + jnp.log(-jnp.expm1(-dt)),
        "gdn_norm_w": gain(ks[12], (DEPTH, GDN_DV)),
        "gdn_w_o": nrm(ks[13], (DEPTH, GDN_VW, D), GDN_VW ** -0.5),
        "b_branch_gate": nrm(ks[14], (DEPTH, 2, D), 0.02),
        "w_out": nrm(ks[15], (DEPTH, D, D), D ** -0.5),
        "g_pre_ffn": gain(ks[16], (DEPTH, D)),
        "g_post_ffn": gain(ks[17], (DEPTH, D)),
        "peer_w_query": nrm(ks[18], (DEPTH, D, PEER_HEADS * PEER_DQ), D ** -0.5),
        "peer_keys1": nrm(ks[19], (DEPTH, N_KEYS, PEER_DQ // 2), (PEER_DQ // 2) ** -0.5),
        "peer_keys2": nrm(ks[20], (DEPTH, N_KEYS, PEER_DQ // 2), (PEER_DQ // 2) ** -0.5),
        "peer_u": nrm(ks[21], (DEPTH, N_EXPERTS, D), D ** -0.5),
        "peer_v": nrm(ks[22], (DEPTH, N_EXPERTS, D), D ** -0.5),
    }

def reference(x, c, w_ada, b_ada, g_pre_mix, g_post_mix, w_in, b_fgate, fox_w_o, conv_w, a_log,
              dt_bias, gdn_norm_w, gdn_w_o, b_branch_gate, w_out, g_pre_ffn, g_post_ffn,
              peer_w_query, peer_keys1, peer_keys2, peer_u, peer_v):
    B, S, D = x.shape
    split_idx = np.cumsum(SPLITS)[:-1].tolist()
    for l in range(DEPTH):
        mod = jax.nn.silu(c) @ w_ada[l] + b_ada[l]
        sh1, sc1, gt1, sh2, sc2, gt2 = [m[:, None, :] for m in jnp.split(mod, 6, axis=-1)]

        h = rms_norm(x, g_pre_mix[l]) * (1.0 + sc1) + sh1
        proj = h @ w_in[l]
        fq, fk, fv, f_logit, gq, gk, gv, gz, b_logit, a_logit, ga, gb = jnp.split(proj, split_idx, axis=-1)

        log_f = jax.nn.log_sigmoid((f_logit + b_fgate[l]).astype(jnp.float32))
        ya = forgetting_attention(fq.reshape(B, S, FOX_HEADS, FOX_DH),
                                  fk.reshape(B, S, FOX_HEADS, FOX_DH),
                                  fv.reshape(B, S, FOX_HEADS, FOX_DH), log_f)
        ya = ya @ fox_w_o[l]

        qkv = causal_short_conv(jnp.concatenate([gq, gk, gv], axis=-1), conv_w[l])
        cq, ck, cv = jnp.split(qkv, [GDN_KW, 2 * GDN_KW], axis=-1)
        q_b = l2_norm(cq.reshape(B, S, GDN_HEADS, GDN_DK))
        k_b = l2_norm(ck.reshape(B, S, GDN_HEADS, GDN_DK))
        v_b = cv.reshape(B, S, GDN_HEADS, GDN_DV)
        beta = jax.nn.sigmoid(b_logit.astype(jnp.float32))
        g_dec = -jnp.exp(a_log[l].astype(jnp.float32)) * jax.nn.softplus((a_logit + dt_bias[l]).astype(jnp.float32))
        ob = gated_delta_rule(q_b, k_b, v_b, g_dec, beta)
        ob = rms_norm(ob, gdn_norm_w[l]) * jax.nn.silu(gz.reshape(B, S, GDN_HEADS, GDN_DV).astype(jnp.float32))
        yb = ob.reshape(B, S, GDN_VW).astype(x.dtype) @ gdn_w_o[l]

        gate_a = jax.nn.sigmoid(ga + b_branch_gate[l, 0])
        gate_b = jax.nn.sigmoid(gb + b_branch_gate[l, 1])
        mix = (gate_a * ya + gate_b * yb) @ w_out[l]
        x = x + gt1 * rms_norm(mix, g_post_mix[l])

        h2 = rms_norm(x, g_pre_ffn[l]) * (1.0 + sc2) + sh2
        y2 = peer(h2, peer_w_query[l], peer_keys1[l], peer_keys2[l], peer_u[l], peer_v[l])
        x = x + gt2 * rms_norm(y2, g_post_ffn[l])
    return x


_drawn_inputs = setup_inputs


def setup_inputs(seed=0):
    import zlib

    import numpy as np

    out = dict(_drawn_inputs(seed))
    spreads = {}
    factors = {'g_pre_mix': 2.699,
     'g_post_mix': 3.088,
     'gdn_norm_w': 3.849,
     'b_branch_gate': 3.715,
     'g_post_ffn': 8.0}
    for name, (base, spread) in spreads.items():
        noise = np.random.default_rng([zlib.crc32(name.encode()), seed]).standard_normal(out[name].shape)
        drawn = base * np.exp(spread * noise) if base else spread * noise
        out[name] = __import__('jax').numpy.asarray(drawn.astype(out[name].dtype))
    for name, factor in factors.items():
        out[name] = (out[name] * factor).astype(out[name].dtype)
    return out
```

```python
from contextlib import ExitStack

import numpy as np

import concourse.bass as bass
from concourse import mybir

P = 128
D = 1024
KD = D // P
S = 512
NT = S // P
FH, FDH = 8, 64
GH = 4
CH = 64
CONV = 4
PH = 8
NK = 128
TOPK = 16
EPS = 1e-6
NEG = -1.0e30
LOWEST = -3.0e38

RING = 8
USL, VSL = 8, 8

N_COL = 2 * KD
N_CONV = 12
N_GZ = 4
N_F = 12
N_ROW = 4 * KD
N_MIX = 3 * KD
N_OUT = KD
N_Q = 16
W_COL = 0
W_CONV = W_COL + N_COL
W_GZ = W_CONV + N_CONV
W_F = W_GZ + N_GZ
W_ROW = W_F + N_F
W_MIX = W_ROW + N_ROW
W_OUT = W_MIX + N_MIX
W_Q = W_OUT + N_OUT
N_W = W_Q + N_Q

F32 = mybir.dt.float32
U32 = mybir.dt.uint32
ALU = mybir.AluOpType
ACT = mybir.ActivationFunctionType
AX = mybir.AxisListType


def psum_jobs():
    order = [("ada_col",), ("xsq",), ("small",)]
    order += [("conv", c) for c in range(N_CONV)]
    order += [("gz", c) for c in range(N_GZ)]
    order += [("ssq", h) for h in range(2 * GH)]
    order += [("fq", c) for c in range(4)] + [("fk", c) for c in range(4)] + [("fv", c) for c in range(4)]
    order += [("cols",)]
    order += [("row", c) for c in range(2 * NT)]
    units = [(h, i) for h in range(FH) for i in range(NT)]
    for n, (h, i) in enumerate(units):
        order += [("S", h, i)]
        if n:
            order += [("PT",) + units[n - 1]]
    order += [("PT",) + units[-1]]
    table, used = {}, [0] * 8
    turn = 0
    for job in order:
        if job[0] in ("S", "PT"):
            bank = turn % 7
            table[job] = (bank, used[bank] + 1)
            used[bank] += 1
            turn += 1
            if job[0] == "PT" and job[2] == NT - 1:
                used[7] += 1
                table[("O", job[1])] = (7, used[7])
            continue
        bank = turn % 8
        used[bank] += 1
        table[job] = (bank, used[bank])
        turn += 1
    late = [("bg", h) for h in range(GH)] + [("bb", h) for h in range(GH)]
    for g in range(NT):
        late += [("kt", g), ("vt", g), ("kk", g), ("qk", g), ("D", g), ("E", g), ("D2", g), ("N2", g),
                 ("Y1", g), ("D4", g), ("N4", g), ("Y2", g), ("D8", g), ("Y3", g), ("W", g), ("M", g),
                 ("Q", g), ("M2", g), ("C", g), ("TT", g), ("u", g), ("wT", g)]
        for n in (2 * g, 2 * g + 1):
            late += [("ws", n), ("o", n), ("su", n)]
    late += [("oss", h) for h in range(GH)]
    late += [(w, c) for c in range(KD) for w in ("ga", "gb", "ya", "yb")]
    late += [("mix", i, half) for half in range(2) for i in range(NT)]
    late += [("h2T", i, half) for i in range(NT) for half in range(2)]
    late += [("qy", 0)]
    for q in range(N_Q):
        late += ([("qy", q + 1)] if q + 1 < N_Q else []) + [("sc", q)]
    for job in late:
        bank = turn % 8
        used[bank] += 1
        table[job] = (bank, used[bank])
        turn += 1
    return table, used


def hybrid_block(nc, x_rows, x_cols, c_cols, w_tiles, w_small, b_small, ada_cols, ada_rows, gains_cols,
                 gain_rows, conv_cols, keys_t, peer_u, peer_v, out):
    jobs, bank_uses = psum_jobs()
    ctx = ExitStack()
    with ctx:
        def sb(name, shape, dt=F32):
            return ctx.enter_context(nc.sbuf_tensor(name, shape, dt))

        def sem(name):
            return ctx.enter_context(nc.semaphore(name))

        ident = sb("ident", [P, P])
        ones = sb("ones", [P, P])
        near = sb("near_mask", [P, P])
        far = sb("far_mask", [P, P])
        causal = sb("causal_mask", [P, P])
        fox_mask = sb("fox_mask", [P, P])
        iota16 = sb("iota16", [P, TOPK])
        eps = sb("eps", [P, 1])
        c_sb = sb("c_sb", [P, KD])
        silu_c = sb("silu_c", [P, KD])
        small_b = sb("small_b", [P, 4])
        bcol = sb("bcol", [P, N_COL])
        gcols = sb("gcols", [P, 3 * KD + 1])
        convw = sb("convw", [P, N_CONV, CONV])
        scale1 = sb("scale1", [P, KD])
        shift1 = sb("shift1", [P, KD])
        stat = sb("stat", [P, 48])
        X = sb("X", [P, NT, D])
        mods = sb("mods", [P, 4, D])
        H2 = sb("H2", [P, NT, D])
        arena = sb("arena", [P, USL + VSL, D])
        hT = sb("hT", [P, KD, S])
        FQK = sb("FQK", [P, 16, S])
        Vr = sb("Vr", [P, NT, S])
        gzT = sb("gzT", [P, GH, S])
        OT = sb("OT", [P, NT, S])
        FT = sb("FT", [P, 8, S])

        ring = arena[:, 0:RING, :].rearrange("p s (k m) -> p s k m", k=KD)
        gT = arena[:, RING:RING + 6, :].rearrange("p s (c t) -> p (s c) t", c=2)
        spare = arena[:, RING + 6:RING + 8, :].rearrange("p s (c t) -> p (s c) t", c=2)
        R = spare[:, 0, :]
        CF = spare[:, 1, :]
        scan_a = spare[:, 2, :]
        wsm = FT[:, 6:8, :].rearrange("p a b -> p (a b)")[:, 0:KD * 96].rearrange("p (k m) -> p k m", k=KD)
        wsm_in = FT[:, 5, 0:KD * 16]
        Z, T1, T2, T3, T4 = (FT[:, n, :] for n in range(5))
        silu_cb = OT[:, 0:2, :].rearrange("p a (k m) -> p (a k) m", m=P)
        grow = H2[:, 0:3, :]
        sel = X[0:36, 1, 0:GH * P].rearrange("p (h m) -> p h m", h=GH)
        keys = sb("keys", [P, 2, NK])
        rcols = X[:, 0, 0:NT * P].rearrange("p (i m) -> p i m", i=NT)
        qaug = FQK[:, 0:8, :]
        kaug = FQK[:, 8:16, :]
        qT, kT, vT = gT[:, 0:4, :], gT[:, 4:8, :], gT[:, 8:12, :]
        Gb, expG, kbT, qdT = FQK[:, 0:4, :], FQK[:, 4:8, :], FQK[:, 8:12, :], FQK[:, 12:16, :]
        h2u = H2[:, :, :].rearrange("p a (b t) -> p (a b) t", b=2)
        uB, wB, aB, kdB = ([h2u[:, 2 * n + b, :] for b in range(2)] for n in range(4))
        tA, tB, tN, tET = (Vr[:, n, :] for n in range(4))
        tD, tE, tY, tC, rv, rw, St, vn = (FT[:, n, :] for n in range(8))
        OBT = spare
        mixT = FQK[:, 0:8, :]
        scores = FQK[:, :, :].rearrange("p a (b k) -> p (a b) k", k=2 * NK)

        PS = ctx.enter_context(nc.psum_tensor("PS", [P, 8, S], F32))

        def bank(job):
            return PS[:, jobs[job][0], :]

        full = [sem(f"full{b}") for b in range(8)]
        free = [sem(f"free{b}") for b in range(8)]
        w_landed = [sem(f"w_landed{s}") for s in range(RING)]
        w_used = sem("w_used")
        x_landed = sem("x_landed")
        xc_landed = sem("xc_landed")
        c_landed = sem("c_landed")
        small_landed = sem("small_landed")
        rows_landed = sem("rows_landed")
        aug_landed = sem("aug_landed")
        out_landed = sem("out_landed")
        pool_chain = sem("pool_chain")
        consts_ready = sem("consts_ready")
        wsm_ready = sem("wsm_ready")
        act_chain = sem("act_chain")
        dve_chain = sem("dve_chain")
        silu_ready = sem("silu_ready")
        silub_ready = sem("silub_ready")
        sq_ready = sem("sq_ready")
        mod_cols = sem("mod_cols")
        root_ready = sem("root_ready")
        h_ready = sem("h_ready")
        ln_ready = sem("ln_ready")
        g_ready = sem("g_ready")
        gexp_ready = sem("gexp_ready")
        rows_ready = sem("rows_ready")
        cum_ready = sem("cum_ready")
        tap_ready = sem("tap_ready")
        conv_ready = sem("conv_ready")
        conv_silu = sem("conv_silu")
        gsq_ready = sem("gsq_ready")
        qkn_ready = sem("qkn_ready")
        smax_ready = sem("smax_ready")
        p_ready = sem("p_ready")
        pn_ready = sem("pn_ready")
        mods_ready = sem("mods_ready")
        qd_ready = sem("qd_ready")
        dec_in = sem("dec_in")
        dec_ready = sem("dec_ready")
        near_ready = sem("near_ready")
        y0_ready = sem("y0_ready")
        c0_ready = sem("c0_ready")
        state_zero = sem("state_zero")
        osq_ready = sem("osq_ready")
        oroot_ready = sem("oroot_ready")
        ob_ready = sem("ob_ready")
        sig_ready = sem("sig_ready")
        sig_used = sem("sig_used")
        mix_ready = sem("mix_ready")
        mss_ready = sem("mss_ready")
        mroot_ready = sem("mroot_ready")
        x1_ready = sem("x1_ready")
        h2_ready = sem("h2_ready")
        u_landed = [sem(f"u_landed{s}") for s in range(USL)]
        v_landed = [sem(f"v_landed{s}") for s in range(VSL)]
        u_free = sem("u_free")
        v_free = sem("v_free")
        idx_ready = sem("idx_ready")
        top_ready = sem("top_ready")
        gate_ready = sem("gate_ready")
        gelu_ready = sem("gelu_ready")
        wts_ready = sem("wts_ready")
        diag_ready = sem("diag_ready")
        y_zero = sem("y_zero")
        y_out = sem("y_out")
        seen_pool = sem("seen_pool")
        seen_act = sem("seen_act")
        seen_pe = sem("seen_pe")
        keys_landed = sem("keys_landed")
        fss_ready = sem("fss_ready")
        froot_ready = sem("froot_ready")
        fin_ready = sem("fin_ready")

        idx_sb = [sb(f"idx{p}", [P, TOPK], U32) for p in range(2)]
        tops = [sb(f"tops{p}", [P, TOPK]) for p in range(2)]
        gate = [sb(f"gate{p}", [P, TOPK + 4]) for p in range(2)]
        dots = [sb(f"dots{p}", [P, TOPK]) for p in range(2)]
        acts = [sb(f"acts{p}", [P, TOPK]) for p in range(2)]
        wts = [sb(f"wts{p}", [P, TOPK]) for p in range(2)]
        ystore = hT[:, :, :].rearrange("p (a b) t -> p a (b t)", a=NT)
        diag = OT[:, 0:1, :].rearrange("p a (n m) -> p (a n) m", m=P)
        zeros = OT[:, 1, :]
        NDG = 4
        st1, st2 = Vr[:, 0, 0:2 * NK], Vr[:, 0, 2 * NK:4 * NK]
        cand, cand2 = Vr[:, 1, 0:256], Vr[:, 1, 256:512]
        onehot, picked = Vr[:, 2, 0:256], Vr[:, 2, 256:512]
        kv = Vr[:, 3, 0:32]
        ki = Vr[:, 3, 32:64].bitcast(U32)
        kf = Vr[:, 3, 64:96]
        pos = Vr[:, 3, 96:112].bitcast(U32)
        pa = Vr[:, 3, 112:128].bitcast(U32)
        pb = Vr[:, 3, 128:144].bitcast(U32)
        paf, pbf = Vr[:, 3, 144:160], Vr[:, 3, 160:176]
        e1, e2 = Vr[:, 3, 176:192], Vr[:, 3, 192:208]

        def wait_full(eng, job):
            eng.wait_ge(full[jobs[job][0]], jobs[job][1])

        def wait_free(eng, job):
            eng.wait_ge(free[jobs[job][0]], jobs[job][1])

        def frees(ins, job):
            ins.then_inc(free[jobs[job][0]], 1)

        def bcast(ap, n):
            return ap.unsqueeze(2).to_broadcast([ap.shape[0], ap.shape[1], n])

        def heads(ap):
            return ap.rearrange("p (h m) -> p h m", h=GH)

        def mid(ap, n):
            return ap.unsqueeze(1).to_broadcast([ap.shape[0], n, ap.shape[1]])

        block = ctx.enter_context(nc.Block())

        @block.sync
        def _(sp):
            sp.dma_start(c_sb[:, :], c_cols).then_inc(c_landed, 16)
            sp.dma_start(keys[:, :, :], keys_t).then_inc(keys_landed, 16)
            for s in range(RING):
                sp.dma_start(arena[:, s, :], w_tiles[s]).then_inc(w_landed[s], 16)
                if s == 3:
                    sp.dma_start(hT[:, :, :], x_cols).then_inc(xc_landed, 16)
            rounds = N_W // RING
            with sp.Fori(1, rounds) as r:
                for s in range(RING):
                    sp.wait_ge(w_used, r * RING + (s + 1 - RING))
                    sp.dma_start(arena[:, s, :], w_tiles[bass.ds(r * RING + s, 1)].rearrange("o p m -> (o p) m")
                                 ).then_inc(w_landed[s], 16)
            for n in range(rounds * RING, N_W):
                sp.wait_ge(w_used, n + 1 - RING)
                sp.dma_start(arena[:, n % RING, :], w_tiles[n]).then_inc(w_landed[n % RING], 16)
            for i in range(NT):
                sp.wait_ge(fin_ready, i + 1)
                sp.dma_start(out[i], X[:, i, :]).then_inc(out_landed, 16)
            sp.wait_ge(out_landed, 16 * NT)

        @block.gpsimd
        def _(pool):
            n_chain = [0]

            def link(ins):
                n_chain[0] += 1
                ins.then_inc(pool_chain, 1)
                pool.wait_ge(pool_chain, n_chain[0])

            pool.dma_start(wsm_in, w_small).then_inc(small_landed, 16)
            pool.dma_start(bcol[:, :], ada_cols).then_inc(small_landed, 16)
            pool.dma_start(gcols[:, :], gains_cols).then_inc(small_landed, 16)
            pool.dma_start(convw[:, :, :], conv_cols).then_inc(small_landed, 16)
            link(pool.memset(small_b[:, :], 0.0))
            pool.dma_start(small_b[0:FH, 0:1], b_small[0:FH, :]).then_inc(small_landed, 16)
            pool.dma_start(small_b[64:64 + GH, 0:1], b_small[FH:FH + GH, :]).then_inc(small_landed, 16)
            pool.dma_start(small_b[64:64 + GH, 1:2], b_small[FH + GH:FH + 2 * GH, :]).then_inc(small_landed, 16)
            pool.dma_start(mods[:, :, :].rearrange("p a b -> p (a b)"), ada_rows.partition_broadcast(P)).then_inc(rows_landed, 16)
            pool.dma_start(grow.rearrange("p a b -> p (a b)"), gain_rows.partition_broadcast(P)).then_inc(rows_landed, 16)

            link(pool.memset(ones[:, :], 1.0))
            link(pool.memset(eps[:, :], EPS))
            link(pool.memset(ident[:, :], 0.0))
            link(pool.affine_select(out=ident[:, :], in_=ident[:, :], compare_op=ALU.not_equal, fill=1.0,
                                    base=0, pattern=[[-1, P]], channel_multiplier=1))
            link(pool.affine_select(out=causal[:, :], in_=ones[:, :], compare_op=ALU.is_ge, fill=0.0,
                                    base=0, pattern=[[1, P]], channel_multiplier=-1))
            blk = causal[:, :].rearrange("p (b i) -> p b i", i=CH)
            link(pool.affine_select(out=blk, in_=blk, compare_op=ALU.is_ge, fill=0.0,
                                    base=0, pattern=[[-CH, P // CH], [0, CH]], channel_multiplier=1))
            link(pool.affine_select(out=near[:, :], in_=ones[:, :], compare_op=ALU.is_gt, fill=0.0,
                                    base=0, pattern=[[1, P]], channel_multiplier=-1))
            blk = near[:, :].rearrange("p (b i) -> p b i", i=16)
            link(pool.affine_select(out=blk, in_=blk, compare_op=ALU.is_ge, fill=0.0,
                                    base=0, pattern=[[-16, P // 16], [0, 16]], channel_multiplier=1))
            link(pool.tensor_tensor(out=far[:, :], in0=causal[:, :], in1=near[:, :], op=ALU.subtract))
            link(pool.tensor_tensor(out=far[:, :], in0=far[:, :], in1=ident[:, :], op=ALU.subtract))
            link(pool.memset(fox_mask[:, :], 0.0))
            link(pool.affine_select(out=fox_mask[:, :], in_=fox_mask[:, :], compare_op=ALU.is_ge, fill=NEG,
                                    base=0, pattern=[[-1, P]], channel_multiplier=1))
            link(pool.iota(iota16[:, :], pattern=[[1, TOPK]], base=0, channel_multiplier=0,
                           allow_small_or_imprecise_dtypes=True))
            for b in (0, 32):
                link(pool.memset(sel[b:b + GH, :, :], 1.0))
                link(pool.affine_select(out=sel[b:b + GH, :, :], in_=sel[b:b + GH, :, :], compare_op=ALU.is_equal,
                                        fill=0.0, base=0, pattern=[[-1, GH], [0, P]], channel_multiplier=1))
            link(pool.memset(scan_a[:, :], 1.0))
            link(pool.memset(scan_a.rearrange("p (n i) -> p n i", i=CH)[64:64 + GH, :, 0:1], 0.0))
            link(pool.memset(R, 0.0))
            link(pool.memset(wsm[:, :, :], 0.0))
            pool.wait_ge(small_landed, 7 * 16)
            win = wsm_in.rearrange("p (k m) -> p k m", k=KD)
            link(pool.tensor_copy(wsm[:, :, 0:8], win[:, :, 0:8]))
            link(pool.tensor_copy(wsm[:, :, 32:36], win[:, :, 8:12]))
            link(pool.tensor_copy(wsm[:, :, 64:68], win[:, :, 12:16]))
            pool.sem_inc(consts_ready, 1)
            pool.wait_ge(cum_ready, 3)
            for h in range(FH):
                pool.dma_start(qaug[64:65, h, :], CF[h:h + 1, :]).then_inc(aug_landed, 16)
                pool.dma_start(kaug[65:66, h, :], CF[32 + h:33 + h, :]).then_inc(aug_landed, 16)

            pool.wait_ge(ob_ready, GH)
            pool.dma_start(X[:, :, :], x_rows).then_inc(x_landed, 16)

            with pool.Fori(0, NT) as i:
                with pool.Fori(0, PH // 2) as b:
                    for p in range(2):
                        head = i * PH + b * 2 + p
                        pool.wait_ge(idx_ready, head + 1)
                        pool.sem_inc(seen_pool, 1)
                        for k in range(TOPK):
                            if k % 4 == 0:
                                pool.wait_ge(u_free, head * TOPK + (k + 4))
                                pool.sem_inc(seen_pool, 1)
                            pool.indirect_dma_start(
                                out=arena[:, k % USL, :], out_offset=None, in_=peer_u,
                                in_offset=bass.IndirectOffsetOnAxis(ap=idx_sb[p][:, k:k + 1], axis=0),
                            ).then_inc(u_landed[k % USL], 16)
                        for k in range(TOPK):
                            if k % 4 == 0:
                                pool.wait_ge(v_free, head * TOPK + (k + 4))
                                pool.sem_inc(seen_pool, 1)
                            pool.indirect_dma_start(
                                out=arena[:, USL + k % VSL, :], out_offset=None, in_=peer_v,
                                in_offset=bass.IndirectOffsetOnAxis(ap=idx_sb[p][:, k:k + 1], axis=0),
                            ).then_inc(v_landed[k % VSL], 16)

        @block.scalar
        def _(act):
            n_chain = [0]

            def link(ins):
                n_chain[0] += 1
                ins.then_inc(act_chain, 1)
                act.wait_ge(act_chain, n_chain[0])

            act.wait_ge(c_landed, 16)
            act.activation(silu_c[:, :], c_sb[:, :], ACT.Silu).then_inc(silu_ready, 1)
            act.wait_ge(silu_ready, 1)
            act.wait_ge(consts_ready, 1)
            for k in range(KD):
                ins = act.mul(silu_cb[:, k, :], ones[:, :], silu_c[:, k:k + 1])
            ins.then_inc(silub_ready, 1)
            act.wait_ge(xc_landed, 16)
            for k in range(KD):
                act.activation(FQK[:, k, :], hT[:, k, :], ACT.Square).then_inc(sq_ready, 1)
            wait_full(act, ("xsq",))
            frees(act.activation(T1, bank(("xsq",)), ACT.Sqrt, bias=eps[:, 0:1], scale=1.0 / D), ("xsq",))

            act.wait_ge(mod_cols, 2)
            for k in range(KD):
                act.wait_ge(root_ready, k + 1)
                act.activation(hT[:, k, :], hT[:, k, :], ACT.Identity, bias=shift1[:, k:k + 1],
                               scale=scale1[:, k:k + 1]).then_inc(h_ready, 1)

            def conv_silu_of(c):
                act.wait_ge(conv_ready, c + 1)
                act.activation(gT[:, c, :], gT[:, c, :], ACT.Silu).then_inc(conv_silu, 1)

            for c in range(N_CONV):
                wait_full(act, ("conv", c))
                act.mul(gT[:, c, :], bank(("conv", c)), convw[:, c, CONV - 1:CONV]).then_inc(tap_ready, 1)
                if c >= 2:
                    conv_silu_of(c - 2)
            conv_silu_of(N_CONV - 2)
            conv_silu_of(N_CONV - 1)
            for c in range(N_GZ):
                wait_full(act, ("gz", c))
                frees(act.activation(gzT[:, c, :], bank(("gz", c)), ACT.Silu), ("gz", c))
            for h in range(2 * GH):
                act.wait_ge(conv_silu, h + 1)
                if h >= 2:
                    wait_full(act, ("ssq", h - 2))
                act.activation(FT[:, 3 + h % 2, :], gT[:, h, :], ACT.Square).then_inc(gsq_ready, 1)
            for h in range(2 * GH):
                wait_full(act, ("ssq", h))
                if h >= 2:
                    act.wait_ge(qkn_ready, h - 1)
                frees(act.activation(FT[:, 5 + h % 2, :], bank(("ssq", h)), ACT.Sqrt, bias=eps[:, 0:1]),
                      ("ssq", h))
            for which, dst, scale in (("fq", qaug, FDH ** -0.5), ("fk", kaug, 1.0)):
                for c in range(4):
                    wait_full(act, (which, c))
                    act.mul(dst[0:FDH, 2 * c, :], bank((which, c))[0:FDH, :], scale)
                    frees(act.mul(dst[0:FDH, 2 * c + 1, :], bank((which, c))[FDH:P, :], scale), (which, c))
            for c in range(4):
                wait_full(act, ("fv", c))
                frees(act.copy(Vr[:, :, c * P:(c + 1) * P],
                               bank(("fv", c)).rearrange("p (i m) -> p i m", i=NT)), ("fv", c))

            wait_free(act, ("small",))
            link(act.activation(T1[0:68, :], Z[0:68, :], ACT.Abs))
            link(act.activation(T1[0:68, :], T1[0:68, :], ACT.Exp, scale=-1.0))
            link(act.activation(T1[0:68, :], T1[0:68, :], ACT.Ln, bias=ones[0:68, 0:1]))
            link(act.activation(T2[32:32 + GH, :], Z[32:32 + GH, :], ACT.Exp, scale=-1.0))
            act.activation(small_b[64:64 + GH, 2:3], small_b[64:64 + GH, 1:2], ACT.Exp).then_inc(ln_ready, 1)
            act.wait_ge(g_ready, 2)
            act.activation(T4[32:32 + GH, :], T3[64:64 + GH, :], ACT.Exp).then_inc(gexp_ready, 1)
            act.copy(R[0:GH, :], T3[64:64 + GH, :]).then_inc(rows_ready, 1)
            act.activation(R[96:96 + GH, :], T4[64:64 + GH, :], ACT.Exp, scale=-1.0).then_inc(rows_ready, 1)

            wait_full(act, ("cols",))
            frees(act.copy(rcols[:, :, :], bank(("cols",)).rearrange("p (i m) -> p i m", i=NT)), ("cols",))

            units = [(h, i) for h in range(FH) for i in range(NT)]

            def keep_head(h):
                wait_full(act, ("O", h))
                frees(act.copy(OT[64 * (h % 2):64 * (h % 2) + 64, h // 2, :], bank(("O", h))[0:FDH, :]), ("O", h))

            for n, (h, i) in enumerate(units):
                act.wait_ge(smax_ready, n + 1)
                if n >= 2:
                    wait_full(act, ("PT",) + units[n - 2])
                if n >= 2 and units[n - 2][1] == NT - 1:
                    keep_head(units[n - 2][0])
                w = (i + 1) * P
                frees(act.activation(FT[:, n % 2, 0:w], bank(("S", h, i))[:, 0:w], ACT.Exp,
                                     bias=stat[:, n % 2:n % 2 + 1], accum_out=stat[:, 2 + n % 2:3 + n % 2]),
                      ("S", h, i))
                if n >= 1:
                    hh, ii = units[n - 1]
                    wait_full(act, ("PT", hh, ii))
                    frees(act.copy(FT[:, 2 + (n - 1) % 2, 0:(ii + 1) * P], bank(("PT", hh, ii))[:, 0:(ii + 1) * P]),
                          ("PT", hh, ii))
            hh, ii = units[-1]
            wait_full(act, ("PT", hh, ii))
            frees(act.copy(FT[:, 2 + (len(units) - 1) % 2, :], bank(("PT", hh, ii))), ("PT", hh, ii))
            keep_head(FH - 1)

            for h in range(GH):
                wait_full(act, ("bg", h))
                act.copy(Gb[:, h, :], bank(("bg", h)))
                frees(act.activation(expG[:, h, :], bank(("bg", h)), ACT.Exp), ("bg", h))

            for g in range(NT):
                act.wait_ge(dec_in, g + 1)
                act.activation(tA, tA, ACT.Exp).then_inc(dec_ready, 1)
                for job, dst in (("D", tD), ("E", tE), ("D2", tA), ("N2", tB), ("D4", tD), ("N4", tN), ("D8", tA),
                                 ("W", tB), ("M", tD), ("M2", tA), ("TT", tET), ("u", uB[g % 2]),
                                 ("wT", wB[g % 2])):
                    wait_full(act, (job, g))
                    frees(act.copy(dst, bank((job, g))), (job, g))
                for n in (2 * g, 2 * g + 1):
                    wait_full(act, ("o", n))
                    frees(act.copy(OBT[:, :, n * CH:(n + 1) * CH],
                                   bank(("o", n))[:, 0:GH * CH].rearrange("p (h t) -> p h t", h=GH)), ("o", n))
            last = ("o", 2 * NT - 1)
            wait_free(act, last)
            for h in range(GH):
                act.activation(Vr[:, h, :], OBT[:, h, :], ACT.Square).then_inc(osq_ready, 1)
            for h in range(GH):
                wait_full(act, ("oss", h))
                frees(act.activation(FT[:, h, :], bank(("oss", h)), ACT.Sqrt, bias=eps[:, 0:1], scale=1.0 / P),
                      ("oss", h))
            for c in range(KD):
                if c >= 1:
                    act.wait_ge(sig_used, c)
                for n, w in enumerate(("ga", "gb")):
                    wait_full(act, (w, c))
                    frees(act.activation(FT[:, 4 + n, :], bank((w, c)), ACT.Sigmoid,
                                         bias=gcols[:, KD * (n + 1) + c:KD * (n + 1) + c + 1]), (w, c))
            for i in range(NT):
                for half in range(2):
                    wait_full(act, ("mix", i, half))
                    act.activation(FT[:, 0, :], bank(("mix", i, half)), ACT.Square,
                                   accum_out=stat[:, 8 + 2 * i + half:9 + 2 * i + half]).then_inc(act_chain, 1)
                    n_chain[0] += 1
                    act.wait_ge(act_chain, n_chain[0])
                link(act.activation(stat[:, 16 + i:17 + i], stat[:, 8 + 2 * i:9 + 2 * i], ACT.Identity,
                                    bias=stat[:, 9 + 2 * i:10 + 2 * i]))
                act.activation(stat[:, 20 + i:21 + i], stat[:, 16 + i:17 + i], ACT.Sqrt, bias=eps[:, 0:1],
                               scale=1.0 / D).then_inc(mroot_ready, 1)
                act.wait_ge(x1_ready, i + 1)
                link(act.activation(FT[:, 0:2, :].rearrange("p a b -> p (a b)"), X[:, i, :], ACT.Square,
                                    accum_out=stat[:, 24 + i:25 + i]))
                act.activation(stat[:, 28 + i:29 + i], stat[:, 24 + i:25 + i], ACT.Sqrt, bias=eps[:, 0:1],
                               scale=1.0 / D).then_inc(mroot_ready, 1)
            for i in range(NT):
                for half in range(2):
                    wait_full(act, ("h2T", i, half))
                    frees(act.copy(hT[:, 4 * half:4 * half + 4, i * P:(i + 1) * P],
                                   bank(("h2T", i, half)).rearrange("p (k t) -> p k t", k=4)), ("h2T", i, half))
            for q in range(N_Q):
                wait_full(act, ("qy", q))
                frees(act.copy(FT[:, 2 + q % 2, :], bank(("qy", q))), ("qy", q))
                wait_full(act, ("sc", q))
                dst = scores.rearrange("p (i h) (s k) -> p i h s k", i=NT, s=2)[:, :, q // 2, q % 2, :]
                frees(act.copy(dst, bank(("sc", q)).rearrange("p (i k) -> p i k", i=NT)), ("sc", q))

            act.mul(zeros, ones[:, 0:1].to_broadcast([P, S]), 0.0).then_inc(seen_act, 1)
            act.wait_ge(seen_act, 1)
            act.copy(PS[:, 0, :], zeros)
            act.copy(PS[:, 1, :], zeros).then_inc(y_zero, 1)
            with act.Fori(0, NT) as i:
                with act.Fori(0, PH // 2) as b:
                    for p in range(2):
                        head = i * PH + b * 2 + p
                        act.wait_ge(top_ready, head + 1)
                        act.activation(gate[p][:, 0:TOPK], tops[p][:, :], ACT.Exp, bias=gate[p][:, TOPK:TOPK + 1],
                                       accum_out=gate[p][:, TOPK + 1:TOPK + 2]).then_inc(gate_ready, 1)
                        act.wait_ge(u_free, (head + 1) * TOPK + USL)
                        act.activation(acts[p][:, :], dots[p][:, :], ACT.Gelu).then_inc(gelu_ready, 1)
                        act.wait_ge(wts_ready, head + 1)
                        for k in range(TOPK):
                            act.wait_ge(v_free, head * TOPK + (k + 1 + VSL - NDG))
                            act.mul(diag[:, k % NDG, :], ident[:, :], wts[p][:, k:k + 1]).then_inc(diag_ready, 1)
                act.wait_ge(v_free, (i + 1) * (PH * TOPK) + VSL)
                act.sem_inc(seen_act, 1)
                act.copy(ystore[:, bass.ds(i, 1), 0:S].rearrange("p a b -> p (a b)"), PS[:, 0, :])
                act.copy(ystore[:, bass.ds(i, 1), S:2 * S].rearrange("p a b -> p (a b)"), PS[:, 1, :]).then_inc(y_out, 1)
                act.wait_ge(y_out, i + 1)
                act.sem_inc(seen_act, 1)
                act.copy(PS[:, 0, :], zeros)
                act.copy(PS[:, 1, :], zeros).then_inc(y_zero, 1)
            for i in range(NT):
                if i:
                    act.wait_ge(fss_ready, i)
                act.activation(FT[:, 0:2, :].rearrange("p a b -> p (a b)"), ystore[:, i, :], ACT.Square,
                               accum_out=stat[:, 32 + i:33 + i]).then_inc(fss_ready, 1)
            act.wait_ge(fss_ready, NT)
            act.activation(stat[:, 36:36 + NT], stat[:, 32:32 + NT], ACT.Sqrt, bias=eps[:, 0:1],
                           scale=1.0 / D).then_inc(froot_ready, 1)

        @block.vector
        def _(dve):
            n_chain = [0]

            def link(ins):
                n_chain[0] += 1
                ins.then_inc(dve_chain, 1)
                dve.wait_ge(dve_chain, n_chain[0])

            dve.wait_ge(consts_ready, 1)
            wait_full(dve, ("ada_col",))
            dve.wait_ge(small_landed, 7 * 16)
            dve.tensor_tensor(out=shift1[:, :], in0=PS[:, jobs[("ada_col",)][0], 0:KD], in1=bcol[:, 0:KD],
                              op=ALU.add).then_inc(mod_cols, 1)
            link(dve.tensor_tensor(out=scale1[:, :], in0=PS[:, jobs[("ada_col",)][0], KD:2 * KD],
                                   in1=bcol[:, KD:2 * KD], op=ALU.add))
            dve.scalar_tensor_tensor(out=scale1[:, :], in0=scale1[:, :], scalar=1.0, in1=gcols[:, 0:KD],
                                     op0=ALU.add, op1=ALU.mult).then_inc(mod_cols, 1)
            dve.sem_inc(free[jobs[("ada_col",)][0]], 1)
            wait_free(dve, ("xsq",))
            link(dve.reciprocal(T1, T1))
            for k in range(KD):
                dve.tensor_tensor(out=hT[:, k, :], in0=hT[:, k, :], in1=T1, op=ALU.mult).then_inc(root_ready, 1)

            wait_full(dve, ("small",))
            frees(dve.tensor_scalar(Z[0:68, :], bank(("small",))[0:68, :], small_b[0:68, 0:1], None, ALU.add),
                  ("small",))

            for c in range(N_CONV):
                dve.wait_ge(tap_ready, c + 1)
                for d in range(1, CONV):
                    ins = dve.scalar_tensor_tensor(
                        out=gT[:, c, d:S], in0=bank(("conv", c))[:, 0:S - d],
                        scalar=convw[:, c, CONV - 1 - d:CONV - d], in1=gT[:, c, d:S], op0=ALU.mult, op1=ALU.add)
                    if d < CONV - 1:
                        link(ins)
                link(ins)
                dve.sem_inc(conv_ready, 1)
                dve.sem_inc(free[jobs[("conv", c)][0]], 1)
            for h in range(2 * GH):
                wait_free(dve, ("ssq", h))
                r = FT[:, 5 + h % 2, :]
                link(dve.reciprocal(r, r))
                dve.scalar_tensor_tensor(out=gT[:, h, :], in0=gT[:, h, :], scalar=(P ** -0.5 if h < GH else 1.0),
                                         in1=r, op0=ALU.mult, op1=ALU.mult).then_inc(qkn_ready, 1)

            dve.wait_ge(ln_ready, 1)
            link(dve.tensor_scalar(T2[0:FH, :], Z[0:FH, :], 0.0, None, ALU.min))
            link(dve.tensor_tensor(out=T2[0:FH, :], in0=T2[0:FH, :], in1=T1[0:FH, :], op=ALU.subtract))
            dve.tensor_tensor_scan(CF[0:FH, :], scan_a[0:FH, :], T2[0:FH, :], 0.0, ALU.mult,
                                   ALU.add).then_inc(cum_ready, 1)
            dve.wait_ge(cum_ready, 1)
            dve.tensor_scalar(CF[32:32 + FH, :], CF[0:FH, :], -1.0, None, ALU.mult).then_inc(cum_ready, 1)
            dve.memset(qaug[64:66, :, :], 1.0)
            dve.memset(kaug[64:66, :, :], 1.0).then_inc(cum_ready, 1)
            link(dve.tensor_scalar(T2[32:32 + GH, :], T2[32:32 + GH, :], 1.0, None, ALU.add))
            link(dve.reciprocal(R[32:32 + GH, :], T2[32:32 + GH, :]))
            a0, a1 = 64, 64 + GH
            link(dve.scalar_tensor_tensor(out=T2[a0:a1, :], in0=Z[a0:a1, :], scalar=0.0, in1=T1[a0:a1, :],
                                          op0=ALU.max, op1=ALU.add))
            link(dve.tensor_scalar(T2[a0:a1, :], T2[a0:a1, :], small_b[a0:a1, 2:3], -1.0, ALU.mult, ALU.mult))
            dve.tensor_tensor_scan(T3[a0:a1, :], scan_a[a0:a1, :], T2[a0:a1, :], 0.0, ALU.mult,
                                   ALU.add).then_inc(g_ready, 1)
            dve.wait_ge(g_ready, 1)
            g3 = T3[a0:a1, :].rearrange("p (n i) -> p n i", i=CH)
            dve.tensor_tensor(out=T4[a0:a1, :].rearrange("p (n i) -> p n i", i=CH), in0=g3,
                              in1=g3[:, :, CH - 1:CH].to_broadcast([GH, S // CH, CH]),
                              op=ALU.subtract).then_inc(g_ready, 1)
            dve.wait_ge(gexp_ready, 1)
            dve.tensor_tensor(out=R[64:64 + GH, :], in0=R[32:32 + GH, :], in1=T4[32:32 + GH, :],
                              op=ALU.mult).then_inc(rows_ready, 1)

            dve.wait_ge(rows_landed, 32)
            for c in range(2 * NT):
                wait_full(dve, ("row", c))
                m = mods[:, c // 2, (c % 2) * S:(c % 2 + 1) * S]
                frees(dve.tensor_tensor(out=m, in0=bank(("row", c)), in1=m, op=ALU.add), ("row", c))
            wait_free(dve, ("row", 2 * NT - 1))
            link(dve.tensor_tensor(out=mods[:, 0, :], in0=mods[:, 0, :], in1=grow[:, 0, :], op=ALU.mult))
            link(dve.scalar_tensor_tensor(out=mods[:, 2, :], in0=mods[:, 2, :], scalar=1.0, in1=grow[:, 1, :],
                                          op0=ALU.add, op1=ALU.mult))
            link(dve.tensor_tensor(out=mods[:, 3, :], in0=mods[:, 3, :], in1=grow[:, 2, :], op=ALU.mult))

            units = [(h, i) for h in range(FH) for i in range(NT)]

            def normalise(n):
                h, i = units[n]
                wait_free(dve, ("S", h, i))
                if n:
                    dve.wait_ge(pn_ready, n)
                link(dve.reciprocal(stat[:, 4:5], stat[:, 2 + n % 2:3 + n % 2]))
                w = (i + 1) * P
                dve.tensor_scalar(FT[:, n % 2, 0:w], FT[:, n % 2, 0:w], stat[:, 4:5], None,
                                  ALU.mult).then_inc(pn_ready, 1)

            for n, (h, i) in enumerate(units):
                wait_full(dve, ("S", h, i))
                if n >= 2:
                    wait_free(dve, ("S",) + units[n - 2])
                dve.tensor_reduce(stat[:, n % 2:n % 2 + 1], bank(("S", h, i))[:, 0:(i + 1) * P], AX.X, ALU.max,
                                  negate=True).then_inc(smax_ready, 1)
                if n:
                    normalise(n - 1)
            normalise(len(units) - 1)

            for h in range(GH):
                wait_full(dve, ("bb", h))
                frees(dve.tensor_tensor(out=kbT[:, h, :], in0=bank(("bb", h)), in1=kT[:, h, :], op=ALU.mult),
                      ("bb", h))
            for h in range(GH):
                wait_free(dve, ("bg", h))
                dve.tensor_tensor(out=qdT[:, h, :], in0=expG[:, h, :], in1=qT[:, h, :],
                                  op=ALU.mult).then_inc(qd_ready, 1)
            dve.memset(St, 0.0).then_inc(state_zero, 1)

            wait_free(dve, ("cols",))
            for g in range(NT):
                tok = slice(g * P, (g + 1) * P)
                wait_full(dve, ("kt", g))
                dve.tensor_tensor(out=heads(rw), in0=heads(bank(("kt", g))), in1=bcast(rcols[:, g, 64:64 + GH], P),
                                  op=ALU.mult)
                frees(dve.tensor_tensor(out=heads(kdB[g % 2]), in0=heads(bank(("kt", g))),
                                        in1=bcast(rcols[:, g, 96:96 + GH], P), op=ALU.mult), ("kt", g))
                wait_full(dve, ("vt", g))
                frees(dve.tensor_tensor(out=heads(rv), in0=heads(bank(("vt", g))),
                                        in1=bcast(rcols[:, g, 32:32 + GH], P), op=ALU.mult), ("vt", g))
                for h in range(GH):
                    ins = dve.tensor_scalar(tA[:, h * P:(h + 1) * P], Gb[:, h, tok], rcols[:, g, h:h + 1], 0.0,
                                            ALU.subtract, ALU.min)
                ins.then_inc(dec_in, 1)
                dve.wait_ge(dec_ready, g + 1)
                link(dve.tensor_tensor(out=heads(tA), in0=heads(tA), in1=mid(causal[:, :], GH), op=ALU.mult))
                wait_full(dve, ("kk", g))
                frees(dve.tensor_tensor(out=tB, in0=bank(("kk", g)), in1=tA, op=ALU.mult), ("kk", g))
                wait_full(dve, ("qk", g))
                frees(dve.tensor_tensor(out=aB[g % 2], in0=bank(("qk", g)), in1=tA, op=ALU.mult), ("qk", g))
                wait_free(dve, ("kk", g))
                dve.tensor_tensor(out=heads(tN), in0=heads(tB), in1=mid(near[:, :], GH),
                                  op=ALU.mult).then_inc(near_ready, 1)
                dve.tensor_tensor(out=heads(tET), in0=heads(tB), in1=mid(far[:, :], GH),
                                  op=ALU.mult).then_inc(near_ready, 1)
                dve.wait_ge(near_ready, 2 * g + 2)
                dve.scalar_tensor_tensor(out=heads(tY), in0=heads(tN), scalar=-1.0, in1=mid(ident[:, :], GH),
                                         op0=ALU.mult, op1=ALU.add).then_inc(y0_ready, 1)
                for job in ("Y1", "Y2", "Y3"):
                    wait_full(dve, (job, g))
                    if job == "Y1":
                        dve.wait_ge(y0_ready, g + 1)
                    else:
                        wait_free(dve, ("Y1" if job == "Y2" else "Y2", g))
                    frees(dve.tensor_tensor(out=tY, in0=bank((job, g)), in1=tY, op=ALU.add), (job, g))
                wait_full(dve, ("Q", g))
                dve.tensor_copy(tN, bank(("Q", g))).then_inc(free[jobs[("Q", g)][0]], 1)
                wait_free(dve, ("Q", g))
                dve.scalar_tensor_tensor(out=heads(tC), in0=heads(tN), scalar=-1.0, in1=mid(ident[:, :], GH),
                                         op0=ALU.mult, op1=ALU.add).then_inc(c0_ready, 1)
                wait_full(dve, ("C", g))
                dve.wait_ge(c0_ready, g + 1)
                frees(dve.tensor_tensor(out=tC, in0=bank(("C", g)), in1=tC, op=ALU.add), ("C", g))
                for n in (2 * g, 2 * g + 1):
                    b0 = CH * (n % 2)
                    rows = slice(b0, b0 + CH)
                    wait_full(dve, ("ws", n))
                    wait_free(dve, ("u", g))
                    frees(dve.tensor_tensor(out=vn[rows, :], in0=uB[g % 2][rows, :], in1=bank(("ws", n))[rows, :],
                                            op=ALU.subtract), ("ws", n))
                    wait_full(dve, ("su", n))
                    last = (n + 1) * CH - 1
                    for h in range(GH):
                        hs = slice(h * P, (h + 1) * P)
                        ins = dve.scalar_tensor_tensor(out=St[:, hs], in0=St[:, hs], scalar=expG[:, h, last:last + 1],
                                                       in1=bank(("su", n))[:, hs], op0=ALU.mult, op1=ALU.add)
                    frees(ins, ("su", n))
            for h in range(GH):
                wait_free(dve, ("oss", h))
                link(dve.reciprocal(FT[:, h, :], FT[:, h, :]))
                link(dve.scalar_tensor_tensor(out=OBT[:, h, :], in0=OBT[:, h, :], scalar=gcols[:, 3 * KD:3 * KD + 1],
                                              in1=FT[:, h, :], op0=ALU.mult, op1=ALU.mult))
                dve.tensor_tensor(out=OBT[:, h, :], in0=OBT[:, h, :], in1=gzT[:, h, :],
                                  op=ALU.mult).then_inc(ob_ready, 1)
            for c in range(KD):
                wait_full(dve, ("ya", c))
                wait_free(dve, ("ga", c))
                link(dve.tensor_tensor(out=FT[:, 6, :], in0=bank(("ya", c)), in1=FT[:, 4, :], op=ALU.mult))
                dve.sem_inc(free[jobs[("ya", c)][0]], 1)
                wait_full(dve, ("yb", c))
                wait_free(dve, ("gb", c))
                link(dve.tensor_tensor(out=FT[:, 7, :], in0=bank(("yb", c)), in1=FT[:, 5, :], op=ALU.mult))
                dve.sem_inc(free[jobs[("yb", c)][0]], 1)
                dve.sem_inc(sig_used, 1)
                dve.tensor_tensor(out=mixT[:, c, :], in0=FT[:, 6, :], in1=FT[:, 7, :],
                                  op=ALU.add).then_inc(mix_ready, 1)
                dve.wait_ge(mix_ready, c + 1)
            dve.wait_ge(x_landed, 16)
            for i in range(NT):
                dve.wait_ge(mroot_ready, 2 * i + 1)
                link(dve.reciprocal(stat[:, 40:41], stat[:, 20 + i:21 + i]))
                for half in range(2):
                    hs = slice(half * S, (half + 1) * S)
                    dve.scalar_tensor_tensor(out=H2[:, i, hs], in0=bank(("mix", i, half)), scalar=stat[:, 40:41],
                                             in1=mods[:, 0, hs], op0=ALU.mult,
                                             op1=ALU.mult).then_inc(free[jobs[("mix", i, half)][0]], 1)
                wait_free(dve, ("mix", i, 0))
                wait_free(dve, ("mix", i, 1))
                dve.tensor_tensor(out=X[:, i, :], in0=X[:, i, :], in1=H2[:, i, :], op=ALU.add).then_inc(x1_ready, 1)
                dve.wait_ge(mroot_ready, 2 * i + 2)
                link(dve.reciprocal(stat[:, 41:42], stat[:, 28 + i:29 + i]))
                link(dve.scalar_tensor_tensor(out=H2[:, i, :], in0=X[:, i, :], scalar=stat[:, 41:42], in1=mods[:, 2, :],
                                              op0=ALU.mult, op1=ALU.mult))
                dve.tensor_tensor(out=H2[:, i, :], in0=H2[:, i, :], in1=mods[:, 1, :],
                                  op=ALU.add).then_inc(h2_ready, 1)
            for q in range(N_Q - 8, N_Q):
                wait_free(dve, ("sc", q))
            dve.wait_ge(h2_ready, NT)
            dve.sem_inc(u_free, USL)

            def chain(ins):
                dve.drain()

            with dve.Fori(0, NT) as i:
                with dve.Fori(0, PH // 2) as b:
                    for p in range(2):
                        head = i * PH + b * 2 + p
                        chain(dve.tensor_copy(st1, scores[:, bass.ds(head, 1), :].rearrange("p a k -> p (a k)")))
                        for s in range(2):
                            v, ix = kv[:, s * TOPK:(s + 1) * TOPK], ki[:, s * TOPK:(s + 1) * TOPK]
                            a, z = st1[:, s * NK:(s + 1) * NK], st2[:, s * NK:(s + 1) * NK]
                            chain(dve.max(v[:, 0:8], a))
                            dve.max_index(ix[:, 0:8], v[:, 0:8], a)
                            chain(dve.match_replace(z, v[:, 0:8], a, LOWEST))
                            chain(dve.max(v[:, 8:16], z))
                            dve.max_index(ix[:, 8:16], v[:, 8:16], z)
                        chain(dve.tensor_tensor(out=cand.rearrange("p (a b) -> p a b", a=TOPK),
                                                in0=bcast(kv[:, 0:TOPK], TOPK), in1=mid(kv[:, TOPK:2 * TOPK], TOPK),
                                                op=ALU.add))
                        chain(dve.max(tops[p][:, 0:8], cand))
                        dve.max_index(pos[:, 0:8], tops[p][:, 0:8], cand)
                        chain(dve.match_replace(cand2, tops[p][:, 0:8], cand, LOWEST))
                        chain(dve.max(tops[p][:, 8:16], cand2))
                        dve.max_index(pos[:, 8:16], tops[p][:, 8:16], cand2)
                        dve.tensor_scalar(gate[p][:, TOPK:TOPK + 1], tops[p][:, 0:1], -1.0, None,
                                          ALU.mult).then_inc(top_ready, 1)
                        chain(dve.tensor_copy(kf, ki))
                        dve.tensor_scalar(pa, pos, 4, None, ALU.logical_shift_right)
                        chain(dve.tensor_scalar(pb, pos, 15, None, ALU.bitwise_and))
                        dve.tensor_copy(paf, pa)
                        chain(dve.tensor_copy(pbf, pb))
                        for posf, s, e in ((paf, 0, e1), (pbf, 1, e2)):
                            oh = onehot.rearrange("p (a b) -> p a b", a=TOPK)
                            pk = picked.rearrange("p (a b) -> p a b", a=TOPK)
                            chain(dve.tensor_tensor(out=oh, in0=bcast(posf, TOPK), in1=mid(iota16[:, :], TOPK),
                                                    op=ALU.is_equal))
                            chain(dve.tensor_tensor(out=pk, in0=oh, in1=mid(kf[:, s * TOPK:(s + 1) * TOPK], TOPK),
                                                    op=ALU.mult))
                            chain(dve.tensor_reduce(e, pk, AX.X, ALU.add))
                        dve.scalar_tensor_tensor(out=idx_sb[p][:, :], in0=e1, scalar=float(NK), in1=e2,
                                                 op0=ALU.mult, op1=ALU.add).then_inc(idx_ready, 1)
                        for k in range(TOPK):
                            slot = k % USL
                            dve.wait_ge(u_landed[slot], head * (16 * TOPK // USL) + (k // USL + 1) * 16)
                            u = arena[:, slot, :]
                            dve.scalar_tensor_tensor(
                                out=u, in0=u, scalar=1.0, in1=H2[:, bass.ds(i, 1), :].rearrange("p a b -> p (a b)"),
                                op0=ALU.mult, op1=ALU.mult, accum_out=dots[p][:, k:k + 1]).then_inc(u_free, 1)
                        dve.wait_ge(gate_ready, head + 1)
                        chain(dve.reciprocal(gate[p][:, TOPK + 2:TOPK + 3], gate[p][:, TOPK + 1:TOPK + 2]))
                        dve.wait_ge(gelu_ready, head + 1)
                        dve.scalar_tensor_tensor(out=wts[p][:, :], in0=acts[p][:, :],
                                                 scalar=gate[p][:, TOPK + 2:TOPK + 3], in1=gate[p][:, 0:TOPK],
                                                 op0=ALU.mult, op1=ALU.mult).then_inc(wts_ready, 1)
            dve.wait_ge(froot_ready, 1)
            link(dve.reciprocal(stat[:, 42:42 + NT], stat[:, 36:36 + NT]))
            for i in range(NT):
                link(dve.scalar_tensor_tensor(out=ystore[:, i, :], in0=ystore[:, i, :], scalar=stat[:, 42 + i:43 + i],
                                              in1=mods[:, 3, :], op0=ALU.mult, op1=ALU.mult))
                dve.tensor_tensor(out=X[:, i, :], in0=X[:, i, :], in1=ystore[:, i, :],
                                  op=ALU.add).then_inc(fin_ready, 1)

        @block.tensor
        def _(pe):
            n_w = [0]

            def weights(n):
                assert n == n_w[0], (n, n_w[0])
                n_w[0] += 1
                pe.wait_ge(w_landed[n % RING], 16 * (n // RING + 1))
                return ring[:, n % RING, :, :]

            def begin(job):
                b, n = jobs[job]
                if n > 1:
                    pe.wait_ge(free[b], n - 1)
                return PS[:, b, :]

            def done(ins, job):
                ins.then_inc(full[jobs[job][0]], 1)

            def past(ins, n, first):
                if first and n:
                    ins.then_inc(w_used, 1)

            pe.wait_ge(silu_ready, 1)
            ps = begin(("ada_col",))
            for c in range(N_COL):
                w = weights(W_COL + c)
                for k in range(KD):
                    ins = pe.matmul(ps[:, c:c + 1], w[:, k, :], silu_c[:, k:k + 1], start=(k == 0), stop=(k == KD - 1))
                    past(ins, W_COL + c, k == 0)
            done(ins, ("ada_col",))
            pe.wait_ge(consts_ready, 1)
            ps = begin(("xsq",))
            for k in range(KD):
                pe.wait_ge(sq_ready, k + 1)
                ins = pe.matmul(ps, ones[:, :], FQK[:, k, :], start=(k == 0), stop=(k == KD - 1))
            done(ins, ("xsq",))
            ps = begin(("small",))
            for k in range(KD):
                pe.wait_ge(h_ready, k + 1)
                ins = pe.matmul(ps[0:68, :], wsm[:, k, 0:68], hT[:, k, :], start=(k == 0), stop=(k == KD - 1))
            done(ins, ("small",))

            def project(job, n, src, ks=range(KD), srcs=range(KD), first=True):
                w = weights(n) if first else ring[:, n % RING, :, :]
                ps = begin(job)
                for k, m in zip(ks, srcs):
                    ins = pe.matmul(ps, w[:, k, :], src[:, m, :], start=(k == ks[0]), stop=(k == ks[-1]))
                    past(ins, n, first and k == ks[0])
                done(ins, job)

            for c in range(N_CONV):
                project(("conv", c), W_CONV + c, hT)
            for c in range(N_GZ):
                project(("gz", c), W_GZ + c, hT)
            for h in range(2 * GH):
                ps = begin(("ssq", h))
                pe.wait_ge(gsq_ready, h + 1)
                done(pe.matmul(ps, ones[:, :], FT[:, 3 + h % 2, :], start=True, stop=True), ("ssq", h))
            for n, which in enumerate(("fq", "fk")):
                for c in range(4):
                    project((which, c), W_F + 4 * n + c, hT)
            for c in range(4):
                w = weights(W_F + 8 + c)
                ps = begin(("fv", c))
                for i in range(NT):
                    for k in range(KD):
                        ins = pe.matmul(ps[:, i * P:(i + 1) * P], hT[:, k, i * P:(i + 1) * P], w[:, k, :],
                                        start=(k == 0), stop=(k == KD - 1))
                        past(ins, W_F + 8 + c, i == 0 and k == 0)
                done(ins, ("fv", c))

            pe.wait_ge(rows_ready, 3)
            ps = begin(("cols",))
            for i in range(NT):
                ins = pe.transpose(ps[:, i * P:(i + 1) * P], R[:, i * P:(i + 1) * P], ident[:, :])
            done(ins, ("cols",))

            pe.wait_ge(silub_ready, 1)
            for c in range(2 * NT):
                ps = begin(("row", c))
                for j in range(4):
                    w = weights(W_ROW + 4 * c + j)
                    for k in range(KD):
                        ins = pe.matmul(ps[:, j * P:(j + 1) * P], silu_cb[:, k, :], w[:, k, :],
                                        start=(k == 0), stop=(k == KD - 1))
                        past(ins, W_ROW + 4 * c + j, k == 0)
                done(ins, ("row", c))

            pe.wait_ge(aug_landed, 2 * FH * 16)
            pe.wait_ge(cum_ready, 3)
            for c in range(4):
                for which in ("fq", "fk", "fv"):
                    wait_free(pe, (which, c))
            units = [(h, i) for h in range(FH) for i in range(NT)]

            def attend(n):
                h, i = units[n]
                pe.wait_ge(pn_ready, n + 1)
                ps = begin(("PT", h, i))
                for j in range(i + 1):
                    ins = pe.transpose(ps[:, j * P:(j + 1) * P], FT[:, n % 2, j * P:(j + 1) * P], ident[:, :])
                done(ins, ("PT", h, i))

            def values(n):
                h, i = units[n]
                wait_free(pe, ("PT", h, i))
                ps = PS[:, 7, :] if i else begin(("O", h))
                for j in range(i + 1):
                    ins = pe.matmul(ps[0:FDH, i * P:(i + 1) * P], Vr[:, j, h * FDH:(h + 1) * FDH],
                                    FT[:, 2 + n % 2, j * P:(j + 1) * P], start=(j == 0), stop=(j == i))
                if i == NT - 1:
                    done(ins, ("O", h))

            for n, (h, i) in enumerate(units):
                ps = begin(("S", h, i))
                w = (i + 1) * P
                pe.matmul(ps[:, 0:w], qaug[0:66, h, i * P:(i + 1) * P], kaug[0:66, h, 0:w], start=True, stop=False)
                done(pe.matmul(ps[:, i * P:w], ident[:, :], fox_mask[:, :], start=False, stop=True), ("S", h, i))
                if n:
                    attend(n - 1)
                if n >= 2:
                    values(n - 2)
            values(len(units) - 2)
            attend(len(units) - 1)
            values(len(units) - 1)

            for job, b0 in (("bg", 0), ("bb", 32)):
                for h in range(GH):
                    ps = begin((job, h))
                    done(pe.matmul(ps, sel[b0:b0 + GH, h, :], R[b0:b0 + GH, :], start=True, stop=True), (job, h))

            def four(job, g, lhs, rhs):
                ps = begin((job, g))
                for h in range(GH):
                    ins = pe.matmul(ps[:, h * P:(h + 1) * P], lhs(h), rhs(h), start=True, stop=True)
                done(ins, (job, g))

            def turn(job, g, src):
                ps = begin((job, g))
                for h in range(GH):
                    ins = pe.transpose(ps[:, h * P:(h + 1) * P], src(h), ident[:, :])
                done(ins, (job, g))

            def of(tile):
                return lambda h: tile[:, h * P:(h + 1) * P]

            def at(tile, tok):
                return lambda h: tile[:, h, tok]

            pe.wait_ge(qkn_ready, 2 * GH)
            pe.wait_ge(conv_silu, N_CONV)
            pe.wait_ge(qd_ready, GH)
            pe.wait_ge(state_zero, 1)
            for h in range(GH):
                wait_free(pe, ("bb", h))
            for g in range(NT):
                tok = slice(g * P, (g + 1) * P)
                turn("kt", g, at(kT, tok))
                turn("vt", g, at(vT, tok))
                four("kk", g, at(kT, tok), at(kbT, tok))
                four("qk", g, at(kT, tok), at(qT, tok))
                pe.wait_ge(near_ready, 2 * g + 2)
                turn("D", g, of(tN))
                turn("E", g, of(tET))
                wait_free(pe, ("D", g))
                four("D2", g, of(tN), of(tD))
                four("N2", g, of(tD), of(tN))
                wait_free(pe, ("D2", g))
                pe.wait_ge(y0_ready, g + 1)
                four("Y1", g, of(tA), of(tY))
                wait_free(pe, ("N2", g))
                four("D4", g, of(tB), of(tA))
                four("N4", g, of(tA), of(tB))
                wait_free(pe, ("D4", g))
                wait_free(pe, ("Y1", g))
                four("Y2", g, of(tD), of(tY))
                wait_free(pe, ("N4", g))
                four("D8", g, of(tN), of(tD))
                wait_free(pe, ("D8", g))
                wait_free(pe, ("Y2", g))
                four("Y3", g, of(tA), of(tY))
                wait_free(pe, ("Y3", g))
                turn("W", g, of(tY))
                wait_free(pe, ("E", g))
                four("M", g, of(tY), of(tE))
                four("Q", g, of(tE), of(tY))
                wait_free(pe, ("M", g))
                wait_free(pe, ("Q", g))
                four("M2", g, of(tN), of(tD))
                wait_free(pe, ("M2", g))
                pe.wait_ge(c0_ready, g + 1)
                four("C", g, of(tA), of(tC))
                wait_free(pe, ("C", g))
                wait_free(pe, ("W", g))
                four("TT", g, of(tB), of(tC))
                wait_free(pe, ("TT", g))
                wait_free(pe, ("vt", g))
                wait_free(pe, ("kt", g))
                four("u", g, of(tET), of(rv))
                four("wT", g, of(rw), of(tET))
                wait_free(pe, ("wT", g))
                wait_free(pe, ("qk", g))
                for n in (2 * g, 2 * g + 1):
                    b0 = CH * (n % 2)
                    rows = slice(b0, b0 + CH)
                    if n:
                        wait_free(pe, ("su", n - 1))
                    ps = begin(("ws", n))
                    for h in range(GH):
                        hs = slice(h * P, (h + 1) * P)
                        ins = pe.matmul(ps[rows, hs], wB[g % 2][:, h * P + b0:h * P + b0 + CH], St[:, hs],
                                        start=True, stop=True)
                    done(ins, ("ws", n))
                    wait_free(pe, ("ws", n))
                    ps = begin(("o", n))
                    for h in range(GH):
                        hs = slice(h * P, (h + 1) * P)
                        dst = ps[:, h * CH:(h + 1) * CH]
                        pe.matmul(dst, St[:, hs], qdT[:, h, n * CH:(n + 1) * CH], start=True, stop=False)
                        ins = pe.matmul(dst, vn[rows, hs], aB[g % 2][rows, h * P + b0:h * P + b0 + CH],
                                        start=False, stop=True)
                    done(ins, ("o", n))
                    ps = begin(("su", n))
                    for h in range(GH):
                        hs = slice(h * P, (h + 1) * P)
                        ins = pe.matmul(ps[:, hs], kdB[g % 2][rows, hs], vn[rows, hs], start=True, stop=True)
                    done(ins, ("su", n))
            for h in range(GH):
                pe.wait_ge(osq_ready, h + 1)
                ps = begin(("oss", h))
                done(pe.matmul(ps, ones[:, :], Vr[:, h, :], start=True, stop=True), ("oss", h))

            for h in range(FH):
                wait_free(pe, ("O", h))
            for c in range(KD):
                n = W_MIX + 3 * c
                project(("ga", c), n, hT)
                project(("gb", c), n + 1, hT)
                project(("ya", c), n + 2, OT, range(4), range(4))
                pe.wait_ge(ob_ready, GH)
                project(("yb", c), n + 2, OBT, range(4, 8), range(4), first=False)
            pe.wait_ge(mix_ready, KD)
            for half in range(2):
                banks = [begin(("mix", i, half)) for i in range(NT)]
                for c in range(4):
                    n = W_OUT + 4 * half + c
                    w = weights(n)
                    for i in range(NT):
                        for k in range(KD):
                            ins = pe.matmul(banks[i][:, c * P:(c + 1) * P], mixT[:, k, i * P:(i + 1) * P], w[:, k, :],
                                            start=(k == 0), stop=(k == KD - 1))
                            past(ins, n, i == 0 and k == 0)
                        if c == 3:
                            done(ins, ("mix", i, half))
            for i in range(NT):
                pe.wait_ge(h2_ready, i + 1)
                for half in range(2):
                    ps = begin(("h2T", i, half))
                    for k in range(4):
                        ins = pe.transpose(ps[:, k * P:(k + 1) * P],
                                           H2[:, i, half * S + k * P:half * S + (k + 1) * P], ident[:, :])
                    done(ins, ("h2T", i, half))
            for i in range(NT):
                for half in range(2):
                    wait_free(pe, ("h2T", i, half))
            project(("qy", 0), W_Q, hT)
            pe.wait_ge(keys_landed, 16)
            for q in range(N_Q):
                if q + 1 < N_Q:
                    project(("qy", q + 1), W_Q + q + 1, hT)
                wait_free(pe, ("qy", q))
                ps = begin(("sc", q))
                for i in range(NT):
                    ins = pe.matmul(ps[:, i * P:(i + 1) * P], FT[:, 2 + q % 2, i * P:(i + 1) * P], keys[:, q % 2, :],
                                    start=True, stop=True)
                done(ins, ("sc", q))
            assert n_w[0] == N_W

            pe.sem_inc(v_free, VSL)
            with pe.Fori(0, NT) as i:
                pe.wait_ge(y_zero, i + 1)
                pe.sem_inc(seen_pe, 1)
                with pe.Fori(0, PH // 2) as b:
                    for p in range(2):
                        head = i * PH + b * 2 + p
                        for k in range(TOPK):
                            slot = k % VSL
                            pe.wait_ge(diag_ready, head * TOPK + (k + 1))
                            pe.wait_ge(v_landed[slot], head * (16 * TOPK // VSL) + (k // VSL + 1) * 16)
                            for half in range(2):
                                ins = pe.matmul(PS[:, half, :], diag[:, k % NDG, :],
                                                arena[:, USL + slot, half * S:(half + 1) * S],
                                                start=False, stop=False, skip_group_check=True)
                            ins.then_inc(v_free, 1)


def kernel(x, c, w_ada, b_ada, g_pre_mix, g_post_mix, w_in, b_fgate, fox_w_o, conv_w, a_log, dt_bias,
           gdn_norm_w, gdn_w_o, b_branch_gate, w_out, g_pre_ffn, g_post_ffn, peer_w_query, peer_keys1,
           peer_keys2, peer_u, peer_v):
    import concourse.bacc as bacc
    from concourse.bass_utils import run_bass_kernel_spmd as run

    def tiles(m):
        m = np.asarray(m)
        k, n = m.shape
        return m.reshape(k // P, P, n // P, P).transpose(2, 1, 0, 3).reshape(n // P, P, k)

    def cols(v):
        return np.asarray(v).reshape(-1, P).T

    wi = np.asarray(w_in)[0]
    cut = np.cumsum([0, 512, 512, 512, FH, 512, 512, 512, 512, GH, GH, D, D])
    fq, fk, fv, f, gq, gk, gv, gz, beta, decay, ga, gb = (wi[:, a:b] for a, b in zip(cut[:-1], cut[1:]))
    ada = np.asarray(w_ada)[0]
    mix = np.stack([tiles(ga), tiles(gb), np.concatenate([tiles(fox_w_o[0]), tiles(gdn_w_o[0])], axis=2)], axis=1)
    w_tiles = np.concatenate([
        tiles(ada[:, 0:2 * D]), tiles(gq), tiles(gk), tiles(gv), tiles(gz), tiles(fq), tiles(fk), tiles(fv),
        tiles(ada[:, 2 * D:6 * D]), mix.reshape(3 * KD, P, D), tiles(w_out[0]), tiles(peer_w_query[0])], axis=0)
    small = np.concatenate([f, beta, decay], axis=1).reshape(KD, P, 16).transpose(1, 0, 2).reshape(P, KD * 16)
    bias = np.asarray(b_ada)[0]
    arrays = {
        "x_rows": np.asarray(x)[0].reshape(NT, P, D).transpose(1, 0, 2),
        "x_cols": np.asarray(x)[0].T.reshape(KD, P, S).transpose(1, 0, 2),
        "c_cols": cols(c),
        "w_tiles": w_tiles,
        "w_small": small,
        "b_small": np.concatenate([np.asarray(b_fgate)[0], np.asarray(dt_bias)[0], np.asarray(a_log)[0]]).reshape(-1, 1),
        "ada_cols": cols(bias[0:2 * D]),
        "ada_rows": bias[2 * D:6 * D],
        "gains_cols": np.concatenate([cols(g_pre_mix), cols(np.asarray(b_branch_gate)[0, 0]),
                                      cols(np.asarray(b_branch_gate)[0, 1]), cols(gdn_norm_w)], axis=1),
        "gain_rows": np.concatenate([np.asarray(g_post_mix)[0], np.asarray(g_pre_ffn)[0], np.asarray(g_post_ffn)[0]]),
        "conv_cols": np.asarray(conv_w)[0].T.reshape(N_CONV, P, CONV).transpose(1, 0, 2),
        "keys_t": np.stack([np.asarray(peer_keys1)[0].T, np.asarray(peer_keys2)[0].T], axis=1),
        "peer_u": np.asarray(peer_u)[0],
        "peer_v": np.asarray(peer_v)[0],
    }
    nc = bacc.Bacc("TRN2", target_bir_lowering=False, num_devices=1)
    fed, args = {}, {}
    for name, a in arrays.items():
        a = np.ascontiguousarray(a)
        fed[f"in_{name}"] = a
        args[name] = nc.dram_tensor(f"in_{name}", a.shape, mybir.dt.from_np(a.dtype), kind="ExternalInput").ap()
    out = nc.dram_tensor("out_x", (NT, P, D), F32, kind="ExternalOutput").ap()
    hybrid_block(nc, out=out, **args)
    return run(nc, [fed], core_ids=[0]).results[0]["out_x"].reshape(1, S, D)
```

```python
from contextlib import ExitStack

import numpy as np

import concourse.bass as bass
from concourse import mybir

P = 128
D = 1024
KD = D // P
S = 512
NT = S // P
HS = S // 2
HT = NT // 2
FH, FDH = 8, 64
GH = 4
CH = 64
CONV = 4
PH = 8
NK = 128
TOPK = 16
EPS = 1e-6
NEG = -1.0e30
LOWEST = -3.0e38

RING = 4
SLOTS = (5, 8)
NDG = 4
LAG = (1, 2)
HEADS = HT * PH
NEXP = HEADS * TOPK

N_COL = 2 * KD
N_ROW = 4 * KD
N_CONV = 12
N_GZ = 4
N_F = 12
N_MIX = 3 * KD
N_OUT = KD
N_Q = 16
W_COL = 0
W_ROW = W_COL + N_COL
W_CONV = W_ROW + N_ROW
W_GZ = W_CONV + N_CONV
W_F = W_GZ + N_GZ
W_MIX = W_F + N_F
W_OUT = W_MIX + N_MIX
W_Q = W_OUT + N_OUT
N_W = W_Q + N_Q
N_AGAIN = N_W - W_CONV

F32 = mybir.dt.float32
U32 = mybir.dt.uint32
ALU = mybir.AluOpType
ACT = mybir.ActivationFunctionType
AX = mybir.AxisListType

TURN, BANK_O, BANK_Y = 5, 5, 6


def attention_stages(u):
    return [(("att", u, n), 2.2 if u else 1.2) for n in range(FH * HT)] + [(("att", u, FH * HT), 1.0),
                                                                          (("att", u, FH * HT + 1), 1.0)]


def deltanet_stages(u):
    out = [(("spread", u), 3.4)]
    for g in (HT * u, HT * u + 1):
        out += [((name, g), cost) for name, cost in (
            ("kv", 0.5), ("kk", 1.7), ("turn", 0.5), ("sq2", 1.7), ("sq4", 2.6), ("sq8", 1.7), ("inv", 0.9),
            ("wmq", 1.9), ("m2", 0.9), ("c", 0.9), ("tt", 0.9), ("uw", 1.7))]
        for n in (2 * g, 2 * g + 1):
            out += [(("ws", n), 0.9), (("os", n), 1.8)]
    return out


def first_stages(u):
    out = [(("norm", u), 3.4), (("small", u), 3.4)]
    out += [(("conv", u, c), 3.4) for c in range(N_CONV)] + [(("gz", u, c), 3.4) for c in range(N_GZ)]
    out += [(("unit", u, j), 0.9) for j in range(4)]
    out += [((w, u, c), 3.4) for w in ("fq", "fk", "fv") for c in range(4)]
    return out + [(("cols", u), 0.2)]


def last_stages(u):
    out = [(("onorm", u), 1.8)]
    for c in range(KD):
        out += [(("ga", u, c), 3.4), (("gb", u, c), 3.4), (("yab", u, c), 3.4)]
    out += [(("out", u, half, c), 3.4) for half in range(2) for c in range(4)]
    out += [(("x1", u, i), 0.5) for i in range(HT)]
    out += [(("qy", u, 0), 6.8)]
    for j in range(N_Q // 2):
        out += ([(("qy", u, j + 1), 6.8)] if j + 1 < N_Q // 2 else []) + [(("sc", u, j), 1.8)]
    return out


def woven(a, b):
    tagged = [((n + 0.5) / len(a), 0, x) for n, x in enumerate(a)] + [((n + 0.5) / len(b), 1, x) for n, x in enumerate(b)]
    return [x for _, _, x in sorted(tagged, key=lambda t: t[:2])]


def build_order():
    order = []

    def now(stages):
        for stage, _ in stages:
            order.extend([("pe",) + stage, ("post",) + stage])

    now([(("ada_col",), 0)])
    now([(("row", c), 0) for c in range(2 * NT)])
    now(first_stages(0))
    now(woven(attention_stages(0), deltanet_stages(0)))
    now(last_stages(0))
    front = first_stages(1) + attention_stages(1) + deltanet_stages(1) + last_stages(1)
    total = sum(cost for _, cost in front)
    order.append(("choose_all", 0))
    order.append(("sums", 0))
    spent, gone, pending = 0.0, 0, None
    for n in range(NEXP):
        h, k = divmod(n, TOPK)
        if k == 0:
            order.append(("gates", h))
            if h % PH == 0 and h:
                order.append(("sums", h // PH))
        order.append(("expert", h, k))
        if pending:
            order.append(("post",) + pending)
            pending = None
        if k % 3 == 0 and k // 3 < 4 and h + 1 < HEADS:
            order.append(("choose", h + 1, k // 3))
        while gone < len(front) and spent < total * (n + 1) / (NEXP - 8):
            if pending:
                order.append(("post",) + pending)
            pending, cost = front[gone]
            order.append(("pe",) + pending)
            spent += cost
            gone += 1
    assert gone == len(front)
    if pending:
        order.append(("post",) + pending)
    return order


JOBS = {
    "kv": ("kt", "vt"), "kk": ("kk", "qk"), "turn": ("D", "E"), "sq2": ("D2", "N2"), "sq4": ("Y1", "D4", "N4"),
    "sq8": ("Y2", "D8"), "inv": ("Y3",), "wmq": ("W", "M", "Q"), "m2": ("M2",), "c": ("C",), "tt": ("TT",),
    "uw": ("u", "wT"), "ws": ("ws",), "os": ("o", "su"),
}


def jobs_of(stage):
    name, *a = stage
    if name == "norm":
        return [("xsq", *a)]
    if name == "att":
        u, n = a
        out = [("S", u, n)] if n < FH * HT else []
        out += [("PT", u, n - 1)] if 1 <= n <= FH * HT else []
        return out + ([("O", u, (n - 2) // HT)] if n >= 2 and n % HT == 0 else [])
    if name == "spread":
        return [("bg", a[0], j) for j in range(2)] + [("bb", a[0], j) for j in range(2)]
    if name == "onorm":
        return [("oss", a[0], j) for j in range(2)]
    if name == "out":
        u, half, c = a
        return [("mix", HT * u + i, half) for i in range(HT)] if c == 0 else []
    if name == "x1":
        u, i = a
        return [("h2T", HT * u + i, half) for half in range(2)]
    if name in JOBS:
        return [(j, *a) for j in JOBS[name]]
    return [stage]


def psum_jobs(order):
    table, used, turn = {}, [0] * 8, 0
    for item in order:
        if item[0] != "pe":
            continue
        for job in jobs_of(item[1:]):
            if job[0] == "O":
                bank = BANK_O
            else:
                bank = turn % TURN
                turn += 1
            used[bank] += 1
            assert job not in table
            table[job] = (bank, used[bank])
    return table


def hybrid_block(nc, x_rows, x_cols, c_cols, w_tiles, w_small, b_small, ada_cols, ada_rows, gains_cols,
                 gain_rows, conv_cols, keys_t, experts, out):
    order = build_order()
    jobs = psum_jobs(order)
    ctx = ExitStack()
    with ctx:
        def sb(name, shape, dt=F32):
            return ctx.enter_context(nc.sbuf_tensor(name, shape, dt))

        def sem(name):
            return ctx.enter_context(nc.semaphore(name))

        ident = sb("ident", [P, P])
        ones = sb("ones", [P, P])
        near = sb("near_mask", [P, P])
        far = sb("far_mask", [P, P])
        causal = sb("causal_mask", [P, P])
        fox_mask = sb("fox_mask", [P, P])
        iota16 = sb("iota16", [P, TOPK])
        eps = sb("eps", [P, 1])
        scan_a = sb("scan_a", [68, HS])
        c_sb = sb("c_sb", [P, KD])
        silu_c = sb("silu_c", [P, KD])
        small_b = sb("small_b", [P, 4])
        bcol = sb("bcol", [P, N_COL])
        gcols = sb("gcols", [P, 3 * KD + 1])
        convw = sb("convw", [P, N_CONV, CONV])
        tails = sb("tails", [P, N_CONV, CONV - 1])
        keys = sb("keys", [P, 2, NK])
        scale1 = sb("scale1", [P, KD])
        shift1 = sb("shift1", [P, KD])
        stat = sb("stat", [P, 56])
        carry = sb("carry", [FH, 1])
        R = sb("R", [P, HS])
        rcols = sb("rcols", [P, HT, P])
        X = sb("X", [P, NT, D])
        mods = sb("mods", [P, 4, D])
        H2 = sb("H2", [P, NT, D])
        pool_e = sb("pool_e", [P, SLOTS[0], 2 * D])
        ring_t = sb("ring", [P, RING, D])
        hT = sb("hT", [P, KD, HS])
        kaug = sb("kaug", [P, FH, S])
        qaug = sb("qaug", [P, FH, HS])
        Vr = sb("Vr", [P, NT, S])
        gT = sb("gT", [P, N_CONV, HS])
        gzT = sb("gzT", [P, GH, HS])
        OT = sb("OT", [P, NT, HS])
        OBT = sb("OBT", [P, GH, HS])
        scores0 = sb("scores0", [P, HEADS, 2 * NK])
        FT = sb("FT", [P, 4, S])
        St = sb("St", [P, S])
        diag = sb("diag", [P, NDG, P])
        work = sb("work", [P, 2, 2 * NK])
        kv = sb("kv", [P, 2 * TOPK])
        ki = sb("ki", [P, 2 * TOPK], U32)
        kf = sb("kf", [P, 2 * TOPK])
        pos = sb("pos", [P, 3 * TOPK], U32)
        posf = sb("posf", [P, 4 * TOPK])
        idx_sb = [sb(f"idx{p}", [P, TOPK], U32) for p in range(2)]
        tops = [sb(f"tops{p}", [P, TOPK]) for p in range(2)]
        gate = [sb(f"gate{p}", [P, TOPK + 4]) for p in range(2)]
        dots = [sb(f"dots{p}", [P, TOPK]) for p in range(2)]
        acts = [sb(f"acts{p}", [P, TOPK]) for p in range(2)]
        wts = [sb(f"wts{p}", [P, TOPK]) for p in range(2)]

        ring = ring_t[:, :, :].rearrange("p s (k m) -> p s k m", k=KD)
        scores = (scores0[:, :, :], kaug[:, :, :].rearrange("p h (a k) -> p (h a) k", a=2))
        slots = ([pool_e[:, s, :] for s in range(SLOTS[0])],
                 [pool_e[:, s, :] for s in range(SLOTS[0])] + [
                     qaug[:, :, :].rearrange("p h t -> p (h t)"), Vr[:, :, :].rearrange("p h t -> p (h t)"),
                     gT[:, 0:8, :].rearrange("p h t -> p (h t)")])
        silu_cb = Vr[:, 0:2, :].rearrange("p a (k m) -> p (a k) m", m=P)
        grow = pool_e[:, 0:2, :].rearrange("p a (b d) -> p (a b) d", b=2)[:, 0:3, :]
        high = H2[:, HT:NT, :].rearrange("p a (b t) -> p (a b) t", t=HS)
        Z, T1, T2, T3, T4 = (high[:, n, :] for n in range(5))
        CF = T3
        wsm = H2[:, HT:NT, :].rearrange("p a d -> p (a d)")[:, 5 * HS:5 * HS + KD * 68].rearrange(
            "p (k m) -> p k m", k=KD)
        wsm_in = FT[:, 3, 0:KD * 16]
        sq = FT[:, :, :].rearrange("p a (b t) -> p (a b) t", b=2)
        flat = FT[:, :, :].rearrange("p a t -> p (a t)")
        pads = [flat[:, n * 260:n * 260 + HS + CONV - 1] for n in range(2)]
        mixT = qaug[:, :, :]

        free_x = X[:, HT:NT, :].rearrange("p a (b t) -> p (a b) t", b=2)
        free_h = H2[:, HT:NT, :].rearrange("p a (b t) -> p (a b) t", b=2)
        space = (
            [pool_e[:, s, t * S:(t + 1) * S] for s in range(SLOTS[0]) for t in range(4)] + [free_x[:, t, :] for t in range(4)],
            [kaug[:, t, :] for t in range(FH)] + [Vr[:, t, :] for t in range(NT)]
            + [qaug[:, 2 * t:2 * t + 2, :].rearrange("p a b -> p (a b)") for t in range(4)]
            + [free_x[:, t, :] for t in range(4)] + [free_h[:, t, :] for t in range(4)])

        def pair(u, n):
            return [space[u][n + h // 2][:, (h % 2) * HS:(h % 2 + 1) * HS] for h in range(GH)]

        names = ("A", "B", "N", "ET", "DD", "E", "Y", "C", "rv", "rw", "vn", "u", "w", "a", "kd")
        dn = [{name: space[u][8 + n] for n, name in enumerate(names)} for u in range(2)]
        Gb, expG, kbT, qdT = ([pair(u, 2 * n) for u in range(2)] for n in range(4))
        qT, kT, vT = gT[:, 0:4, :], gT[:, 4:8, :], gT[:, 8:12, :]

        PS = ctx.enter_context(nc.psum_tensor("PS", [P, 8, S], F32))

        def bank(job):
            return PS[:, jobs[job][0], :]

        full = [sem(f"full{b}") for b in range(6)]
        free = [sem(f"free{b}") for b in range(6)]
        w_landed = [sem(f"w_landed{s}") for s in range(RING)]
        e_landed = [[sem(f"e_landed{u}_{s}") for s in range(SLOTS[u])] for u in range(2)]
        w_used = sem("w_used")
        x_landed = sem("x_landed")
        x2_landed = sem("x2_landed")
        xc_landed = sem("xc_landed")
        c_landed = sem("c_landed")
        keys_landed = sem("keys_landed")
        small_landed = sem("small_landed")
        rows_landed = sem("rows_landed")
        aug_landed = sem("aug_landed")
        out_landed = sem("out_landed")
        pool_chain = sem("pool_chain")
        consts_ready = sem("consts_ready")
        act_chain = sem("act_chain")
        dve_chain = sem("dve_chain")
        silu_ready = sem("silu_ready")
        silub_ready = sem("silub_ready")
        sq_ready = sem("sq_ready")
        mod_cols = sem("mod_cols")
        root_ready = sem("root_ready")
        h_ready = sem("h_ready")
        ln_ready = sem("ln_ready")
        g_ready = sem("g_ready")
        gexp_ready = sem("gexp_ready")
        rows_ready = sem("rows_ready")
        cum_ready = sem("cum_ready")
        tap_ready = sem("tap_ready")
        conv_ready = sem("conv_ready")
        conv_silu = sem("conv_silu")
        gsq_ready = sem("gsq_ready")
        qkn_ready = sem("qkn_ready")
        smax_ready = sem("smax_ready")
        pn_ready = sem("pn_ready")
        qd_ready = sem("qd_ready")
        dec_in = sem("dec_in")
        dec_ready = sem("dec_ready")
        near_ready = sem("near_ready")
        y0_ready = sem("y0_ready")
        c0_ready = sem("c0_ready")
        state_zero = sem("state_zero")
        osq_ready = sem("osq_ready")
        ob_ready = sem("ob_ready")
        sig_used = sem("sig_used")
        mix_ready = sem("mix_ready")
        mroot_ready = sem("mroot_ready")
        x1_ready = sem("x1_ready")
        h2_ready = sem("h2_ready")
        idx_ready = sem("idx_ready")
        top_ready = sem("top_ready")
        gate_ready = sem("gate_ready")
        dot_ready = sem("dot_ready")
        gelu_ready = sem("gelu_ready")
        wts_ready = sem("wts_ready")
        diag_ready = sem("diag_ready")
        e_free = sem("e_free")
        y_zero = sem("y_zero")
        y_out = sem("y_out")
        seen_pool = sem("seen_pool")
        seen_act = sem("seen_act")
        seen_pe = sem("seen_pe")
        fss_ready = sem("fss_ready")
        fin_ready = sem("fin_ready")

        def wait_full(eng, job):
            eng.wait_ge(full[jobs[job][0]], jobs[job][1])

        def wait_free(eng, job):
            eng.wait_ge(free[jobs[job][0]], jobs[job][1])

        def frees(ins, job):
            ins.then_inc(free[jobs[job][0]], 1)

        def bcast(ap, n):
            return ap.unsqueeze(2).to_broadcast([ap.shape[0], ap.shape[1], n])

        def heads(ap):
            return ap.rearrange("p (h m) -> p h m", h=GH)

        def mid(ap, n):
            return ap.unsqueeze(1).to_broadcast([ap.shape[0], n, ap.shape[1]])

        def unit(n):
            return n // HT, n % HT

        def follow(stages):
            for item in order:
                if item[0] in ("pe", "post"):
                    part = stages.get(item[:2])
                    if part:
                        part(*item[2:])
                elif item[0] in stages:
                    stages[item[0]](*item[1:])

        block = ctx.enter_context(nc.Block())

        @block.sync
        def _(sp):
            sp.dma_start(c_sb[:, :], c_cols).then_inc(c_landed, 16)
            for s in range(RING):
                sp.dma_start(ring_t[:, s, :], w_tiles[s]).then_inc(w_landed[s], 16)
            sp.dma_start(hT[:, :, :], x_cols[0]).then_inc(xc_landed, 16)
            sp.dma_start(keys[:, :, :], keys_t).then_inc(keys_landed, 16)

            def tile(r, s, back):
                sp.wait_ge(w_used, r * RING + (s + 1 - RING))
                sp.dma_start(ring_t[:, s, :],
                             w_tiles[bass.ds(r * RING + (s - back), 1)].rearrange("o p m -> (o p) m")
                             ).then_inc(w_landed[s], 16)

            with sp.Fori(1, N_W // RING) as r:
                for s in range(RING):
                    tile(r, s, 0)
            wait_full(sp, ("qy", 0, N_Q // 2 - 1))
            sp.dma_start(hT[:, :, :], x_cols[1]).then_inc(xc_landed, 16)
            with sp.Fori(N_W // RING, (N_W + N_AGAIN) // RING) as r:
                for s in range(RING):
                    tile(r, s, N_AGAIN)
            for i in range(NT):
                sp.wait_ge(fin_ready, i + 1)
                sp.dma_start(out[i], X[:, i, :]).then_inc(out_landed, 16)
            sp.wait_ge(out_landed, 16 * NT)

        @block.gpsimd
        def _(pool):
            n_chain = [0]

            def link(ins):
                n_chain[0] += 1
                ins.then_inc(pool_chain, 1)
                pool.wait_ge(pool_chain, n_chain[0])

            pool.dma_start(wsm_in, w_small).then_inc(small_landed, 16)
            pool.dma_start(bcol[:, :], ada_cols).then_inc(small_landed, 16)
            pool.dma_start(gcols[:, :], gains_cols).then_inc(small_landed, 16)
            pool.dma_start(convw[:, :, :], conv_cols).then_inc(small_landed, 16)
            link(pool.memset(small_b[:, :], 0.0))
            pool.dma_start(small_b[0:FH, 0:1], b_small[0:FH, :]).then_inc(small_landed, 16)
            pool.dma_start(small_b[64:64 + GH, 0:1], b_small[FH:FH + GH, :]).then_inc(small_landed, 16)
            pool.dma_start(small_b[64:64 + GH, 1:2], b_small[FH + GH:FH + 2 * GH, :]).then_inc(small_landed, 16)
            pool.dma_start(mods[:, :, :].rearrange("p a b -> p (a b)"),
                           ada_rows.partition_broadcast(P)).then_inc(rows_landed, 16)
            pool.dma_start(grow.rearrange("p a b -> p (a b)"), gain_rows.partition_broadcast(P)).then_inc(rows_landed, 16)
            pool.dma_start(X[:, 0:HT, :], x_rows[:, 0:HT, :]).then_inc(x_landed, 16)

            link(pool.memset(ones[:, :], 1.0))
            link(pool.memset(eps[:, :], EPS))
            link(pool.memset(ident[:, :], 0.0))
            link(pool.affine_select(out=ident[:, :], in_=ident[:, :], compare_op=ALU.not_equal, fill=1.0,
                                    base=0, pattern=[[-1, P]], channel_multiplier=1))
            link(pool.affine_select(out=causal[:, :], in_=ones[:, :], compare_op=ALU.is_ge, fill=0.0,
                                    base=0, pattern=[[1, P]], channel_multiplier=-1))
            blk = causal[:, :].rearrange("p (b i) -> p b i", i=CH)
            link(pool.affine_select(out=blk, in_=blk, compare_op=ALU.is_ge, fill=0.0,
                                    base=0, pattern=[[-CH, P // CH], [0, CH]], channel_multiplier=1))
            link(pool.affine_select(out=near[:, :], in_=ones[:, :], compare_op=ALU.is_gt, fill=0.0,
                                    base=0, pattern=[[1, P]], channel_multiplier=-1))
            blk = near[:, :].rearrange("p (b i) -> p b i", i=16)
            link(pool.affine_select(out=blk, in_=blk, compare_op=ALU.is_ge, fill=0.0,
                                    base=0, pattern=[[-16, P // 16], [0, 16]], channel_multiplier=1))
            link(pool.tensor_tensor(out=far[:, :], in0=causal[:, :], in1=near[:, :], op=ALU.subtract))
            link(pool.tensor_tensor(out=far[:, :], in0=far[:, :], in1=ident[:, :], op=ALU.subtract))
            link(pool.memset(fox_mask[:, :], 0.0))
            link(pool.affine_select(out=fox_mask[:, :], in_=fox_mask[:, :], compare_op=ALU.is_ge, fill=NEG,
                                    base=0, pattern=[[-1, P]], channel_multiplier=1))
            link(pool.iota(iota16[:, :], pattern=[[1, TOPK]], base=0, channel_multiplier=0,
                           allow_small_or_imprecise_dtypes=True))
            link(pool.memset(scan_a[:, :], 1.0))
            link(pool.memset(scan_a[64:64 + GH, :].rearrange("p (n i) -> p n i", i=CH)[:, :, 0:1], 0.0))
            link(pool.memset(R[:, :], 0.0))
            link(pool.memset(St[:, :], 0.0))
            link(pool.memset(wsm[:, :, :], 0.0))
            pool.wait_ge(small_landed, 7 * 16)
            win = wsm_in.rearrange("p (k m) -> p k m", k=KD)
            link(pool.tensor_copy(wsm[:, :, 0:8], win[:, :, 0:8]))
            link(pool.tensor_copy(wsm[:, :, 32:36], win[:, :, 8:12]))
            link(pool.tensor_copy(wsm[:, :, 64:68], win[:, :, 12:16]))
            pool.sem_inc(consts_ready, 1)

            def gather(u, p, k, slot):
                pool.indirect_dma_start(
                    out=slots[u][slot], out_offset=None, in_=experts,
                    in_offset=bass.IndirectOffsetOnAxis(ap=idx_sb[p][:, k:k + 1], axis=0),
                ).then_inc(e_landed[u][slot], 16)

            for h in range(HEADS):
                for k in range(TOPK):
                    n = h * TOPK + k
                    if k == 0:
                        pool.wait_ge(idx_ready, h + 1)
                    if n >= SLOTS[0]:
                        pool.wait_ge(e_free, n + 1 - SLOTS[0])
                    gather(0, h % 2, k, n % SLOTS[0])
            pool.wait_ge(e_free, NEXP)
            pool.wait_ge(idx_ready, HEADS + 1)
            with pool.Fori(0, HT) as i:
                with pool.Fori(0, PH // 2) as b:
                    for p in range(2):
                        head = i * PH + b * 2 + (HEADS + p)
                        pool.wait_ge(idx_ready, head + 1)
                        pool.sem_inc(seen_pool, 1)
                        for k in range(TOPK):
                            if k % 2 == 0:
                                pool.wait_ge(e_free, head * TOPK + (k + 2 - SLOTS[1]))
                                pool.sem_inc(seen_pool, 1)
                            gather(1, p, k, k % SLOTS[1])

        @block.scalar
        def _(act):
            n_chain = [0]

            def link(ins):
                n_chain[0] += 1
                ins.then_inc(act_chain, 1)
                act.wait_ge(act_chain, n_chain[0])

            act.wait_ge(c_landed, 16)
            act.activation(silu_c[:, :], c_sb[:, :], ACT.Silu).then_inc(silu_ready, 1)
            act.wait_ge(silu_ready, 1)
            act.wait_ge(consts_ready, 1)
            for k in range(KD):
                ins = act.mul(silu_cb[:, k, :], ones[:, :], silu_c[:, k:k + 1])
            ins.then_inc(silub_ready, 1)

            def squares(u):
                act.wait_ge(xc_landed, 16 * (u + 1))
                for k in range(KD):
                    act.activation(sq[:, k, :], hT[:, k, :], ACT.Square).then_inc(sq_ready, 1)

            def norm(u):
                wait_full(act, ("xsq", u))
                frees(act.activation(T1, bank(("xsq", u))[:, 0:HS], ACT.Sqrt, bias=eps[:, 0:1], scale=1.0 / D),
                      ("xsq", u))
                act.wait_ge(mod_cols, 2)
                for k in range(KD):
                    act.wait_ge(root_ready, KD * u + k + 1)
                    act.activation(hT[:, k, :], hT[:, k, :], ACT.Identity, bias=shift1[:, k:k + 1],
                                   scale=scale1[:, k:k + 1]).then_inc(h_ready, 1)

            def conv_silu_of(u, c):
                act.wait_ge(conv_ready, N_CONV * u + c + 1)
                act.activation(gT[:, c, :], gT[:, c, :], ACT.Silu).then_inc(conv_silu, 1)

            def conv(u, c):
                pad = pads[c % 2]
                ps = bank(("conv", u, c))
                wait_full(act, ("conv", u, c))
                if c >= 2:
                    act.wait_ge(conv_ready, N_CONV * u + c - 1)
                if u:
                    act.copy(pad[:, 0:CONV - 1], tails[:, c, :])
                else:
                    act.mul(pad[:, 0:CONV - 1], ones[:, 0:CONV - 1], 0.0)
                    act.copy(tails[:, c, :], ps[:, HS - CONV + 1:HS])
                act.copy(pad[:, CONV - 1:], ps[:, 0:HS])
                frees(act.mul(gT[:, c, :], ps[:, 0:HS], convw[:, c, CONV - 1:CONV]), ("conv", u, c))
                if c >= 1:
                    conv_silu_of(u, c - 1)

            def gz(u, c):
                if c == 0:
                    conv_silu_of(u, N_CONV - 1)
                wait_full(act, ("gz", u, c))
                frees(act.activation(gzT[:, c, :], bank(("gz", u, c))[:, 0:HS], ACT.Silu), ("gz", u, c))
                if c < 2:
                    unit_squares(u, c)

            def unit_squares(u, j):
                act.wait_ge(conv_silu, N_CONV * u + 2 * j + 2)
                act.activation(FT[:, j % 2, :].rearrange("p (a t) -> p a t", a=2), gT[:, 2 * j:2 * j + 2, :],
                               ACT.Square).then_inc(gsq_ready, 1)

            def unit_root(u, j):
                wait_full(act, ("unit", u, j))
                if j >= 2:
                    act.wait_ge(qkn_ready, 4 * u + j - 1)
                frees(act.activation(FT[:, 2 + j % 2, :], bank(("unit", u, j)), ACT.Sqrt, bias=eps[:, 0:1]),
                      ("unit", u, j))
                if j < 2:
                    unit_squares(u, j + 2)

            def pair_rows(which, dst, cols, scale):
                def stage(u, c):
                    wait_full(act, (which, u, c))
                    ps = bank((which, u, c))
                    span = cols(u)
                    act.mul(dst[0:FDH, 2 * c, span], ps[0:FDH, 0:HS], scale)
                    frees(act.mul(dst[0:FDH, 2 * c + 1, span], ps[FDH:P, 0:HS], scale), (which, u, c))
                return stage

            def fv(u, c):
                wait_full(act, ("fv", u, c))
                frees(act.copy(Vr[:, HT * u:HT * u + HT, c * P:(c + 1) * P],
                               bank(("fv", u, c))[:, 0:HS].rearrange("p (i m) -> p i m", i=HT)), ("fv", u, c))

            def small(u):
                wait_free(act, ("small", u))
                link(act.activation(T1[0:68, :], Z[0:68, :], ACT.Abs))
                link(act.activation(T1[0:68, :], T1[0:68, :], ACT.Exp, scale=-1.0))
                link(act.activation(T1[0:68, :], T1[0:68, :], ACT.Ln, bias=ones[0:68, 0:1]))
                link(act.activation(T2[32:32 + GH, :], Z[32:32 + GH, :], ACT.Exp, scale=-1.0))
                if not u:
                    link(act.activation(small_b[64:64 + GH, 2:3], small_b[64:64 + GH, 1:2], ACT.Exp))
                act.sem_inc(ln_ready, 1)
                act.wait_ge(cum_ready, 3 * (u + 1))
                for h in range(FH):
                    act.dma_start(qaug[64:65, h, :], CF[h:h + 1, :]).then_inc(aug_landed, 16)
                    act.dma_start(kaug[65:66, h, HS * u:HS * (u + 1)], CF[32 + h:33 + h, :]).then_inc(aug_landed, 16)
                act.wait_ge(g_ready, 2 * (u + 1))
                act.activation(T4[32:32 + GH, :], T3[64:64 + GH, :], ACT.Exp).then_inc(gexp_ready, 1)
                act.copy(R[0:GH, :], T3[64:64 + GH, :]).then_inc(rows_ready, 1)
                act.activation(R[96:96 + GH, :], T4[64:64 + GH, :], ACT.Exp, scale=-1.0).then_inc(rows_ready, 1)

            def cols(u):
                wait_full(act, ("cols", u))
                frees(act.copy(rcols[:, :, :], bank(("cols", u))[:, 0:HT * P].rearrange("p (i m) -> p i m", i=HT)),
                      ("cols", u))

            def keep_head(u, h):
                wait_full(act, ("O", u, h))
                frees(act.copy(OT[64 * (h % 2):64 * (h % 2) + 64, h // 2, :], bank(("O", u, h))[0:FDH, 0:HS]),
                      ("O", u, h))

            def att(u, n):
                if n < FH * HT:
                    act.wait_ge(smax_ready, FH * HT * u + n + 1)
                    if n >= 2:
                        wait_full(act, ("PT", u, n - 2))
                    w = (HT * u + unit(n)[1] + 1) * P
                    frees(act.activation(FT[:, n % 2, 0:w], bank(("S", u, n))[:, 0:w], ACT.Exp,
                                         bias=stat[:, n % 2:n % 2 + 1], accum_out=stat[:, 2 + n % 2:3 + n % 2]),
                          ("S", u, n))
                if 1 <= n <= FH * HT:
                    w = (HT * u + unit(n - 1)[1] + 1) * P
                    wait_full(act, ("PT", u, n - 1))
                    frees(act.copy(FT[:, 2 + (n - 1) % 2, 0:w], bank(("PT", u, n - 1))[:, 0:w]), ("PT", u, n - 1))
                if n >= 3 and n % HT == 1:
                    keep_head(u, (n - 3) // HT)

            def spread(u):
                for j in range(2):
                    wait_full(act, ("bg", u, j))
                    act.copy(space[u][j], bank(("bg", u, j)))
                    frees(act.activation(space[u][2 + j], bank(("bg", u, j)), ACT.Exp), ("bg", u, j))

            def kv_(g):
                t = dn[g // HT]["A"]
                act.wait_ge(dec_in, g + 1)
                act.activation(t, t, ACT.Exp).then_inc(dec_ready, 1)

            def evac(*pairs):
                def stage(g):
                    for job, name in pairs:
                        wait_full(act, (job, g))
                        frees(act.copy(dn[g // HT][name], bank((job, g))), (job, g))
                return stage

            def os_(n):
                wait_full(act, ("o", n))
                c0 = (n % (2 * HT)) * CH
                frees(act.copy(OBT[:, :, c0:c0 + CH],
                               bank(("o", n))[:, 0:GH * CH].rearrange("p (h t) -> p h t", h=GH)), ("o", n))
                if n % (2 * HT) == 2 * HT - 1:
                    wait_free(act, ("o", n))
                    for j in range(2):
                        act.activation(dn[g_of(n)][("rv", "rw")[j]].rearrange("p (a t) -> p a t", a=2),
                                       OBT[:, 2 * j:2 * j + 2, :], ACT.Square).then_inc(osq_ready, 1)

            def g_of(n):
                return n // (2 * HT)

            def onorm(u):
                for j in range(2):
                    wait_full(act, ("oss", u, j))
                    frees(act.activation(dn[u][("u", "w")[j]], bank(("oss", u, j)), ACT.Sqrt, bias=eps[:, 0:1],
                                         scale=1.0 / P), ("oss", u, j))

            def gated(which, n):
                def stage(u, c):
                    if c >= 1 and n == 0:
                        act.wait_ge(sig_used, KD * u + c)
                    wait_full(act, (which, u, c))
                    frees(act.activation(FT[:, 0, n * HS:(n + 1) * HS], bank((which, u, c))[:, 0:HS], ACT.Sigmoid,
                                         bias=gcols[:, KD * (n + 1) + c:KD * (n + 1) + c + 1]), (which, u, c))
                return stage

            def x1(u, i):
                t = HT * u + i
                if i == 0 and u:
                    act.wait_ge(ob_ready, GH * (u + 1))
                    act.dma_start(X[:, HT:NT, :], x_rows[:, HT:NT, :]).then_inc(x2_landed, 16)
                for half in range(2):
                    wait_full(act, ("mix", t, half))
                    link(act.activation(FT[:, 0, :], bank(("mix", t, half)), ACT.Square,
                                        accum_out=stat[:, 8 + 2 * t + half:9 + 2 * t + half]))
                link(act.activation(stat[:, 16 + t:17 + t], stat[:, 8 + 2 * t:9 + 2 * t], ACT.Identity,
                                    bias=stat[:, 9 + 2 * t:10 + 2 * t]))
                act.activation(stat[:, 20 + t:21 + t], stat[:, 16 + t:17 + t], ACT.Sqrt, bias=eps[:, 0:1],
                               scale=1.0 / D).then_inc(mroot_ready, 1)
                act.wait_ge(x1_ready, t + 1)
                link(act.activation(flat[:, 0:D], X[:, t, :], ACT.Square, accum_out=stat[:, 24 + t:25 + t]))
                act.activation(stat[:, 28 + t:29 + t], stat[:, 24 + t:25 + t], ACT.Sqrt, bias=eps[:, 0:1],
                               scale=1.0 / D).then_inc(mroot_ready, 1)

            def h2_turned(u, i):
                t = HT * u + i
                for half in range(2):
                    wait_full(act, ("h2T", t, half))
                    frees(act.copy(hT[:, 4 * half:4 * half + 4, i * P:(i + 1) * P],
                                   bank(("h2T", t, half)).rearrange("p (k t) -> p k t", k=4)), ("h2T", t, half))

            def qy(u, j):
                if j == 0:
                    pass
                wait_full(act, ("qy", u, j))
                frees(act.copy(FT[:, 2 + j % 2, :], bank(("qy", u, j))), ("qy", u, j))

            def sc(u, j):
                wait_full(act, ("sc", u, j))
                dst = scores[u].rearrange("p (i h) k -> p i h k", i=HT)[:, :, j, :]
                frees(act.copy(dst, bank(("sc", u, j)).rearrange("p (i k) -> p i k", i=HT)), ("sc", u, j))

            def gate_exp(n, p):
                act.wait_ge(top_ready, n + 1)
                act.activation(gate[p][:, 0:TOPK], tops[p][:, :], ACT.Exp, bias=gate[p][:, TOPK:TOPK + 1],
                               accum_out=gate[p][:, TOPK + 1:TOPK + 2]).then_inc(gate_ready, 1)

            def gelu(head, p, k):
                act.wait_ge(dot_ready, head * TOPK + (k + 1))
                act.activation(acts[p][:, k:k + 1], dots[p][:, k:k + 1], ACT.Gelu).then_inc(gelu_ready, 1)

            def clear():
                nothing = ones[:, 0:1].to_broadcast([P, S])
                act.mul(PS[:, BANK_Y, :], nothing, 0.0)
                act.mul(PS[:, BANK_Y + 1, :], nothing, 0.0).then_inc(y_zero, 1)

            def keep(t, static):
                act.wait_ge(e_free, (t + 1) * (PH * TOPK))
                if not static:
                    act.sem_inc(seen_act, 1)
                row = H2[:, t, :] if static else H2[:, bass.ds(t, 1), :].rearrange("p a b -> p (a b)")
                act.copy(row[:, 0:S], PS[:, BANK_Y, :])
                act.copy(row[:, S:D], PS[:, BANK_Y + 1, :]).then_inc(y_out, 1)
                act.wait_ge(y_out, t + 1)
                if not static:
                    act.sem_inc(seen_act, 1)

            def sums(t):
                if t:
                    keep(t - 1, True)
                clear()

            follow({
                ("post", "norm"): norm, ("pe", "norm"): squares, ("post", "conv"): conv, ("post", "gz"): gz,
                ("post", "unit"): unit_root, ("post", "fq"): pair_rows("fq", qaug, lambda u: slice(0, HS), FDH ** -0.5),
                ("post", "fk"): pair_rows("fk", kaug, lambda u: slice(HS * u, HS * (u + 1)), 1.0),
                ("post", "fv"): fv, ("post", "small"): small, ("post", "cols"): cols, ("post", "att"): att,
                ("post", "spread"): spread, ("post", "kv"): kv_, ("post", "turn"): evac(("D", "DD"), ("E", "E")),
                ("post", "sq2"): evac(("D2", "A"), ("N2", "B")), ("post", "sq4"): evac(("D4", "DD"), ("N4", "N")),
                ("post", "sq8"): evac(("D8", "A")), ("post", "wmq"): evac(("W", "B"), ("M", "DD")),
                ("post", "m2"): evac(("M2", "A")), ("post", "tt"): evac(("TT", "ET")),
                ("post", "uw"): evac(("u", "u"), ("wT", "w")), ("post", "os"): os_, ("post", "onorm"): onorm,
                ("post", "ga"): gated("ga", 0), ("post", "gb"): gated("gb", 1), ("pe", "x1"): x1,
                ("post", "x1"): h2_turned, ("post", "qy"): qy, ("post", "sc"): sc,
                "sums": sums, "choose_all": lambda h: gate_exp(h, h % 2),
                "choose": lambda h, part: gate_exp(h, h % 2) if part == 3 else None,
                "expert": lambda h, k: gelu(h, h % 2, k),
            })
            keep(HT - 1, True)
            clear()
            gate_exp(HEADS, 0)
            with act.Fori(HT, NT) as t:
                with act.Fori(0, PH // 2) as b:
                    for p in range(2):
                        head = t * PH + b * 2 + p
                        for k in range(TOPK):
                            gelu(head, p, k)
                            if k == 11:
                                gate_exp(head + 1, 1 - p)
                keep(t, False)
                clear()
            for t in range(NT):
                link(act.activation(flat[:, 0:D], H2[:, t, :], ACT.Square, accum_out=stat[:, 32 + t:33 + t]))
            act.activation(stat[:, 36:36 + NT], stat[:, 32:32 + NT], ACT.Sqrt, bias=eps[:, 0:1],
                           scale=1.0 / D).then_inc(fss_ready, 1)

        @block.vector
        def _(dve):
            n_chain = [0]

            def link(ins):
                n_chain[0] += 1
                ins.then_inc(dve_chain, 1)
                dve.wait_ge(dve_chain, n_chain[0])

            dve.wait_ge(consts_ready, 1)

            def ada_col():
                job = ("ada_col",)
                wait_full(dve, job)
                dve.wait_ge(small_landed, 7 * 16)
                dve.tensor_tensor(out=shift1[:, :], in0=bank(job)[:, 0:KD], in1=bcol[:, 0:KD],
                                  op=ALU.add).then_inc(mod_cols, 1)
                frees(dve.tensor_tensor(out=scale1[:, :], in0=bank(job)[:, KD:2 * KD], in1=bcol[:, KD:2 * KD],
                                        op=ALU.add), job)
                wait_free(dve, job)
                dve.scalar_tensor_tensor(out=scale1[:, :], in0=scale1[:, :], scalar=1.0, in1=gcols[:, 0:KD],
                                         op0=ALU.add, op1=ALU.mult).then_inc(mod_cols, 1)

            def row(c):
                if c == 0:
                    dve.wait_ge(rows_landed, 32)
                wait_full(dve, ("row", c))
                m = mods[:, c // 2, (c % 2) * S:(c % 2 + 1) * S]
                frees(dve.tensor_tensor(out=m, in0=bank(("row", c)), in1=m, op=ALU.add), ("row", c))
                if c == 2 * NT - 1:
                    wait_free(dve, ("row", c))
                    for n in (0, 2, 3):
                        link(dve.scalar_tensor_tensor(out=mods[:, n, :], in0=mods[:, n, :],
                                                      scalar=(1.0 if n == 2 else 0.0), in1=grow[:, (n + 1) // 2, :],
                                                      op0=ALU.add, op1=ALU.mult))

            def norm(u):
                wait_free(dve, ("xsq", u))
                link(dve.reciprocal(T1, T1))
                for k in range(KD):
                    dve.tensor_tensor(out=hT[:, k, :], in0=hT[:, k, :], in1=T1, op=ALU.mult).then_inc(root_ready, 1)

            def small(u):
                wait_full(dve, ("small", u))
                frees(dve.tensor_scalar(Z[0:68, :], bank(("small", u))[0:68, 0:HS], small_b[0:68, 0:1], None,
                                        ALU.add), ("small", u))
                dve.wait_ge(ln_ready, u + 1)
                link(dve.tensor_scalar(T2[0:FH, :], Z[0:FH, :], 0.0, None, ALU.min))
                link(dve.tensor_tensor(out=T2[0:FH, :], in0=T2[0:FH, :], in1=T1[0:FH, :], op=ALU.subtract))
                dve.tensor_tensor_scan(CF[0:FH, :], scan_a[0:FH, :], T2[0:FH, :], carry[:, 0:1] if u else 0.0,
                                       ALU.mult, ALU.add).then_inc(cum_ready, 1)
                dve.wait_ge(cum_ready, 3 * u + 1)
                if not u:
                    link(dve.tensor_copy(carry[:, :], CF[0:FH, HS - 1:HS]))
                dve.tensor_scalar(CF[32:32 + FH, :], CF[0:FH, :], -1.0, None, ALU.mult).then_inc(cum_ready, 1)
                dve.memset(qaug[64:66, :, :], 1.0)
                dve.memset(kaug[64:66, :, HS * u:HS * (u + 1)], 1.0).then_inc(cum_ready, 1)
                link(dve.tensor_scalar(T2[32:32 + GH, :], T2[32:32 + GH, :], 1.0, None, ALU.add))
                link(dve.reciprocal(R[32:32 + GH, :], T2[32:32 + GH, :]))
                a0, a1 = 64, 64 + GH
                link(dve.scalar_tensor_tensor(out=T2[a0:a1, :], in0=Z[a0:a1, :], scalar=0.0, in1=T1[a0:a1, :],
                                              op0=ALU.max, op1=ALU.add))
                link(dve.tensor_scalar(T2[a0:a1, :], T2[a0:a1, :], small_b[a0:a1, 2:3], -1.0, ALU.mult, ALU.mult))
                dve.tensor_tensor_scan(T3[a0:a1, :], scan_a[a0:a1, :], T2[a0:a1, :], 0.0, ALU.mult,
                                       ALU.add).then_inc(g_ready, 1)
                dve.wait_ge(g_ready, 2 * u + 1)
                g3 = T3[a0:a1, :].rearrange("p (n i) -> p n i", i=CH)
                dve.tensor_tensor(out=T4[a0:a1, :].rearrange("p (n i) -> p n i", i=CH), in0=g3,
                                  in1=g3[:, :, CH - 1:CH].to_broadcast([GH, HS // CH, CH]),
                                  op=ALU.subtract).then_inc(g_ready, 1)
                dve.wait_ge(gexp_ready, u + 1)
                dve.tensor_tensor(out=R[64:64 + GH, :], in0=R[32:32 + GH, :], in1=T4[32:32 + GH, :],
                                  op=ALU.mult).then_inc(rows_ready, 1)

            def conv(u, c):
                wait_free(dve, ("conv", u, c))
                for d in range(1, CONV):
                    ins = dve.scalar_tensor_tensor(
                        out=gT[:, c, :], in0=pads[c % 2][:, CONV - 1 - d:CONV - 1 - d + HS],
                        scalar=convw[:, c, CONV - 1 - d:CONV - d], in1=gT[:, c, :], op0=ALU.mult, op1=ALU.add)
                    if d < CONV - 1:
                        link(ins)
                ins.then_inc(conv_ready, 1)

            def unit_norm(u, j):
                wait_free(dve, ("unit", u, j))
                r = FT[:, 2 + j % 2, :]
                link(dve.reciprocal(r, r))
                dve.scalar_tensor_tensor(out=gT[:, 2 * j:2 * j + 2, :], in0=gT[:, 2 * j:2 * j + 2, :],
                                         scalar=(P ** -0.5 if j < 2 else 1.0), in1=r.rearrange("p (a t) -> p a t", a=2),
                                         op0=ALU.mult, op1=ALU.mult).then_inc(qkn_ready, 1)

            def att(u, n):
                if n >= FH * HT:
                    return
                w = (HT * u + unit(n)[1] + 1) * P
                wait_full(dve, ("S", u, n))
                if n >= 2:
                    wait_free(dve, ("S", u, n - 2))
                dve.tensor_reduce(stat[:, n % 2:n % 2 + 1], bank(("S", u, n))[:, 0:w], AX.X, ALU.max,
                                  negate=True).then_inc(smax_ready, 1)
                wait_free(dve, ("S", u, n))
                done = FH * HT * u + n
                if done:
                    dve.wait_ge(pn_ready, done)
                link(dve.reciprocal(stat[:, 4:5], stat[:, 2 + n % 2:3 + n % 2]))
                dve.tensor_scalar(FT[:, n % 2, 0:w], FT[:, n % 2, 0:w], stat[:, 4:5], None,
                                  ALU.mult).then_inc(pn_ready, 1)

            def spread(u):
                dve.wait_ge(qkn_ready, 4 * (u + 1))
                for j in range(2):
                    wait_full(dve, ("bb", u, j))
                    frees(dve.tensor_tensor(out=space[u][4 + j], in0=bank(("bb", u, j)),
                                            in1=kT[:, 2 * j:2 * j + 2, :].rearrange("p a t -> p (a t)"), op=ALU.mult),
                          ("bb", u, j))
                for j in range(2):
                    wait_free(dve, ("bg", u, j))
                    dve.tensor_tensor(out=space[u][6 + j], in0=space[u][2 + j],
                                      in1=qT[:, 2 * j:2 * j + 2, :].rearrange("p a t -> p (a t)"),
                                      op=ALU.mult).then_inc(qd_ready, 1)
                wait_free(dve, ("cols", u))

            def kv_(g):
                u, i = divmod(g, HT)
                t = dn[u]
                tok = slice(i * P, (i + 1) * P)
                wait_full(dve, ("kt", g))
                dve.tensor_tensor(out=heads(t["rw"]), in0=heads(bank(("kt", g))), in1=bcast(rcols[:, i, 64:64 + GH], P),
                                  op=ALU.mult)
                frees(dve.tensor_tensor(out=heads(t["kd"]), in0=heads(bank(("kt", g))),
                                        in1=bcast(rcols[:, i, 96:96 + GH], P), op=ALU.mult), ("kt", g))
                wait_full(dve, ("vt", g))
                frees(dve.tensor_tensor(out=heads(t["rv"]), in0=heads(bank(("vt", g))),
                                        in1=bcast(rcols[:, i, 32:32 + GH], P), op=ALU.mult), ("vt", g))
                for h in range(GH):
                    ins = dve.tensor_scalar(t["A"][:, h * P:(h + 1) * P], Gb[u][h][:, tok], rcols[:, i, h:h + 1], 0.0,
                                            ALU.subtract, ALU.min)
                ins.then_inc(dec_in, 1)
                dve.wait_ge(dec_ready, g + 1)
                link(dve.tensor_tensor(out=heads(t["A"]), in0=heads(t["A"]), in1=mid(causal[:, :], GH), op=ALU.mult))

            def kk_(g):
                t = dn[g // HT]
                wait_full(dve, ("kk", g))
                frees(dve.tensor_tensor(out=t["B"], in0=bank(("kk", g)), in1=t["A"], op=ALU.mult), ("kk", g))
                wait_full(dve, ("qk", g))
                frees(dve.tensor_tensor(out=t["a"], in0=bank(("qk", g)), in1=t["A"], op=ALU.mult), ("qk", g))
                wait_free(dve, ("kk", g))
                dve.tensor_tensor(out=heads(t["N"]), in0=heads(t["B"]), in1=mid(near[:, :], GH),
                                  op=ALU.mult).then_inc(near_ready, 1)
                dve.tensor_tensor(out=heads(t["ET"]), in0=heads(t["B"]), in1=mid(far[:, :], GH),
                                  op=ALU.mult).then_inc(near_ready, 1)
                dve.wait_ge(near_ready, 2 * g + 2)
                dve.scalar_tensor_tensor(out=heads(t["Y"]), in0=heads(t["N"]), scalar=-1.0, in1=mid(ident[:, :], GH),
                                         op0=ALU.mult, op1=ALU.add).then_inc(y0_ready, 1)
                dve.wait_ge(y0_ready, g + 1)

            def add_to(job, name):
                def stage(g):
                    t = dn[g // HT][name]
                    wait_full(dve, (job, g))
                    frees(dve.tensor_tensor(out=t, in0=bank((job, g)), in1=t, op=ALU.add), (job, g))
                    wait_free(dve, (job, g))
                return stage

            def wmq(g):
                t = dn[g // HT]
                wait_full(dve, ("Q", g))
                frees(dve.tensor_copy(t["N"], bank(("Q", g))), ("Q", g))
                wait_free(dve, ("Q", g))
                dve.scalar_tensor_tensor(out=heads(t["C"]), in0=heads(t["N"]), scalar=-1.0, in1=mid(ident[:, :], GH),
                                         op0=ALU.mult, op1=ALU.add).then_inc(c0_ready, 1)
                dve.wait_ge(c0_ready, g + 1)

            def ws(n):
                g = n // 2
                t = dn[g // HT]
                rows = slice(CH * (n % 2), CH * (n % 2) + CH)
                wait_full(dve, ("ws", n))
                wait_free(dve, ("u", g))
                frees(dve.tensor_tensor(out=t["vn"][rows, :], in0=t["u"][rows, :], in1=bank(("ws", n))[rows, :],
                                        op=ALU.subtract), ("ws", n))

            def os_(n):
                u = n // (2 * HT)
                wait_full(dve, ("su", n))
                last = (n % (2 * HT) + 1) * CH - 1
                for h in range(GH):
                    hs = slice(h * P, (h + 1) * P)
                    ins = dve.scalar_tensor_tensor(out=St[:, hs], in0=St[:, hs], scalar=expG[u][h][:, last:last + 1],
                                                   in1=bank(("su", n))[:, hs], op0=ALU.mult, op1=ALU.add)
                frees(ins, ("su", n))

            def onorm(u):
                for j in range(2):
                    wait_free(dve, ("oss", u, j))
                    r = dn[u][("u", "w")[j]]
                    o = OBT[:, 2 * j:2 * j + 2, :].rearrange("p a t -> p (a t)")
                    link(dve.reciprocal(r, r))
                    link(dve.scalar_tensor_tensor(out=o, in0=o, scalar=gcols[:, 3 * KD:3 * KD + 1], in1=r,
                                                  op0=ALU.mult, op1=ALU.mult))
                    dve.tensor_tensor(out=o, in0=o, in1=gzT[:, 2 * j:2 * j + 2, :].rearrange("p a t -> p (a t)"),
                                      op=ALU.mult).then_inc(ob_ready, 2)

            def yab(u, c):
                wait_full(dve, ("yab", u, c))
                wait_free(dve, ("ga", u, c))
                wait_free(dve, ("gb", u, c))
                if c or u:
                    dve.wait_ge(mix_ready, KD * u + c)
                frees(dve.tensor_tensor(out=FT[:, 1, :], in0=bank(("yab", u, c)), in1=FT[:, 0, :], op=ALU.mult),
                      ("yab", u, c))
                wait_free(dve, ("yab", u, c))
                dve.sem_inc(sig_used, 1)
                dve.tensor_tensor(out=mixT[:, c, :], in0=FT[:, 1, 0:HS], in1=FT[:, 1, HS:S],
                                  op=ALU.add).then_inc(mix_ready, 1)

            def x1(u, i):
                t = HT * u + i
                dve.wait_ge(mix_ready, KD * (u + 1))
                dve.wait_ge(mroot_ready, 2 * t + 1)
                link(dve.reciprocal(stat[:, 40:41], stat[:, 20 + t:21 + t]))
                for half in range(2):
                    hs = slice(half * S, (half + 1) * S)
                    frees(dve.scalar_tensor_tensor(out=H2[:, t, hs], in0=bank(("mix", t, half)), scalar=stat[:, 40:41],
                                                   in1=mods[:, 0, hs], op0=ALU.mult, op1=ALU.mult), ("mix", t, half))
                wait_free(dve, ("mix", t, 0))
                wait_free(dve, ("mix", t, 1))
                dve.wait_ge(x2_landed if u else x_landed, 16)
                dve.tensor_tensor(out=X[:, t, :], in0=X[:, t, :], in1=H2[:, t, :], op=ALU.add).then_inc(x1_ready, 1)
                dve.wait_ge(mroot_ready, 2 * t + 2)
                link(dve.reciprocal(stat[:, 41:42], stat[:, 28 + t:29 + t]))
                link(dve.scalar_tensor_tensor(out=H2[:, t, :], in0=X[:, t, :], scalar=stat[:, 41:42], in1=mods[:, 2, :],
                                              op0=ALU.mult, op1=ALU.mult))
                dve.tensor_tensor(out=H2[:, t, :], in0=H2[:, t, :], in1=mods[:, 1, :],
                                  op=ALU.add).then_inc(h2_ready, 1)
                dve.wait_ge(h2_ready, t + 1)

            def chain(ins):
                dve.drain()

            w1, w2 = work[:, 0, :], work[:, 1, :]
            cells = [w.rearrange("p (a b) -> p a b", a=TOPK) for w in (w1, w2)]

            def choose(u, n, p, part):
                if part == 0:
                    src = scores[u][:, n, :] if isinstance(n, int) else scores[u][:, bass.ds(n, 1), :].rearrange(
                        "p a k -> p (a k)")
                    chain(dve.tensor_copy(w1, src))
                if part < 2:
                    v, ix = kv[:, part * TOPK:(part + 1) * TOPK], ki[:, part * TOPK:(part + 1) * TOPK]
                    a, z = w1[:, part * NK:(part + 1) * NK], w2[:, part * NK:(part + 1) * NK]
                    chain(dve.max(v[:, 0:8], a))
                    dve.max_index(ix[:, 0:8], v[:, 0:8], a)
                    chain(dve.match_replace(z, v[:, 0:8], a, LOWEST))
                    chain(dve.max(v[:, 8:16], z))
                    chain(dve.max_index(ix[:, 8:16], v[:, 8:16], z))
                elif part == 2:
                    chain(dve.tensor_tensor(out=cells[0], in0=bcast(kv[:, 0:TOPK], TOPK),
                                            in1=mid(kv[:, TOPK:2 * TOPK], TOPK), op=ALU.add))
                    chain(dve.max(tops[p][:, 0:8], w1))
                    dve.max_index(pos[:, 0:8], tops[p][:, 0:8], w1)
                    chain(dve.match_replace(w2, tops[p][:, 0:8], w1, LOWEST))
                    chain(dve.max(tops[p][:, 8:16], w2))
                    dve.max_index(pos[:, 8:16], tops[p][:, 8:16], w2)
                    dve.tensor_scalar(gate[p][:, TOPK:TOPK + 1], tops[p][:, 0:1], -1.0, None,
                                      ALU.mult).then_inc(top_ready, 1)
                    chain(dve.tensor_copy(kf[:, :], ki[:, :]))
                else:
                    dve.tensor_scalar(pos[:, 16:32], pos[:, 0:16], 4, None, ALU.logical_shift_right)
                    chain(dve.tensor_scalar(pos[:, 32:48], pos[:, 0:16], 15, None, ALU.bitwise_and))
                    chain(dve.tensor_copy(posf[:, 0:32], pos[:, 16:48]))
                    for s in range(2):
                        chain(dve.tensor_tensor(out=cells[0], in0=bcast(posf[:, s * TOPK:(s + 1) * TOPK], TOPK),
                                                in1=mid(iota16[:, :], TOPK), op=ALU.is_equal))
                        chain(dve.tensor_tensor(out=cells[1], in0=cells[0], in1=mid(kf[:, s * TOPK:(s + 1) * TOPK], TOPK),
                                                op=ALU.mult))
                        chain(dve.tensor_reduce(posf[:, (2 + s) * TOPK:(3 + s) * TOPK], cells[1], AX.X, ALU.add))
                    dve.scalar_tensor_tensor(out=idx_sb[p][:, :], in0=posf[:, 32:48], scalar=float(NK),
                                             in1=posf[:, 48:64], op0=ALU.mult, op1=ALU.add).then_inc(idx_ready, 1)
                    dve.drain()

            def gates(head, p):
                dve.wait_ge(gate_ready, head + 1)
                chain(dve.reciprocal(gate[p][:, TOPK + 2:TOPK + 3], gate[p][:, TOPK + 1:TOPK + 2]))
                dve.tensor_scalar(wts[p][:, :], gate[p][:, 0:TOPK], gate[p][:, TOPK + 2:TOPK + 3], None,
                                  ALU.mult).then_inc(wts_ready, 1)
                dve.drain()

            def weigh(head, p, k):
                dve.wait_ge(gelu_ready, head * TOPK + (k + 1))
                if not isinstance(head, int) or head * TOPK + k >= NDG:
                    dve.wait_ge(e_free, head * TOPK + (k + 1 - NDG))
                dve.tensor_scalar(diag[:, k % NDG, :], ident[:, :], acts[p][:, k:k + 1],
                                  wts[p][:, k:k + 1], ALU.mult, ALU.mult).then_inc(diag_ready, 1)

            def dot(p, k, rows, h2):
                dve.scalar_tensor_tensor(out=rows[:, 0:D], in0=rows[:, 0:D], scalar=1.0, in1=h2, op0=ALU.mult,
                                         op1=ALU.mult, accum_out=dots[p][:, k:k + 1]).then_inc(dot_ready, 1)

            def expert(h, k):
                n = h * TOPK + k
                slot = n % SLOTS[0]
                dve.wait_ge(e_landed[0][slot], 16 * (n // SLOTS[0] + 1))
                dot(h % 2, k, slots[0][slot], H2[:, h // PH, :])
                if k >= LAG[0]:
                    weigh(h, h % 2, k - LAG[0])
                if k == TOPK - 1:
                    for kk in range(TOPK - LAG[0], TOPK):
                        weigh(h, h % 2, kk)

            def choose_all(h):
                for j in range(N_Q // 2):
                    wait_free(dve, ("sc", h // HEADS, j))
                for part in range(4):
                    choose(h // HEADS, h % HEADS, h % 2, part)

            follow({
                ("post", "ada_col"): ada_col, ("post", "row"): row, ("post", "norm"): norm, ("post", "small"): small,
                ("post", "conv"): conv, ("post", "unit"): unit_norm, ("post", "att"): att, ("post", "spread"): spread,
                ("post", "kv"): kv_, ("post", "kk"): kk_, ("post", "sq4"): add_to("Y1", "Y"),
                ("post", "sq8"): add_to("Y2", "Y"), ("post", "inv"): add_to("Y3", "Y"), ("post", "wmq"): wmq,
                ("post", "c"): add_to("C", "C"), ("post", "ws"): ws, ("post", "os"): os_, ("post", "onorm"): onorm,
                ("post", "yab"): yab, ("pe", "x1"): x1,
                "choose_all": choose_all, "choose": lambda h, part: choose(0, h, h % 2, part),
                "gates": lambda h: gates(h, h % 2), "expert": expert,
            })
            choose_all(HEADS)
            with dve.Fori(HT, NT) as t:
                with dve.Fori(0, PH // 2) as b:
                    for p in range(2):
                        head = t * PH + b * 2 + p
                        ahead = t * PH + b * 2 + (p + 1 - HEADS)
                        gates(head, p)
                        h2 = H2[:, bass.ds(t, 1), :].rearrange("p a b -> p (a b)")
                        for k in range(TOPK):
                            slot = k % SLOTS[1]
                            dve.wait_ge(e_landed[1][slot],
                                        head * (16 * TOPK // SLOTS[1]) + (k // SLOTS[1] + 1) * 16
                                        - HEADS * (16 * TOPK // SLOTS[1]))
                            dot(p, k, slots[1][slot], h2)
                            if k >= LAG[1]:
                                weigh(head, p, k - LAG[1])
                            if k % 3 == 0 and k // 3 < 4:
                                choose(1, ahead % HEADS if p else ahead, 1 - p, k // 3)
                        for k in range(TOPK - LAG[1], TOPK):
                            weigh(head, p, k)
            dve.wait_ge(fss_ready, 1)
            link(dve.reciprocal(stat[:, 44:44 + NT], stat[:, 36:36 + NT]))
            for t in range(NT):
                link(dve.scalar_tensor_tensor(out=H2[:, t, :], in0=H2[:, t, :], scalar=stat[:, 44 + t:45 + t],
                                              in1=mods[:, 3, :], op0=ALU.mult, op1=ALU.mult))
                dve.tensor_tensor(out=X[:, t, :], in0=X[:, t, :], in1=H2[:, t, :],
                                  op=ALU.add).then_inc(fin_ready, 1)

        @block.tensor
        def _(pe):
            n_w = [0]

            def weights(n, u=0):
                use = n + N_AGAIN * u
                assert use == n_w[0], (n, u, n_w[0])
                n_w[0] += 1
                pe.wait_ge(w_landed[use % RING], 16 * (use // RING + 1))
                return ring[:, use % RING, :, :]

            def past(ins, first):
                if first and n_w[0] > 1:
                    ins.then_inc(w_used, 1)

            def begin(job):
                b, n = jobs[job]
                if n > 1:
                    pe.wait_ge(free[b], n - 1)
                return PS[:, b, :]

            def done(ins, job):
                ins.then_inc(full[jobs[job][0]], 1)

            def ada_col():
                pe.wait_ge(silu_ready, 1)
                ps = begin(("ada_col",))
                for c in range(N_COL):
                    w = weights(W_COL + c)
                    for k in range(KD):
                        ins = pe.matmul(ps[:, c:c + 1], w[:, k, :], silu_c[:, k:k + 1], start=(k == 0),
                                        stop=(k == KD - 1))
                        past(ins, k == 0)
                done(ins, ("ada_col",))

            def row(c):
                if c == 0:
                    pe.wait_ge(silub_ready, 1)
                ps = begin(("row", c))
                for j in range(4):
                    w = weights(W_ROW + 4 * c + j)
                    for k in range(KD):
                        ins = pe.matmul(ps[:, j * P:(j + 1) * P], silu_cb[:, k, :], w[:, k, :],
                                        start=(k == 0), stop=(k == KD - 1))
                        past(ins, k == 0)
                done(ins, ("row", c))

            def norm(u):
                pe.wait_ge(consts_ready, 1)
                ps = begin(("xsq", u))
                for k in range(KD):
                    pe.wait_ge(sq_ready, KD * u + k + 1)
                    ins = pe.matmul(ps[:, 0:HS], ones[:, :], sq[:, k, :], start=(k == 0), stop=(k == KD - 1))
                done(ins, ("xsq", u))

            def small(u):
                ps = begin(("small", u))
                for k in range(KD):
                    pe.wait_ge(h_ready, KD * u + k + 1)
                    ins = pe.matmul(ps[0:68, 0:HS], wsm[:, k, :], hT[:, k, :], start=(k == 0), stop=(k == KD - 1))
                done(ins, ("small", u))

            def project(w, dst, src, ks=range(KD), first=True):
                for m, k in enumerate(ks):
                    ins = pe.matmul(dst, w[:, k, :], src[:, m, :], start=(m == 0), stop=(m == len(ks) - 1))
                    past(ins, first and m == 0)
                return ins

            def projection(name, base):
                def stage(u, c):
                    w = weights(base(c), u)
                    ps = begin((name, u, c))
                    done(project(w, ps[:, 0:HS], hT), (name, u, c))
                return stage

            def fv(u, c):
                w = weights(W_F + 8 + c, u)
                ps = begin(("fv", u, c))
                for i in range(HT):
                    for k in range(KD):
                        ins = pe.matmul(ps[:, i * P:(i + 1) * P], hT[:, k, i * P:(i + 1) * P], w[:, k, :],
                                        start=(k == 0), stop=(k == KD - 1))
                        past(ins, i == 0 and k == 0)
                done(ins, ("fv", u, c))

            def unit_norm(u, j):
                ps = begin(("unit", u, j))
                pe.wait_ge(gsq_ready, 4 * u + j + 1)
                done(pe.matmul(ps, ones[:, :], FT[:, j % 2, :], start=True, stop=True), ("unit", u, j))

            def cols(u):
                pe.wait_ge(rows_ready, 3 * (u + 1))
                ps = begin(("cols", u))
                for i in range(HT):
                    ins = pe.transpose(ps[:, i * P:(i + 1) * P], R[:, i * P:(i + 1) * P], ident[:, :])
                done(ins, ("cols", u))

            def att(u, n):
                if n == 0:
                    pe.wait_ge(aug_landed, 2 * FH * 16 * (u + 1))
                    for c in range(4):
                        for which in ("fq", "fk", "fv"):
                            wait_free(pe, (which, u, c))
                if n < FH * HT:
                    h, i = unit(n)
                    t = HT * u + i
                    ps = begin(("S", u, n))
                    w = (t + 1) * P
                    pe.matmul(ps[:, 0:w], qaug[0:66, h, i * P:(i + 1) * P], kaug[0:66, h, 0:w], start=True, stop=False)
                    done(pe.matmul(ps[:, t * P:w], ident[:, :], fox_mask[:, :], start=False, stop=True), ("S", u, n))
                if 1 <= n <= FH * HT:
                    t = HT * u + unit(n - 1)[1]
                    pe.wait_ge(pn_ready, FH * HT * u + n)
                    ps = begin(("PT", u, n - 1))
                    for j in range(t + 1):
                        ins = pe.transpose(ps[:, j * P:(j + 1) * P], FT[:, (n - 1) % 2, j * P:(j + 1) * P], ident[:, :])
                    done(ins, ("PT", u, n - 1))
                if n >= 2:
                    h, i = unit(n - 2)
                    t = HT * u + i
                    wait_free(pe, ("PT", u, n - 2))
                    ps = PS[:, BANK_O, :] if i else begin(("O", u, h))
                    for j in range(t + 1):
                        ins = pe.matmul(ps[0:FDH, i * P:(i + 1) * P], Vr[:, j, h * FDH:(h + 1) * FDH],
                                        FT[:, 2 + (n - 2) % 2, j * P:(j + 1) * P], start=(j == 0), stop=(j == t))
                    if i == HT - 1:
                        done(ins, ("O", u, h))

            def spread(u):
                for job, b0 in (("bg", 0), ("bb", 32)):
                    for j in range(2):
                        ps = begin((job, u, j))
                        for a in range(2):
                            h = 2 * j + a
                            pick = ident[b0:b0 + GH, b0 + h:b0 + h + 1].to_broadcast([GH, P])
                            ins = pe.matmul(ps[:, a * HS:(a + 1) * HS], pick, R[b0:b0 + GH, :], start=True, stop=True)
                        done(ins, (job, u, j))
                pe.wait_ge(qkn_ready, 4 * (u + 1))
                pe.wait_ge(conv_silu, N_CONV * (u + 1))

            def four(job, g, lhs, rhs):
                ps = begin((job, g))
                for h in range(GH):
                    ins = pe.matmul(ps[:, h * P:(h + 1) * P], lhs(h), rhs(h), start=True, stop=True)
                done(ins, (job, g))

            def turn(job, g, src):
                ps = begin((job, g))
                for h in range(GH):
                    ins = pe.transpose(ps[:, h * P:(h + 1) * P], src(h), ident[:, :])
                done(ins, (job, g))

            def of(g, name):
                return lambda h: dn[g // HT][name][:, h * P:(h + 1) * P]

            def at(tile, g):
                i = g % HT
                return lambda h: (tile[h] if isinstance(tile, list) else tile[:, h, :])[:, i * P:(i + 1) * P]

            def kv_(g):
                turn("kt", g, at(kT, g))
                turn("vt", g, at(vT, g))

            def kk_(g):
                u = g // HT
                if g % HT == 0:
                    for j in range(2):
                        wait_free(pe, ("bb", u, j))
                    pe.wait_ge(qd_ready, 2 * (u + 1))
                four("kk", g, at(kT, g), at(kbT[u], g))
                four("qk", g, at(kT, g), at(qT, g))

            def turned(g):
                pe.wait_ge(near_ready, 2 * g + 2)
                turn("D", g, of(g, "N"))
                turn("E", g, of(g, "ET"))

            def sq2(g):
                wait_free(pe, ("D", g))
                four("D2", g, of(g, "N"), of(g, "DD"))
                four("N2", g, of(g, "DD"), of(g, "N"))

            def sq4(g):
                wait_free(pe, ("D2", g))
                pe.wait_ge(y0_ready, g + 1)
                four("Y1", g, of(g, "A"), of(g, "Y"))
                wait_free(pe, ("N2", g))
                four("D4", g, of(g, "B"), of(g, "A"))
                four("N4", g, of(g, "A"), of(g, "B"))

            def sq8(g):
                wait_free(pe, ("D4", g))
                wait_free(pe, ("Y1", g))
                four("Y2", g, of(g, "DD"), of(g, "Y"))
                wait_free(pe, ("N4", g))
                four("D8", g, of(g, "N"), of(g, "DD"))

            def inv(g):
                wait_free(pe, ("D8", g))
                wait_free(pe, ("Y2", g))
                four("Y3", g, of(g, "A"), of(g, "Y"))

            def wmq(g):
                wait_free(pe, ("Y3", g))
                turn("W", g, of(g, "Y"))
                wait_free(pe, ("E", g))
                four("M", g, of(g, "Y"), of(g, "E"))
                four("Q", g, of(g, "E"), of(g, "Y"))

            def m2(g):
                wait_free(pe, ("M", g))
                wait_free(pe, ("Q", g))
                four("M2", g, of(g, "N"), of(g, "DD"))

            def c_(g):
                wait_free(pe, ("M2", g))
                pe.wait_ge(c0_ready, g + 1)
                four("C", g, of(g, "A"), of(g, "C"))

            def tt(g):
                wait_free(pe, ("C", g))
                wait_free(pe, ("W", g))
                four("TT", g, of(g, "B"), of(g, "C"))

            def uw(g):
                for job in ("TT", "vt", "kt"):
                    wait_free(pe, (job, g))
                four("u", g, of(g, "ET"), of(g, "rv"))
                four("wT", g, of(g, "rw"), of(g, "ET"))

            def ws(n):
                g = n // 2
                b0 = CH * (n % 2)
                wait_free(pe, ("wT", g))
                wait_free(pe, ("qk", g))
                if n:
                    wait_free(pe, ("su", n - 1))
                ps = begin(("ws", n))
                for h in range(GH):
                    hs = slice(h * P, (h + 1) * P)
                    ins = pe.matmul(ps[b0:b0 + CH, hs], dn[g // HT]["w"][:, h * P + b0:h * P + b0 + CH], St[:, hs],
                                    start=True, stop=True)
                done(ins, ("ws", n))

            def os_(n):
                g = n // 2
                u = g // HT
                t = dn[u]
                b0 = CH * (n % 2)
                c0 = (n % (2 * HT)) * CH
                rows = slice(b0, b0 + CH)
                wait_free(pe, ("ws", n))
                ps = begin(("o", n))
                for h in range(GH):
                    hs = slice(h * P, (h + 1) * P)
                    dst = ps[:, h * CH:(h + 1) * CH]
                    pe.matmul(dst, St[:, hs], qdT[u][h][:, c0:c0 + CH], start=True, stop=False)
                    ins = pe.matmul(dst, t["vn"][rows, hs], t["a"][rows, h * P + b0:h * P + b0 + CH],
                                    start=False, stop=True)
                done(ins, ("o", n))
                ps = begin(("su", n))
                for h in range(GH):
                    hs = slice(h * P, (h + 1) * P)
                    ins = pe.matmul(ps[:, hs], t["kd"][rows, hs], t["vn"][rows, hs], start=True, stop=True)
                done(ins, ("su", n))

            def onorm(u):
                for j in range(2):
                    pe.wait_ge(osq_ready, 2 * u + j + 1)
                    ps = begin(("oss", u, j))
                    done(pe.matmul(ps, ones[:, :], dn[u][("rv", "rw")[j]], start=True, stop=True), ("oss", u, j))

            def yab(u, c):
                if c == 0:
                    for h in range(FH):
                        wait_free(pe, ("O", u, h))
                    pe.wait_ge(ob_ready, GH * (u + 1))
                w = weights(W_MIX + 3 * c + 2, u)
                ps = begin(("yab", u, c))
                project(w, ps[:, 0:HS], OT, range(4))
                done(project(w, ps[:, HS:S], OBT, range(4, 8), first=False), ("yab", u, c))

            def out_(u, half, c):
                if half == 0 and c == 0:
                    pe.wait_ge(mix_ready, KD * (u + 1))
                w = weights(W_OUT + 4 * half + c, u)
                for i in range(HT):
                    job = ("mix", HT * u + i, half)
                    ps = begin(job) if c == 0 else bank(job)
                    for k in range(KD):
                        ins = pe.matmul(ps[:, c * P:(c + 1) * P], mixT[:, k, i * P:(i + 1) * P], w[:, k, :],
                                        start=(k == 0), stop=(k == KD - 1))
                        past(ins, i == 0 and k == 0)
                    if c == 3:
                        done(ins, job)

            def x1(u, i):
                t = HT * u + i
                pe.wait_ge(h2_ready, t + 1)
                for half in range(2):
                    ps = begin(("h2T", t, half))
                    for k in range(4):
                        ins = pe.transpose(ps[:, k * P:(k + 1) * P],
                                           H2[:, t, half * S + k * P:half * S + (k + 1) * P], ident[:, :])
                    done(ins, ("h2T", t, half))

            def qy(u, j):
                if j == 0:
                    pe.wait_ge(keys_landed, 16)
                    for i in range(HT):
                        for half in range(2):
                            wait_free(pe, ("h2T", HT * u + i, half))
                ps = begin(("qy", u, j))
                for s in range(2):
                    ins = project(weights(W_Q + 2 * j + s, u), ps[:, s * HS:(s + 1) * HS], hT)
                done(ins, ("qy", u, j))

            def sc(u, j):
                wait_free(pe, ("qy", u, j))
                ps = begin(("sc", u, j))
                for i in range(HT):
                    for s in range(2):
                        ins = pe.matmul(ps[:, (2 * i + s) * NK:(2 * i + s + 1) * NK],
                                        FT[:, 2 + j % 2, s * HS + i * P:s * HS + (i + 1) * P], keys[:, s, :],
                                        start=True, stop=True)
                done(ins, ("sc", u, j))

            def weighted(head, k, rows):
                pe.wait_ge(diag_ready, head * TOPK + (k + 1))
                for half in range(2):
                    ins = pe.matmul(PS[:, BANK_Y + half, :], diag[:, k % NDG, :],
                                    rows[:, D + half * S:D + (half + 1) * S],
                                    start=False, stop=False, skip_group_check=True)
                ins.then_inc(e_free, 1)

            def expert(h, k):
                for kk in ([k - LAG[0]] if k >= LAG[0] else []) + (
                        list(range(TOPK - LAG[0], TOPK)) if k == TOPK - 1 else []):
                    weighted(h, kk, slots[0][(h * TOPK + kk) % SLOTS[0]])

            follow({
                ("pe", "ada_col"): ada_col, ("pe", "row"): row, ("pe", "norm"): norm, ("pe", "small"): small,
                ("pe", "conv"): projection("conv", lambda c: W_CONV + c), ("pe", "gz"): projection("gz", lambda c: W_GZ + c),
                ("pe", "unit"): unit_norm, ("pe", "fq"): projection("fq", lambda c: W_F + c),
                ("pe", "fk"): projection("fk", lambda c: W_F + 4 + c), ("pe", "fv"): fv, ("pe", "cols"): cols,
                ("pe", "att"): att, ("pe", "spread"): spread, ("pe", "kv"): kv_, ("pe", "kk"): kk_,
                ("pe", "turn"): turned, ("pe", "sq2"): sq2, ("pe", "sq4"): sq4, ("pe", "sq8"): sq8, ("pe", "inv"): inv,
                ("pe", "wmq"): wmq, ("pe", "m2"): m2, ("pe", "c"): c_, ("pe", "tt"): tt, ("pe", "uw"): uw,
                ("pe", "ws"): ws, ("pe", "os"): os_, ("pe", "onorm"): onorm,
                ("pe", "ga"): projection("ga", lambda c: W_MIX + 3 * c),
                ("pe", "gb"): projection("gb", lambda c: W_MIX + 3 * c + 1), ("pe", "yab"): yab, ("pe", "out"): out_,
                ("pe", "x1"): x1, ("pe", "qy"): qy, ("pe", "sc"): sc,
                "sums": lambda t: pe.wait_ge(y_zero, t + 1), "expert": expert,
            })
            assert n_w[0] == N_W + N_AGAIN
            with pe.Fori(HT, NT) as t:
                pe.wait_ge(y_zero, t + 1)
                pe.sem_inc(seen_pe, 1)
                with pe.Fori(0, PH // 2) as b:
                    for p in range(2):
                        for k in range(TOPK):
                            weighted(t * PH + b * 2 + p, k, slots[1][k % SLOTS[1]])


def kernel(x, c, w_ada, b_ada, g_pre_mix, g_post_mix, w_in, b_fgate, fox_w_o, conv_w, a_log, dt_bias,
           gdn_norm_w, gdn_w_o, b_branch_gate, w_out, g_pre_ffn, g_post_ffn, peer_w_query, peer_keys1,
           peer_keys2, peer_u, peer_v):
    import concourse.bacc as bacc
    from concourse.bass_utils import run_bass_kernel_spmd as run

    def tiles(m):
        m = np.asarray(m)
        k, n = m.shape
        return m.reshape(k // P, P, n // P, P).transpose(2, 1, 0, 3).reshape(n // P, P, k)

    def cols(v):
        return np.asarray(v).reshape(-1, P).T

    wi = np.asarray(w_in)[0]
    cut = np.cumsum([0, 512, 512, 512, FH, 512, 512, 512, 512, GH, GH, D, D])
    fq, fk, fv, f, gq, gk, gv, gz, beta, decay, ga, gb = (wi[:, a:b] for a, b in zip(cut[:-1], cut[1:]))
    ada = np.asarray(w_ada)[0]
    mix = np.stack([tiles(ga), tiles(gb), np.concatenate([tiles(fox_w_o[0]), tiles(gdn_w_o[0])], axis=2)], axis=1)
    w_tiles = np.concatenate([
        tiles(ada), tiles(gq), tiles(gk), tiles(gv), tiles(gz), tiles(fq), tiles(fk), tiles(fv), mix.reshape(3 * KD, P, D), tiles(w_out[0]), tiles(peer_w_query[0])], axis=0)
    small = np.concatenate([f, beta, decay], axis=1).reshape(KD, P, 16).transpose(1, 0, 2).reshape(P, KD * 16)
    bias = np.asarray(b_ada)[0]
    arrays = {
        "x_rows": np.asarray(x)[0].reshape(NT, P, D).transpose(1, 0, 2),
        "x_cols": np.asarray(x)[0].T.reshape(KD, P, 2, HS).transpose(2, 1, 0, 3),
        "c_cols": cols(c),
        "w_tiles": w_tiles,
        "w_small": small,
        "b_small": np.concatenate([np.asarray(b_fgate)[0], np.asarray(dt_bias)[0], np.asarray(a_log)[0]]).reshape(-1, 1),
        "ada_cols": cols(bias[0:2 * D]),
        "ada_rows": bias[2 * D:6 * D],
        "gains_cols": np.concatenate([cols(g_pre_mix), cols(np.asarray(b_branch_gate)[0, 0]),
                                      cols(np.asarray(b_branch_gate)[0, 1]), cols(gdn_norm_w)], axis=1),
        "gain_rows": np.concatenate([np.asarray(g_post_mix)[0], np.asarray(g_pre_ffn)[0], np.asarray(g_post_ffn)[0]]),
        "conv_cols": np.asarray(conv_w)[0].T.reshape(N_CONV, P, CONV).transpose(1, 0, 2),
        "keys_t": np.stack([np.asarray(peer_keys1)[0].T, np.asarray(peer_keys2)[0].T], axis=1),
        "experts": np.concatenate([np.asarray(peer_u)[0], np.asarray(peer_v)[0]], axis=1),
    }
    nc = bacc.Bacc("TRN2", target_bir_lowering=False, num_devices=1)
    fed, args = {}, {}
    for name, a in arrays.items():
        a = np.ascontiguousarray(a)
        fed[f"in_{name}"] = a
        args[name] = nc.dram_tensor(f"in_{name}", a.shape, mybir.dt.from_np(a.dtype), kind="ExternalInput").ap()
    out = nc.dram_tensor("out_x", (NT, P, D), F32, kind="ExternalOutput").ap()
    hybrid_block(nc, out=out, **args)
    return run(nc, [fed], core_ids=[0]).results[0]["out_x"].reshape(1, S, D)
```

```python
from contextlib import ExitStack

import numpy as np

import concourse.bass as bass
from concourse import mybir

P = 128
D = 1024
KD = D // P
S = 512
NT = S // P
HS = S // 2
HT = NT // 2
FH, FDH = 8, 64
GH = 4
CH = 64
CONV = 4
PH = 8
NK = 128
TOPK = 16
EPS = 1e-6
NEG = -1.0e30
LOWEST = -3.0e38

RING = 4
U_SLOTS = (4, 8)
V_SLOTS = (6, 8)
V_BEHIND = 2
NDG = 4
LAG = (2, 2)
PE_LAG = 3
HEADS = HT * PH
NEXP = HEADS * TOPK

VEC_K = (1, 3, 6, 9, 11, 14)

N_COL = 2 * KD
N_CONV = 12
N_GZ = 4
N_F = 12
N_MIX = 3 * KD
N_ROW = 4 * KD
N_OUT = KD
N_Q = 16
W_COL = 0
W_CONV = W_COL + N_COL
W_GZ = W_CONV + N_CONV
W_F = W_GZ + N_GZ
W_ROW = W_F + N_F
W_MIX = W_ROW + N_ROW
W_OUT = W_MIX + N_MIX
W_Q = W_OUT + N_OUT
N_W = W_Q + N_Q
USES = list(range(N_W)) + list(range(W_CONV, W_ROW)) + list(range(W_MIX, N_W))

F32 = mybir.dt.float32
U32 = mybir.dt.uint32
ALU = mybir.AluOpType
ACT = mybir.ActivationFunctionType
AX = mybir.AxisListType

TURN, BANK_O, BANK_Y = 5, 5, 6


def attention_stages(u):
    return [(("att", u, n), 2.2 if u else 1.2) for n in range(FH * HT)] + [
        (("att", u, FH * HT + n), 1.0) for n in range(3)]


def deltanet_stages(u):
    out = [(("spread", u), 3.4)]
    for g in (HT * u, HT * u + 1):
        out += [((name, g), cost) for name, cost in (
            ("kv", 0.5), ("kk", 1.7), ("turn", 0.5), ("sq2", 1.7), ("sq4", 2.6), ("sq8", 1.7), ("inv", 0.9),
            ("wmq", 1.9), ("m2", 0.9), ("c", 0.9), ("tt", 0.9), ("uw", 1.7))]
        for n in (2 * g, 2 * g + 1):
            out += [(("ws", n), 0.9), (("os", n), 1.8)]
    return out


def first_stages(u):
    out = [(("norm", u), 3.4), (("small", u), 3.4)]
    convs = [(("conv", u, c), 3.4) for c in range(N_CONV)]
    out += convs[0:2] + [(("small1", u), 0.0)] + convs[2:4] + [(("small2", u), 0.0)] + convs[4:]
    out += [(("gz", u, c), 3.4) for c in range(N_GZ)]
    out += [(("unit", u, j), 0.9) for j in range(4)]
    out += [((w, u, c), 3.4) for w in ("fq", "fk", "fv") for c in range(4)]
    return out + [(("cols", u), 0.2)]


def last_stages(u):
    out = [(("onorm", u), 1.8)]
    for c in range(KD):
        out += [(("ga", u, c), 3.4), (("gb", u, c), 3.4), (("yab", u, c), 3.4)]
    out += [(("out", u, half, c), 3.4) for half in range(2) for c in range(4)]
    for step in ("mixed", "added", "squared", "modulated"):
        out += [((step, u, i), 2.5) for i in range(HT)]
    out += [(("x1", u, i), 0.5) for i in range(HT)]
    out += [(("qy", u, 0), 6.8)]
    for j in range(N_Q // 2):
        out += ([(("qy", u, j + 1), 6.8)] if j + 1 < N_Q // 2 else []) + [(("sc", u, j), 1.8)]
    return out


def mod_stages():
    return [(("row", c), 6.8) for c in range(N_ROW // 4)]


def added_by_pe(n):
    return n % TOPK not in VEC_K


def count_pe(n):
    return sum(added_by_pe(m) for m in range(n))


PE_FIRST = count_pe(NEXP)
LATER = PE_FIRST - NEXP


def behind(n, lag):
    first = n // (PH * TOPK) * (PH * TOPK)
    return range(max(n - lag, first), n + 1 if (n + 1) % (PH * TOPK) == 0 else max(n - lag + 1, first))


def woven(a, b):
    tagged = [((n + 0.5) / len(a), 0, x) for n, x in enumerate(a)] + [((n + 0.5) / len(b), 1, x) for n, x in enumerate(b)]
    return [x for _, _, x in sorted(tagged, key=lambda t: t[:2])]


def build_order():
    order = []

    def now(stages):
        for stage, _ in stages:
            order.extend([("pe",) + stage, ("post",) + stage])

    now([(("ada_col", c), 0) for c in range(N_COL // 4)])
    now(first_stages(0))
    now(woven(woven(attention_stages(0), deltanet_stages(0)), mod_stages()))
    last = last_stages(0)
    cut = [stage for stage, _ in last].index(("sc", 0, 0)) + 1
    now(last[:cut])
    front = (last[cut:] + first_stages(1) + attention_stages(1)
             + [(stage, max(cost, 2.2)) for stage, cost in deltanet_stages(1)] + last_stages(1))
    total = sum(cost for _, cost in front)
    order.append(("choose_all", 0))
    order.append(("sums", 0))
    spent, gone, pending = 0.0, 0, None
    for n in range(NEXP):
        h, k = divmod(n, TOPK)
        if k == 0:
            order.append(("gates", h))
            if h % PH == 0 and h:
                order.append(("sums", h // PH))
        order.append(("expert", h, k))
        if pending:
            order.append(("post",) + pending)
            pending = None
        at = (5, 7, 9, 11) if h == 0 else (1, 4, 7, 10)
        if k in at:
            assert ("post", "sc", (h + 1) // HEADS, (h + 1) % PH) in order
            order.append(("choose", h + 1, at.index(k)))
        while gone < len(front) and spent < total * (n + 1) / (NEXP - 4):
            if pending:
                order.append(("post",) + pending)
            pending, cost = front[gone]
            order.append(("pe",) + pending)
            spent += cost
            gone += 1
    assert gone == len(front)
    if pending:
        order.append(("post",) + pending)
    return order


JOBS = {
    "kv": ("kt", "vt"), "kk": ("kk", "qk"), "turn": ("D", "E"), "sq2": ("D2", "N2"), "sq4": ("Y1", "D4", "N4"),
    "sq8": ("Y2", "D8"), "inv": ("Y3",), "wmq": ("W", "M", "Q"), "m2": ("M2",), "c": ("C",), "tt": ("TT",),
    "uw": ("u", "wT"), "ws": ("ws",), "os": ("o", "su"),
}


def jobs_of(stage):
    name, *a = stage
    if name == "norm":
        return [("xsq", *a)]
    if name in ("small1", "small2", "mixed", "added", "squared", "modulated"):
        return []
    if name == "att":
        u, n = a
        out = [("S", u, n)] if n < FH * HT else []
        out += [("PT", u, n - 2)] if 2 <= n < FH * HT + 2 else []
        return out + ([("O", u, (n - 3) // HT)] if n >= 3 and (n - 3) % HT == 0 else [])
    if name == "spread":
        return [("bg", a[0], j) for j in range(2)] + [("bb", a[0], j) for j in range(2)]
    if name == "onorm":
        return [("oss", a[0], j) for j in range(2)]
    if name == "out":
        u, half, c = a
        return [("mix", HT * u + i, half) for i in range(HT)] if c == 0 else []
    if name == "x1":
        u, i = a
        return [("h2T", HT * u + i, half) for half in range(2)]
    if name in JOBS:
        return [(j, *a) for j in JOBS[name]]
    return [stage]


def psum_jobs(order):
    table, used, turn = {}, [0] * 8, 0
    for item in order:
        if item[0] != "pe":
            continue
        for job in jobs_of(item[1:]):
            if job[0] == "O":
                bank = BANK_O
            else:
                bank = turn % TURN
                turn += 1
            used[bank] += 1
            assert job not in table
            table[job] = (bank, used[bank])
    return table


def hybrid_block(nc, x_rows, x_cols, c_cols, w_tiles, w_small, b_small, ada_cols, ada_rows, gains_cols,
                 gain_rows, conv_cols, keys_t, peer_u, peer_v, out):
    order = build_order()
    jobs = psum_jobs(order)
    ctx = ExitStack()
    with ctx:
        def sb(name, shape, dt=F32):
            return ctx.enter_context(nc.sbuf_tensor(name, shape, dt))

        def sem(name):
            return ctx.enter_context(nc.semaphore(name))

        ident = sb("ident", [P, P])
        ones = sb("ones", [P, P])
        near = sb("near_mask", [P, P])
        far = sb("far_mask", [P, P])
        causal = sb("causal_mask", [P, P])
        fox_mask = sb("fox_mask", [P, P])
        iota16 = sb("iota16", [P, TOPK])
        eps = sb("eps", [P, 1])
        scan_a = sb("scan_a", [68, HS])
        silu_c = sb("silu_c", [P, KD])
        small_b = sb("small_b", [P, 4])
        bcol = sb("bcol", [P, N_COL])
        gcols = sb("gcols", [P, 3 * KD + 1])
        mcol = sb("mcol", [P, N_COL])
        convw = sb("convw", [P, N_CONV, CONV])
        tails = sb("tails", [P, N_CONV, CONV - 1])
        keys = sb("keys", [P, 2, NK])
        scale1 = sb("scale1", [P, KD])
        shift1 = sb("shift1", [P, KD])
        stat = sb("stat", [P, 56])
        carry = sb("carry", [FH, 1])
        R = sb("R", [P, HS])
        rcols = sb("rcols", [P, HT, P])
        X = sb("X", [P, NT, D])
        mods = sb("mods", [P, 4, D])
        H2 = sb("H2", [P, NT, D])
        pool_e = sb("pool_e", [P, U_SLOTS[0] + V_SLOTS[0], D])
        ring_t = sb("ring", [P, RING, D])
        hT = sb("hT", [P, KD, HS])
        kaug = sb("kaug", [P, FH, S])
        qaug = sb("qaug", [P, FH, HS])
        Vr = sb("Vr", [P, NT, S])
        gT = sb("gT", [P, N_CONV, HS])
        gzT = sb("gzT", [P, GH, HS])
        OT = sb("OT", [P, NT, HS])
        OBT = sb("OBT", [P, GH, HS])
        scores0 = sb("scores0", [P, HEADS, 2 * NK])
        FT = sb("FT", [P, 4, S])
        St = sb("St", [P, S])
        diag = sb("diag", [P, NDG, P])
        work = sb("work", [P, 2, 2 * NK])
        kv = sb("kv", [P, 2 * TOPK])
        ki = sb("ki", [P, 2 * TOPK], U32)
        kf = sb("kf", [P, 2 * TOPK])
        pos = sb("pos", [P, 3 * TOPK], U32)
        posf = sb("posf", [P, 4 * TOPK])
        idx_sb = [sb(f"idx{p}", [P, TOPK], U32) for p in range(2)]
        tops = [sb(f"tops{p}", [P, TOPK]) for p in range(2)]
        gate = [sb(f"gate{p}", [P, TOPK + 4]) for p in range(2)]
        dots = [sb(f"dots{p}", [P, TOPK]) for p in range(2)]
        acts = [sb(f"acts{p}", [P, TOPK]) for p in range(2)]
        wts = [sb(f"wts{p}", [P, TOPK]) for p in range(2)]

        ring = ring_t[:, :, :].rearrange("p s (k m) -> p s k m", k=KD)
        scores = (scores0[:, :, :], kaug[:, :, :].rearrange("p h (a k) -> p (h a) k", a=2))
        own = [pool_e[:, s, :] for s in range(U_SLOTS[0] + V_SLOTS[0])]
        u_slots = (own[:U_SLOTS[0]], own[:U_SLOTS[0]] + [
            Vr[:, 0:2, :].rearrange("p h t -> p (h t)"), Vr[:, 2:4, :].rearrange("p h t -> p (h t)"),
            gT[:, 0:4, :].rearrange("p h t -> p (h t)"), gT[:, 4:8, :].rearrange("p h t -> p (h t)")])
        v_slots = (own[U_SLOTS[0]:], own[U_SLOTS[0]:] + [
            qaug[:, 0:4, :].rearrange("p h t -> p (h t)"), qaug[:, 4:8, :].rearrange("p h t -> p (h t)")])
        high = X[:, HT:NT, :].rearrange("p a (b t) -> p (a b) t", t=HS)
        Z, T1, T2, T3, T4 = (high[:, n, :] for n in range(5))
        CF = T3
        wsm = X[:, HT:NT, :].rearrange("p a d -> p (a d)")[:, 5 * HS:5 * HS + KD * 68].rearrange(
            "p (k m) -> p k m", k=KD)
        wsm_in = OT[:, 0, 0:KD * 16]
        sq = FT[:, :, :].rearrange("p a (b t) -> p (a b) t", b=2)
        flat = FT[:, :, :].rearrange("p a t -> p (a t)")
        pads = [flat[:, n * 260:n * 260 + HS + CONV - 1] for n in range(2)]
        mixT = qaug[:, :, :]

        silu_cb = Vr[:, HT:NT, :].rearrange("p a (k m) -> p (a k) m", m=P)
        grow = scores0[:, 0:12, :].rearrange("p (a b) k -> p a (b k)", a=3)
        vec_sum = (H2[:, NT - 1, :], scores0[:, 0:4, :].rearrange("p a b -> p (a b)"))

        space = (
            [tile[:, t * S:(t + 1) * S] for tile in own for t in range(2)],
            [kaug[:, t, :] for t in range(FH)] + [Vr[:, t, :] for t in range(NT)]
            + [qaug[:, 2 * t:2 * t + 2, :].rearrange("p a b -> p (a b)") for t in range(4)]
            + [X[:, HT + t // 2, (t % 2) * S:(t % 2 + 1) * S] for t in range(4)])

        def pair(u, n):
            return [space[u][n + h // 2][:, (h % 2) * HS:(h % 2 + 1) * HS] for h in range(GH)]

        names = ("A", "B", "N", "ET", "DD", "E", "Y", "C", "rv", "rw", "a", "kd")
        dn = [{name: space[u][8 + n] for n, name in enumerate(names)} for u in range(2)]
        for tiles in dn:
            tiles.update(u=tiles["DD"], w=tiles["N"], vn=tiles["Y"])
        Gb, expG, kbT, qdT = ([pair(u, 2 * n) for u in range(2)] for n in range(4))
        qT, kT, vT = gT[:, 0:4, :], gT[:, 4:8, :], gT[:, 8:12, :]

        PS = ctx.enter_context(nc.psum_tensor("PS", [P, 8, S], F32))

        def bank(job):
            return PS[:, jobs[job][0], :]

        full = [sem(f"full{b}") for b in range(6)]
        free = [sem(f"free{b}") for b in range(6)]
        w_landed = [sem(f"w_landed{s}") for s in range(RING)]
        u_landed = [[sem(f"u_landed{u}_{s}") for s in range(U_SLOTS[u])] for u in range(2)]
        v_landed = [[sem(f"v_landed{u}_{s}") for s in range(V_SLOTS[u])] for u in range(2)]
        w_used = sem("w_used")
        x_landed = sem("x_landed")
        x2_landed = sem("x2_landed")
        xc_landed = sem("xc_landed")
        c_landed = sem("c_landed")
        keys_landed = sem("keys_landed")
        small_landed = sem("small_landed")
        aug_landed = sem("aug_landed")
        out_landed = sem("out_landed")
        pool_chain = sem("pool_chain")
        consts_ready = sem("consts_ready")
        act_chain = sem("act_chain")
        dve_chain = sem("dve_chain")
        silu_ready = sem("silu_ready")
        silub_ready = sem("silub_ready")
        base_ready = sem("base_ready")
        rows_landed = sem("rows_landed")
        sq_ready = sem("sq_ready")
        mod_cols = sem("mod_cols")
        root_ready = sem("root_ready")
        h_ready = sem("h_ready")
        abs_ready = sem("abs_ready")
        ln_ready = sem("ln_ready")
        g_ready = sem("g_ready")
        gexp_ready = sem("gexp_ready")
        rows_ready = sem("rows_ready")
        cum_ready = sem("cum_ready")
        conv_ready = sem("conv_ready")
        conv_silu = sem("conv_silu")
        gsq_ready = sem("gsq_ready")
        qkn_ready = sem("qkn_ready")
        smax_ready = sem("smax_ready")
        rsum_ready = sem("rsum_ready")
        pn_ready = sem("pn_ready")
        qd_ready = sem("qd_ready")
        dec_in = sem("dec_in")
        dec_ready = sem("dec_ready")
        near_ready = sem("near_ready")
        y0_ready = sem("y0_ready")
        c0_ready = sem("c0_ready")
        osq_ready = sem("osq_ready")
        ob_ready = sem("ob_ready")
        sig_used = sem("sig_used")
        mix_ready = sem("mix_ready")
        mroot_ready = sem("mroot_ready")
        xroot_ready = sem("xroot_ready")
        x1_ready = sem("x1_ready")
        h2_ready = sem("h2_ready")
        idx_ready = sem("idx_ready")
        top_ready = sem("top_ready")
        gate_ready = sem("gate_ready")
        dot_ready = sem("dot_ready")
        gelu_ready = sem("gelu_ready")
        diag_ready = sem("diag_ready")
        e_free = sem("e_free")
        vec_used = sem("vec_used")
        y_whole = sem("y_whole")
        y_zero = sem("y_zero")
        y_out = sem("y_out")
        seen_pool = sem("seen_pool")
        seen_act = sem("seen_act")
        seen_pe = sem("seen_pe")
        fsq_ready = sem("fsq_ready")
        fss_ready = sem("fss_ready")
        fin_ready = sem("fin_ready")

        def wait_full(eng, job):
            eng.wait_ge(full[jobs[job][0]], jobs[job][1])

        def wait_free(eng, job):
            eng.wait_ge(free[jobs[job][0]], jobs[job][1])

        def frees(ins, job):
            ins.then_inc(free[jobs[job][0]], 1)

        def bcast(ap, n):
            return ap.unsqueeze(2).to_broadcast([ap.shape[0], ap.shape[1], n])

        def heads(ap):
            return ap.rearrange("p (h m) -> p h m", h=GH)

        def mid(ap, n):
            return ap.unsqueeze(1).to_broadcast([ap.shape[0], n, ap.shape[1]])

        def wait_v_used(eng, n):
            if added_by_pe(n):
                eng.wait_ge(e_free, count_pe(n + 1))
            else:
                eng.wait_ge(vec_used, n + 1 - count_pe(n + 1))

        def unit(n):
            return n // HT, n % HT

        def follow(stages):
            for item in order:
                if item[0] in ("pe", "post"):
                    part = stages.get(item[:2])
                    if part:
                        part(*item[2:])
                elif item[0] in stages:
                    stages[item[0]](*item[1:])

        block = ctx.enter_context(nc.Block())

        @block.sync
        def _(sp):
            sp.dma_start(silu_c[:, :], c_cols).then_inc(c_landed, 16)
            for s in range(RING):
                sp.dma_start(ring_t[:, s, :], w_tiles[s]).then_inc(w_landed[s], 16)
            sp.dma_start(hT[:, :, :], x_cols[0]).then_inc(xc_landed, 16)
            sp.dma_start(keys[:, :, :], keys_t).then_inc(keys_landed, 16)

            def tile(r, s, back):
                sp.wait_ge(w_used, r * RING + (s + 1 - RING))
                sp.dma_start(ring_t[:, s, :],
                             w_tiles[bass.ds(r * RING + (s - back), 1)].rearrange("o p m -> (o p) m")
                             ).then_inc(w_landed[s], 16)

            with sp.Fori(1, N_W // RING) as r:
                for s in range(RING):
                    tile(r, s, 0)
            wait_full(sp, ("qy", 0, N_Q // 2 - 1))
            sp.dma_start(hT[:, :, :], x_cols[1]).then_inc(xc_landed, 16)
            again = N_W + (W_ROW - W_CONV)
            with sp.Fori(N_W // RING, again // RING) as r:
                for s in range(RING):
                    tile(r, s, N_W - W_CONV)
            with sp.Fori(again // RING, len(USES) // RING) as r:
                for s in range(RING):
                    tile(r, s, again - W_MIX)
            for i in range(NT):
                sp.wait_ge(fin_ready, i + 1)
                sp.dma_start(out[i], X[:, i, :]).then_inc(out_landed, 16)
            sp.wait_ge(out_landed, 16 * NT)

        @block.gpsimd
        def _(pool):
            n_chain = [0]

            def link(ins):
                n_chain[0] += 1
                ins.then_inc(pool_chain, 1)
                pool.wait_ge(pool_chain, n_chain[0])

            link(pool.memset(ones[:, :], 1.0))
            link(pool.memset(ident[:, :], 0.0))
            link(pool.affine_select(out=ident[:, :], in_=ident[:, :], compare_op=ALU.not_equal, fill=1.0,
                                    base=0, pattern=[[-1, P]], channel_multiplier=1))
            link(pool.memset(eps[:, :], EPS))
            pool.sem_inc(base_ready, 1)
            pool.dma_start(wsm_in, w_small).then_inc(small_landed, 16)
            pool.dma_start(bcol[:, :], ada_cols).then_inc(small_landed, 16)
            pool.dma_start(gcols[:, :], gains_cols).then_inc(small_landed, 16)
            pool.dma_start(convw[:, :, :], conv_cols).then_inc(small_landed, 16)
            link(pool.memset(small_b[:, :], 0.0))
            pool.dma_start(small_b[0:FH, 0:1], b_small[0:FH, :]).then_inc(small_landed, 16)
            pool.dma_start(small_b[64:64 + GH, 0:1], b_small[FH:FH + GH, :]).then_inc(small_landed, 16)
            pool.dma_start(small_b[64:64 + GH, 1:2], b_small[FH + GH:FH + 2 * GH, :]).then_inc(small_landed, 16)
            link(pool.affine_select(out=causal[:, :], in_=ones[:, :], compare_op=ALU.is_ge, fill=0.0,
                                    base=0, pattern=[[1, P]], channel_multiplier=-1))
            blk = causal[:, :].rearrange("p (b i) -> p b i", i=CH)
            link(pool.affine_select(out=blk, in_=blk, compare_op=ALU.is_ge, fill=0.0,
                                    base=0, pattern=[[-CH, P // CH], [0, CH]], channel_multiplier=1))
            link(pool.affine_select(out=near[:, :], in_=ones[:, :], compare_op=ALU.is_gt, fill=0.0,
                                    base=0, pattern=[[1, P]], channel_multiplier=-1))
            blk = near[:, :].rearrange("p (b i) -> p b i", i=16)
            link(pool.affine_select(out=blk, in_=blk, compare_op=ALU.is_ge, fill=0.0,
                                    base=0, pattern=[[-16, P // 16], [0, 16]], channel_multiplier=1))
            link(pool.tensor_tensor(out=far[:, :], in0=causal[:, :], in1=near[:, :], op=ALU.subtract))
            link(pool.tensor_tensor(out=far[:, :], in0=far[:, :], in1=ident[:, :], op=ALU.subtract))
            link(pool.memset(fox_mask[:, :], 0.0))
            link(pool.affine_select(out=fox_mask[:, :], in_=fox_mask[:, :], compare_op=ALU.is_ge, fill=NEG,
                                    base=0, pattern=[[-1, P]], channel_multiplier=1))
            link(pool.iota(iota16[:, :], pattern=[[1, TOPK]], base=0, channel_multiplier=0,
                           allow_small_or_imprecise_dtypes=True))
            link(pool.memset(scan_a[:, :], 1.0))
            link(pool.memset(scan_a[64:64 + GH, :].rearrange("p (n i) -> p n i", i=CH)[:, :, 0:1], 0.0))
            link(pool.memset(R[:, :], 0.0))
            link(pool.memset(St[:, :], 0.0))
            link(pool.memset(wsm[:, :, :], 0.0))
            pool.wait_ge(small_landed, 7 * 16)
            win = wsm_in.rearrange("p (k m) -> p k m", k=KD)
            link(pool.tensor_copy(wsm[:, :, 0:8], win[:, :, 0:8]))
            link(pool.tensor_copy(wsm[:, :, 32:36], win[:, :, 8:12]))
            link(pool.tensor_copy(wsm[:, :, 64:68], win[:, :, 12:16]))
            pool.sem_inc(consts_ready, 1)
            pool.dma_start(mods[:, :, :].rearrange("p a b -> p (a b)"),
                           ada_rows.partition_broadcast(P)).then_inc(rows_landed, 16)
            pool.dma_start(grow.rearrange("p a b -> p (a b)"), gain_rows.partition_broadcast(P)).then_inc(rows_landed, 16)
            pool.dma_start(X[:, 0:HT, :], x_rows[:, 0:HT, :]).then_inc(x_landed, 16)

            def gather(table, p, k, slot, landed):
                pool.indirect_dma_start(
                    out=slot, out_offset=None, in_=table,
                    in_offset=bass.IndirectOffsetOnAxis(ap=idx_sb[p][:, k:k + 1], axis=0),
                ).then_inc(landed, 16)

            def gather_u(u, n, p, k):
                slot = n % U_SLOTS[u]
                gather(peer_u, p, k, u_slots[u][slot], u_landed[u][slot])

            def gather_v(u, n, p, k):
                slot = n % V_SLOTS[u]
                gather(peer_v, p, k, v_slots[u][slot], v_landed[u][slot])

            for n in range(NEXP + V_BEHIND):
                if n < NEXP:
                    h, k = divmod(n, TOPK)
                    if k == 0:
                        pool.wait_ge(idx_ready, h + 1)
                    if n >= U_SLOTS[0]:
                        pool.wait_ge(dot_ready, n + 1 - U_SLOTS[0])
                    gather_u(0, n, h % 2, k)
                m = n - V_BEHIND
                if m >= 0:
                    if m >= V_SLOTS[0]:
                        wait_v_used(pool, m - V_SLOTS[0])
                    gather_v(0, m, m // TOPK % 2, m % TOPK)
            for k in range(2 * TOPK):
                if k % TOPK == 0:
                    pool.wait_ge(idx_ready, HEADS + 1 + k // TOPK)
                if k < U_SLOTS[0]:
                    pool.wait_ge(dot_ready, 1 + max(n for n in range(NEXP) if n % U_SLOTS[0] == k))
                elif k >= U_SLOTS[1]:
                    pool.wait_ge(dot_ready, NEXP + k + 1 - U_SLOTS[1])
                gather_u(1, k, k // TOPK, k % TOPK)
                if k < V_SLOTS[0]:
                    wait_v_used(pool, max(n for n in range(NEXP) if n % V_SLOTS[0] == k))
                elif k >= V_SLOTS[1]:
                    pool.wait_ge(e_free, PE_FIRST + k + 1 - V_SLOTS[1])
                gather_v(1, k, k // TOPK, k % TOPK)
            with pool.Fori(1, HEADS // 2) as b:
                for p in range(2):
                    head = b * 2 + (HEADS + p)
                    pool.wait_ge(idx_ready, head + 1)
                    pool.sem_inc(seen_pool, 1)
                    for k in range(0, TOPK, 2):
                        pool.wait_ge(dot_ready, head * TOPK + (k + 2 - U_SLOTS[1]))
                        pool.sem_inc(seen_pool, 1)
                        gather_u(1, k, p, k)
                        gather_u(1, k + 1, p, k + 1)
                        pool.wait_ge(e_free, head * TOPK + (k + 2 - V_SLOTS[1] + LATER))
                        pool.sem_inc(seen_pool, 1)
                        gather_v(1, k, p, k)
                        gather_v(1, k + 1, p, k + 1)

        @block.scalar
        def _(act):
            n_chain = [0]

            def link(ins):
                n_chain[0] += 1
                ins.then_inc(act_chain, 1)
                act.wait_ge(act_chain, n_chain[0])

            act.wait_ge(c_landed, 16)
            act.activation(silu_c[:, :], silu_c[:, :], ACT.Silu).then_inc(silu_ready, 1)
            act.wait_ge(silu_ready, 1)
            act.wait_ge(base_ready, 1)
            for k in range(KD):
                ins = act.mul(silu_cb[:, k, :], ones[:, :], silu_c[:, k:k + 1])
            ins.then_inc(silub_ready, 1)

            def squares(u):
                act.wait_ge(xc_landed, 16 * (u + 1))
                for k in range(KD):
                    act.activation(sq[:, k, :], hT[:, k, :], ACT.Square).then_inc(sq_ready, 1)

            def norm(u):
                wait_full(act, ("xsq", u))
                frees(act.activation(T1, bank(("xsq", u))[:, 0:HS], ACT.Sqrt, bias=eps[:, 0:1], scale=1.0 / D),
                      ("xsq", u))
                act.wait_ge(mod_cols, 2)
                for k in range(KD):
                    act.wait_ge(root_ready, KD * u + k + 1)
                    act.activation(hT[:, k, :], hT[:, k, :], ACT.Identity, bias=shift1[:, k:k + 1],
                                   scale=scale1[:, k:k + 1]).then_inc(h_ready, 1)

            def conv_silu_of(u, c):
                act.wait_ge(conv_ready, N_CONV * u + c + 1)
                act.activation(gT[:, c, :], gT[:, c, :], ACT.Silu).then_inc(conv_silu, 1)

            def conv(u, c):
                pad = pads[c % 2]
                ps = bank(("conv", u, c))
                wait_full(act, ("conv", u, c))
                if c >= 2:
                    act.wait_ge(conv_ready, N_CONV * u + c - 1)
                if u:
                    act.copy(pad[:, 0:CONV - 1], tails[:, c, :])
                else:
                    act.mul(pad[:, 0:CONV - 1], ones[:, 0:CONV - 1], 0.0)
                    act.copy(tails[:, c, :], ps[:, HS - CONV + 1:HS])
                act.copy(pad[:, CONV - 1:], ps[:, 0:HS])
                frees(act.mul(gT[:, c, :], ps[:, 0:HS], convw[:, c, CONV - 1:CONV]), ("conv", u, c))
                if c >= 1:
                    conv_silu_of(u, c - 1)

            def gz(u, c):
                if c == 0:
                    conv_silu_of(u, N_CONV - 1)
                wait_full(act, ("gz", u, c))
                frees(act.activation(gzT[:, c, :], bank(("gz", u, c))[:, 0:HS], ACT.Silu), ("gz", u, c))
                if c < 2:
                    unit_squares(u, c)

            def unit_squares(u, j):
                act.wait_ge(conv_silu, N_CONV * u + 2 * j + 2)
                act.activation(FT[:, j % 2, :].rearrange("p (a t) -> p a t", a=2), gT[:, 2 * j:2 * j + 2, :],
                               ACT.Square).then_inc(gsq_ready, 1)

            def unit_root(u, j):
                wait_full(act, ("unit", u, j))
                if j >= 2:
                    act.wait_ge(qkn_ready, 4 * u + j - 1)
                frees(act.activation(FT[:, 2 + j % 2, :], bank(("unit", u, j)), ACT.Sqrt, bias=eps[:, 0:1]),
                      ("unit", u, j))
                if j < 2:
                    unit_squares(u, j + 2)

            def pair_rows(which, dst, cols, scale):
                def stage(u, c):
                    wait_full(act, (which, u, c))
                    ps = bank((which, u, c))
                    span = cols(u)
                    act.mul(dst[0:FDH, 2 * c, span], ps[0:FDH, 0:HS], scale)
                    frees(act.mul(dst[0:FDH, 2 * c + 1, span], ps[FDH:P, 0:HS], scale), (which, u, c))
                return stage

            def fv(u, c):
                wait_full(act, ("fv", u, c))
                frees(act.copy(Vr[:, HT * u:HT * u + HT, c * P:(c + 1) * P],
                               bank(("fv", u, c))[:, 0:HS].rearrange("p (i m) -> p i m", i=HT)), ("fv", u, c))

            def small(u):
                act.wait_ge(abs_ready, u + 1)
                link(act.activation(T1[0:68, :], T1[0:68, :], ACT.Exp, scale=-1.0))
                link(act.activation(T2[32:32 + GH, :], Z[32:32 + GH, :], ACT.Exp, scale=-1.0))
                if not u:
                    link(act.activation(small_b[64:64 + GH, 2:3], small_b[64:64 + GH, 1:2], ACT.Exp))
                link(act.activation(T1[0:68, :], T1[0:68, :], ACT.Ln, bias=ones[0:68, 0:1]))
                act.sem_inc(ln_ready, 1)

            def small2(u):
                act.wait_ge(g_ready, 2 * (u + 1))
                act.activation(T4[32:32 + GH, :], T3[64:64 + GH, :], ACT.Exp).then_inc(gexp_ready, 1)
                act.copy(R[0:GH, :], T3[64:64 + GH, :]).then_inc(rows_ready, 1)
                act.activation(R[96:96 + GH, :], T4[64:64 + GH, :], ACT.Exp, scale=-1.0).then_inc(rows_ready, 1)
                act.wait_ge(cum_ready, 3 * (u + 1))
                act.dma_start(qaug[64:65, :, :], CF[0:FH, :]).then_inc(aug_landed, 16)
                act.dma_start(kaug[65:66, :, HS * u:HS * (u + 1)], CF[32:32 + FH, :]).then_inc(aug_landed, 16)

            def cols(u):
                wait_full(act, ("cols", u))
                frees(act.copy(rcols[:, :, :], bank(("cols", u))[:, 0:HT * P].rearrange("p (i m) -> p i m", i=HT)),
                      ("cols", u))

            def keep_head(u, h):
                wait_full(act, ("O", u, h))
                frees(act.copy(OT[64 * (h % 2):64 * (h % 2) + 64, h // 2, :], bank(("O", u, h))[0:FDH, 0:HS]),
                      ("O", u, h))

            def att(u, n):
                if 1 <= n <= FH * HT:
                    w = (HT * u + unit(n - 1)[1] + 1) * P
                    act.wait_ge(rsum_ready, FH * HT * u + n)
                    act.mul(FT[:, (n - 1) % 2, 0:w], FT[:, (n - 1) % 2, 0:w],
                            stat[:, 4 + (n - 1) % 2:5 + (n - 1) % 2]).then_inc(pn_ready, 1)
                if n < FH * HT:
                    act.wait_ge(smax_ready, FH * HT * u + n + 1)
                    if n >= 2:
                        wait_full(act, ("PT", u, n - 2))
                    w = (HT * u + unit(n)[1] + 1) * P
                    frees(act.activation(FT[:, n % 2, 0:w], bank(("S", u, n))[:, 0:w], ACT.Exp,
                                         bias=stat[:, n % 2:n % 2 + 1], accum_out=stat[:, 2 + n % 2:3 + n % 2]),
                          ("S", u, n))
                if 2 <= n < FH * HT + 2:
                    w = (HT * u + unit(n - 2)[1] + 1) * P
                    wait_full(act, ("PT", u, n - 2))
                    frees(act.copy(FT[:, 2 + n % 2, 0:w], bank(("PT", u, n - 2))[:, 0:w]), ("PT", u, n - 2))
                if n >= 3 and unit(n - 3)[1] == HT - 1:
                    keep_head(u, (n - 3) // HT)

            def spread(u):
                for j in range(2):
                    wait_full(act, ("bg", u, j))
                    act.copy(space[u][j], bank(("bg", u, j)))
                    frees(act.activation(space[u][2 + j], bank(("bg", u, j)), ACT.Exp), ("bg", u, j))

            def kv_(g):
                t = dn[g // HT]["A"]
                act.wait_ge(dec_in, g + 1)
                act.activation(t, t, ACT.Exp).then_inc(dec_ready, 1)

            def evac(*pairs):
                def stage(g):
                    for job, name in pairs:
                        wait_full(act, (job, g))
                        frees(act.copy(dn[g // HT][name], bank((job, g))), (job, g))
                return stage

            def os_(n):
                wait_full(act, ("o", n))
                c0 = (n % (2 * HT)) * CH
                frees(act.copy(OBT[:, :, c0:c0 + CH],
                               bank(("o", n))[:, 0:GH * CH].rearrange("p (h t) -> p h t", h=GH)), ("o", n))
                if n % (2 * HT) == 2 * HT - 1:
                    wait_free(act, ("o", n))
                    for j in range(2):
                        act.activation(dn[g_of(n)][("rv", "rw")[j]].rearrange("p (a t) -> p a t", a=2),
                                       OBT[:, 2 * j:2 * j + 2, :], ACT.Square).then_inc(osq_ready, 1)

            def g_of(n):
                return n // (2 * HT)

            def onorm(u):
                for j in range(2):
                    wait_full(act, ("oss", u, j))
                    frees(act.activation(dn[u][("u", "w")[j]], bank(("oss", u, j)), ACT.Sqrt, bias=eps[:, 0:1],
                                         scale=1.0 / P), ("oss", u, j))

            def gated(which, n):
                def stage(u, c):
                    if c >= 1 and n == 0:
                        act.wait_ge(sig_used, KD * u + c)
                    if u and c == 1 and n == 0:
                        act.wait_ge(ob_ready, GH * (u + 1))
                        act.dma_start(X[:, HT:NT, :], x_rows[:, HT:NT, :]).then_inc(x2_landed, 16)
                    wait_full(act, (which, u, c))
                    frees(act.activation(FT[:, 0, n * HS:(n + 1) * HS], bank((which, u, c))[:, 0:HS], ACT.Sigmoid,
                                         bias=gcols[:, KD * (n + 1) + c:KD * (n + 1) + c + 1]), (which, u, c))
                return stage

            def mixed(u, i):
                t = HT * u + i
                for half in range(2):
                    wait_full(act, ("mix", t, half))
                    link(act.activation(FT[:, 0, :], bank(("mix", t, half)), ACT.Square,
                                        accum_out=stat[:, 8 + 2 * t + half:9 + 2 * t + half]))
                link(act.activation(stat[:, 16 + t:17 + t], stat[:, 8 + 2 * t:9 + 2 * t], ACT.Identity,
                                    bias=stat[:, 9 + 2 * t:10 + 2 * t]))
                act.activation(stat[:, 20 + t:21 + t], stat[:, 16 + t:17 + t], ACT.Sqrt, bias=eps[:, 0:1],
                               scale=1.0 / D).then_inc(mroot_ready, 1)

            def squared(u, i):
                t = HT * u + i
                act.wait_ge(x1_ready, t + 1)
                link(act.activation(flat[:, 0:D], X[:, t, :], ACT.Square, accum_out=stat[:, 24 + t:25 + t]))
                act.activation(stat[:, 28 + t:29 + t], stat[:, 24 + t:25 + t], ACT.Sqrt, bias=eps[:, 0:1],
                               scale=1.0 / D).then_inc(xroot_ready, 1)

            def h2_turned(u, i):
                t = HT * u + i
                for half in range(2):
                    wait_full(act, ("h2T", t, half))
                    frees(act.copy(hT[:, 4 * half:4 * half + 4, i * P:(i + 1) * P],
                                   bank(("h2T", t, half)).rearrange("p (k t) -> p k t", k=4)), ("h2T", t, half))

            def qy(u, j):
                wait_full(act, ("qy", u, j))
                frees(act.copy(FT[:, 2 + j % 2, :], bank(("qy", u, j))), ("qy", u, j))

            def sc(u, j):
                wait_full(act, ("sc", u, j))
                dst = scores[u].rearrange("p (i h) k -> p i h k", i=HT)[:, :, j, :]
                frees(act.copy(dst, bank(("sc", u, j)).rearrange("p (i k) -> p i k", i=HT)), ("sc", u, j))

            def gate_exp(n, p):
                act.wait_ge(top_ready, n + 1)
                act.activation(gate[p][:, 0:TOPK], tops[p][:, :], ACT.Exp, bias=gate[p][:, TOPK:TOPK + 1],
                               accum_out=gate[p][:, TOPK + 1:TOPK + 2]).then_inc(gate_ready, 1)

            def gelu(head, p, k):
                act.wait_ge(dot_ready, head * TOPK + (k + 1))
                act.activation(acts[p][:, k:k + 1], dots[p][:, k:k + 1], ACT.Gelu).then_inc(gelu_ready, 1)

            def gelu_pair(h, k):
                if k % 2:
                    act.wait_ge(dot_ready, h * TOPK + k + 1)
                    act.activation(acts[h % 2][:, k - 1:k + 1], dots[h % 2][:, k - 1:k + 1],
                                   ACT.Gelu).then_inc(gelu_ready, 2)

            def clear():
                nothing = ones[:, 0:1].to_broadcast([P, S])
                act.mul(PS[:, BANK_Y, :], nothing, 0.0)
                act.mul(PS[:, BANK_Y + 1, :], nothing, 0.0).then_inc(y_zero, 1)

            def keep(t, static):
                if static:
                    act.wait_ge(y_whole, t + 1)
                    row = H2[:, t, :]
                else:
                    act.wait_ge(e_free, (t + 1) * (PH * TOPK) + LATER)
                    act.sem_inc(seen_act, 1)
                    row = H2[:, bass.ds(t, 1), :].rearrange("p a b -> p (a b)")
                act.copy(row[:, 0:S], PS[:, BANK_Y, :])
                act.copy(row[:, S:D], PS[:, BANK_Y + 1, :]).then_inc(y_out, 1)
                act.wait_ge(y_out, t + 1)
                if not static:
                    act.sem_inc(seen_act, 1)

            def root(t, static):
                if t if static else True:
                    act.wait_ge(fss_ready, t)
                if not static:
                    act.sem_inc(seen_act, 1)
                row = H2[:, t, :] if static else H2[:, bass.ds(t, 1), :].rearrange("p a b -> p (a b)")
                act.activation(flat[:, 0:D], row, ACT.Square, accum_out=stat[:, 32:33]).then_inc(fsq_ready, 1)
                act.wait_ge(fsq_ready, t + 1)
                if not static:
                    act.sem_inc(seen_act, 1)
                elif t:
                    act.wait_ge(fin_ready, t)
                act.activation(stat[:, 36:37], stat[:, 32:33], ACT.Sqrt, bias=eps[:, 0:1],
                               scale=1.0 / D).then_inc(fss_ready, 1)

            def sums(t):
                if t:
                    keep(t - 1, True)
                clear()

            follow({
                ("post", "norm"): norm, ("pe", "norm"): squares, ("post", "conv"): conv, ("post", "gz"): gz,
                ("post", "unit"): unit_root, ("post", "fq"): pair_rows("fq", qaug, lambda u: slice(0, HS), FDH ** -0.5),
                ("post", "fk"): pair_rows("fk", kaug, lambda u: slice(HS * u, HS * (u + 1)), 1.0),
                ("post", "fv"): fv, ("post", "small"): small, ("post", "small2"): small2, ("post", "cols"): cols, ("post", "att"): att,
                ("post", "spread"): spread, ("post", "kv"): kv_, ("post", "turn"): evac(("D", "DD"), ("E", "E")),
                ("post", "sq2"): evac(("D2", "A"), ("N2", "B")), ("post", "sq4"): evac(("D4", "DD"), ("N4", "N")),
                ("post", "sq8"): evac(("D8", "A")), ("post", "wmq"): evac(("W", "B"), ("M", "DD")),
                ("post", "m2"): evac(("M2", "A")), ("post", "tt"): evac(("TT", "ET")),
                ("post", "uw"): evac(("u", "u"), ("wT", "w")), ("post", "os"): os_, ("post", "onorm"): onorm,
                ("post", "ga"): gated("ga", 0), ("post", "gb"): gated("gb", 1), ("post", "mixed"): mixed, ("post", "squared"): squared,
                ("post", "x1"): h2_turned, ("post", "qy"): qy, ("post", "sc"): sc,
                "sums": sums, "choose_all": lambda h: gate_exp(h, h % 2),
                "choose": lambda h, part: gate_exp(h, h % 2) if part == 3 else None,
                "expert": gelu_pair,
            })
            keep(HT - 1, True)
            clear()
            for t in range(HT):
                root(t, True)
            with act.Fori(HT, NT) as t:
                with act.Fori(0, PH // 2) as b:
                    for p in range(2):
                        head = t * PH + b * 2 + p
                        for k in range(TOPK):
                            gelu(head, p, k)
                            if k == 11:
                                gate_exp(head + 1, 1 - p)
                keep(t, False)
                clear()
                root(t, False)

        @block.vector
        def _(dve):
            n_chain = [0]

            def link(ins):
                n_chain[0] += 1
                ins.then_inc(dve_chain, 1)
                dve.wait_ge(dve_chain, n_chain[0])

            dve.wait_ge(base_ready, 1)

            def ada_col(c):
                wait_full(dve, ("ada_col", c))
                for j in range(4):
                    ins = dve.scalar_tensor_tensor(out=diag[:, j, :], in0=bank(("ada_col", c))[:, j * P:(j + 1) * P],
                                                   scalar=1.0, in1=ident[:, :], op0=ALU.mult, op1=ALU.mult,
                                                   accum_out=mcol[:, 4 * c + j:4 * c + j + 1])
                frees(ins, ("ada_col", c))
                wait_free(dve, ("ada_col", c))
                if 4 * (c + 1) == N_COL:
                    dve.wait_ge(small_landed, 7 * 16)
                    link(dve.tensor_tensor(out=mcol[:, :], in0=mcol[:, :], in1=bcol[:, :], op=ALU.add))
                    dve.tensor_copy(shift1[:, :], mcol[:, 0:KD]).then_inc(mod_cols, 1)
                    dve.scalar_tensor_tensor(out=scale1[:, :], in0=mcol[:, KD:2 * KD], scalar=1.0, in1=gcols[:, 0:KD],
                                             op0=ALU.add, op1=ALU.mult).then_inc(mod_cols, 1)

            def row(c):
                if c == 0:
                    dve.wait_ge(rows_landed, 32)
                wait_full(dve, ("row", c))
                q, hs = c // 2, slice((c % 2) * S, (c % 2 + 1) * S)
                m = mods[:, q, hs]
                frees(dve.tensor_tensor(out=m, in0=bank(("row", c)), in1=m, op=ALU.add), ("row", c))
                wait_free(dve, ("row", c))
                if q != 1:
                    link(dve.scalar_tensor_tensor(out=m, in0=m, scalar=(1.0 if q == 2 else 0.0),
                                                  in1=grow[:, (q + 1) // 2, hs], op0=ALU.add, op1=ALU.mult))

            def norm(u):
                wait_free(dve, ("xsq", u))
                link(dve.reciprocal(T1, T1))
                for k in range(KD):
                    dve.tensor_tensor(out=hT[:, k, :], in0=hT[:, k, :], in1=T1, op=ALU.mult).then_inc(root_ready, 1)

            def small(u):
                dve.wait_ge(consts_ready, 1)
                wait_full(dve, ("small", u))
                frees(dve.tensor_scalar(Z[0:68, :], bank(("small", u))[0:68, 0:HS], small_b[0:68, 0:1], None,
                                        ALU.add), ("small", u))
                wait_free(dve, ("small", u))
                dve.scalar_tensor_tensor(out=T1[0:68, :], in0=Z[0:68, :], scalar=-1.0, in1=Z[0:68, :], op0=ALU.mult,
                                         op1=ALU.max).then_inc(abs_ready, 1)

            def small1(u):
                dve.wait_ge(ln_ready, u + 1)
                link(dve.tensor_scalar(T2[0:FH, :], Z[0:FH, :], 0.0, None, ALU.min))
                link(dve.tensor_tensor(out=T2[0:FH, :], in0=T2[0:FH, :], in1=T1[0:FH, :], op=ALU.subtract))
                dve.tensor_tensor_scan(CF[0:FH, :], scan_a[0:FH, :], T2[0:FH, :], carry[:, 0:1] if u else 0.0,
                                       ALU.mult, ALU.add).then_inc(cum_ready, 1)
                dve.wait_ge(cum_ready, 3 * u + 1)
                if not u:
                    link(dve.tensor_copy(carry[:, :], CF[0:FH, HS - 1:HS]))
                dve.tensor_scalar(CF[32:32 + FH, :], CF[0:FH, :], -1.0, None, ALU.mult).then_inc(cum_ready, 1)
                link(dve.tensor_scalar(T2[32:32 + GH, :], T2[32:32 + GH, :], 1.0, None, ALU.add))
                link(dve.reciprocal(R[32:32 + GH, :], T2[32:32 + GH, :]))
                a0, a1 = 64, 64 + GH
                link(dve.scalar_tensor_tensor(out=T2[a0:a1, :], in0=Z[a0:a1, :], scalar=0.0, in1=T1[a0:a1, :],
                                              op0=ALU.max, op1=ALU.add))
                link(dve.tensor_scalar(T2[a0:a1, :], T2[a0:a1, :], small_b[a0:a1, 2:3], -1.0, ALU.mult, ALU.mult))
                dve.tensor_tensor_scan(T3[a0:a1, :], scan_a[a0:a1, :], T2[a0:a1, :], 0.0, ALU.mult,
                                       ALU.add).then_inc(g_ready, 1)
                dve.wait_ge(g_ready, 2 * u + 1)
                g3 = T3[a0:a1, :].rearrange("p (n i) -> p n i", i=CH)
                dve.tensor_tensor(out=T4[a0:a1, :].rearrange("p (n i) -> p n i", i=CH), in0=g3,
                                  in1=g3[:, :, CH - 1:CH].to_broadcast([GH, HS // CH, CH]),
                                  op=ALU.subtract).then_inc(g_ready, 1)

            def small2(u):
                if not u:
                    dve.memset(kaug[64:66, :, :], 1.0)
                dve.memset(qaug[64:66, :, :], 1.0).then_inc(cum_ready, 1)
                dve.wait_ge(gexp_ready, u + 1)
                dve.tensor_tensor(out=R[64:64 + GH, :], in0=R[32:32 + GH, :], in1=T4[32:32 + GH, :],
                                  op=ALU.mult).then_inc(rows_ready, 1)

            def conv(u, c):
                wait_free(dve, ("conv", u, c))
                for d in range(1, CONV):
                    ins = dve.scalar_tensor_tensor(
                        out=gT[:, c, :], in0=pads[c % 2][:, CONV - 1 - d:CONV - 1 - d + HS],
                        scalar=convw[:, c, CONV - 1 - d:CONV - d], in1=gT[:, c, :], op0=ALU.mult, op1=ALU.add)
                    if d < CONV - 1:
                        link(ins)
                ins.then_inc(conv_ready, 1)

            def unit_norm(u, j):
                wait_free(dve, ("unit", u, j))
                r = FT[:, 2 + j % 2, :]
                link(dve.reciprocal(r, r))
                dve.scalar_tensor_tensor(out=gT[:, 2 * j:2 * j + 2, :], in0=gT[:, 2 * j:2 * j + 2, :],
                                         scalar=(P ** -0.5 if j < 2 else 1.0), in1=r.rearrange("p (a t) -> p a t", a=2),
                                         op0=ALU.mult, op1=ALU.mult).then_inc(qkn_ready, 1)

            def att(u, n):
                if 1 <= n <= FH * HT:
                    wait_free(dve, ("S", u, n - 1))
                    if FH * HT * u + n > 2:
                        dve.wait_ge(pn_ready, FH * HT * u + n - 2)
                    dve.reciprocal(stat[:, 4 + (n - 1) % 2:5 + (n - 1) % 2],
                                   stat[:, 2 + (n - 1) % 2:3 + (n - 1) % 2]).then_inc(rsum_ready, 1)
                if n < FH * HT:
                    w = (HT * u + unit(n)[1] + 1) * P
                    wait_full(dve, ("S", u, n))
                    if n >= 2:
                        wait_free(dve, ("S", u, n - 2))
                    dve.tensor_reduce(stat[:, n % 2:n % 2 + 1], bank(("S", u, n))[:, 0:w], AX.X, ALU.max,
                                      negate=True).then_inc(smax_ready, 1)

            def spread(u):
                dve.wait_ge(qkn_ready, 4 * (u + 1))
                for j in range(2):
                    wait_full(dve, ("bb", u, j))
                    frees(dve.tensor_tensor(out=space[u][4 + j], in0=bank(("bb", u, j)),
                                            in1=kT[:, 2 * j:2 * j + 2, :].rearrange("p a t -> p (a t)"), op=ALU.mult),
                          ("bb", u, j))
                for j in range(2):
                    wait_free(dve, ("bg", u, j))
                    dve.tensor_tensor(out=space[u][6 + j], in0=space[u][2 + j],
                                      in1=qT[:, 2 * j:2 * j + 2, :].rearrange("p a t -> p (a t)"),
                                      op=ALU.mult).then_inc(qd_ready, 1)
                wait_free(dve, ("cols", u))

            def kv_(g):
                u, i = divmod(g, HT)
                t = dn[u]
                tok = slice(i * P, (i + 1) * P)
                wait_full(dve, ("kt", g))
                dve.tensor_tensor(out=heads(t["rw"]), in0=heads(bank(("kt", g))), in1=bcast(rcols[:, i, 64:64 + GH], P),
                                  op=ALU.mult)
                frees(dve.tensor_tensor(out=heads(t["kd"]), in0=heads(bank(("kt", g))),
                                        in1=bcast(rcols[:, i, 96:96 + GH], P), op=ALU.mult), ("kt", g))
                wait_full(dve, ("vt", g))
                frees(dve.tensor_tensor(out=heads(t["rv"]), in0=heads(bank(("vt", g))),
                                        in1=bcast(rcols[:, i, 32:32 + GH], P), op=ALU.mult), ("vt", g))
                for h in range(GH):
                    ins = dve.tensor_scalar(t["A"][:, h * P:(h + 1) * P], Gb[u][h][:, tok], rcols[:, i, h:h + 1], 0.0,
                                            ALU.subtract, ALU.min)
                ins.then_inc(dec_in, 1)
                dve.wait_ge(dec_ready, g + 1)
                link(dve.tensor_tensor(out=heads(t["A"]), in0=heads(t["A"]), in1=mid(causal[:, :], GH), op=ALU.mult))

            def kk_(g):
                t = dn[g // HT]
                wait_full(dve, ("kk", g))
                frees(dve.tensor_tensor(out=t["B"], in0=bank(("kk", g)), in1=t["A"], op=ALU.mult), ("kk", g))
                wait_full(dve, ("qk", g))
                frees(dve.tensor_tensor(out=t["a"], in0=bank(("qk", g)), in1=t["A"], op=ALU.mult), ("qk", g))
                wait_free(dve, ("kk", g))
                dve.tensor_tensor(out=heads(t["N"]), in0=heads(t["B"]), in1=mid(near[:, :], GH),
                                  op=ALU.mult).then_inc(near_ready, 1)
                dve.tensor_tensor(out=heads(t["ET"]), in0=heads(t["B"]), in1=mid(far[:, :], GH),
                                  op=ALU.mult).then_inc(near_ready, 1)
                dve.wait_ge(near_ready, 2 * g + 2)
                dve.scalar_tensor_tensor(out=heads(t["Y"]), in0=heads(t["N"]), scalar=-1.0, in1=mid(ident[:, :], GH),
                                         op0=ALU.mult, op1=ALU.add).then_inc(y0_ready, 1)
                dve.wait_ge(y0_ready, g + 1)

            def add_to(job, name):
                def stage(g):
                    t = dn[g // HT][name]
                    wait_full(dve, (job, g))
                    frees(dve.tensor_tensor(out=t, in0=bank((job, g)), in1=t, op=ALU.add), (job, g))
                    wait_free(dve, (job, g))
                return stage

            def wmq(g):
                t = dn[g // HT]
                wait_full(dve, ("Q", g))
                frees(dve.tensor_copy(t["N"], bank(("Q", g))), ("Q", g))
                wait_free(dve, ("Q", g))
                dve.scalar_tensor_tensor(out=heads(t["C"]), in0=heads(t["N"]), scalar=-1.0, in1=mid(ident[:, :], GH),
                                         op0=ALU.mult, op1=ALU.add).then_inc(c0_ready, 1)
                dve.wait_ge(c0_ready, g + 1)

            def ws(n):
                g = n // 2
                t = dn[g // HT]
                rows = slice(CH * (n % 2), CH * (n % 2) + CH)
                wait_full(dve, ("ws", n))
                wait_free(dve, ("u", g))
                frees(dve.tensor_tensor(out=t["vn"][rows, :], in0=t["u"][rows, :], in1=bank(("ws", n))[rows, :],
                                        op=ALU.subtract), ("ws", n))

            def os_(n):
                u = n // (2 * HT)
                wait_full(dve, ("su", n))
                last = (n % (2 * HT) + 1) * CH - 1
                for h in range(GH):
                    hs = slice(h * P, (h + 1) * P)
                    ins = dve.scalar_tensor_tensor(out=St[:, hs], in0=St[:, hs], scalar=expG[u][h][:, last:last + 1],
                                                   in1=bank(("su", n))[:, hs], op0=ALU.mult, op1=ALU.add)
                frees(ins, ("su", n))

            def onorm(u):
                for j in range(2):
                    wait_free(dve, ("oss", u, j))
                    r = dn[u][("u", "w")[j]]
                    o = OBT[:, 2 * j:2 * j + 2, :].rearrange("p a t -> p (a t)")
                    link(dve.reciprocal(r, r))
                    link(dve.scalar_tensor_tensor(out=o, in0=o, scalar=gcols[:, 3 * KD:3 * KD + 1], in1=r,
                                                  op0=ALU.mult, op1=ALU.mult))
                    dve.tensor_tensor(out=o, in0=o, in1=gzT[:, 2 * j:2 * j + 2, :].rearrange("p a t -> p (a t)"),
                                      op=ALU.mult).then_inc(ob_ready, 2)

            def yab(u, c):
                wait_full(dve, ("yab", u, c))
                wait_free(dve, ("ga", u, c))
                wait_free(dve, ("gb", u, c))
                if c or u:
                    dve.wait_ge(mix_ready, KD * u + c)
                frees(dve.tensor_tensor(out=FT[:, 1, :], in0=bank(("yab", u, c)), in1=FT[:, 0, :], op=ALU.mult),
                      ("yab", u, c))
                wait_free(dve, ("yab", u, c))
                dve.sem_inc(sig_used, 1)
                dve.tensor_tensor(out=mixT[:, c, :], in0=FT[:, 1, 0:HS], in1=FT[:, 1, HS:S],
                                  op=ALU.add).then_inc(mix_ready, 1)

            def added(u, i):
                t = HT * u + i
                dve.wait_ge(mix_ready, KD * (u + 1))
                dve.wait_ge(mroot_ready, t + 1)
                r = stat[:, 40 + t:41 + t]
                link(dve.reciprocal(r, stat[:, 20 + t:21 + t]))
                for half in range(2):
                    hs = slice(half * S, (half + 1) * S)
                    frees(dve.scalar_tensor_tensor(out=H2[:, t, hs], in0=bank(("mix", t, half)), scalar=r,
                                                   in1=mods[:, 0, hs], op0=ALU.mult, op1=ALU.mult), ("mix", t, half))
                wait_free(dve, ("mix", t, 0))
                wait_free(dve, ("mix", t, 1))
                dve.wait_ge(x2_landed if u else x_landed, 16)
                dve.tensor_tensor(out=X[:, t, :], in0=X[:, t, :], in1=H2[:, t, :], op=ALU.add).then_inc(x1_ready, 1)

            def modulated(u, i):
                t = HT * u + i
                dve.wait_ge(xroot_ready, t + 1)
                r = stat[:, 16 + t:17 + t]
                link(dve.reciprocal(r, stat[:, 28 + t:29 + t]))
                link(dve.scalar_tensor_tensor(out=H2[:, t, :], in0=X[:, t, :], scalar=r, in1=mods[:, 2, :],
                                              op0=ALU.mult, op1=ALU.mult))
                dve.tensor_tensor(out=H2[:, t, :], in0=H2[:, t, :], in1=mods[:, 1, :],
                                  op=ALU.add).then_inc(h2_ready, 1)
                dve.wait_ge(h2_ready, t + 1)

            def chain(ins):
                dve.drain()

            w1, w2 = work[:, 0, :], work[:, 1, :]
            cells = [w.rearrange("p (a b) -> p a b", a=TOPK) for w in (w1, w2)]

            def choose(u, n, p, part):
                if part == 0:
                    src = scores[u][:, n, :] if isinstance(n, int) else scores[u][:, bass.ds(n, 1), :].rearrange(
                        "p a k -> p (a k)")
                    chain(dve.tensor_copy(w1, src))
                if part < 2:
                    v, ix = kv[:, part * TOPK:(part + 1) * TOPK], ki[:, part * TOPK:(part + 1) * TOPK]
                    a, z = w1[:, part * NK:(part + 1) * NK], w2[:, part * NK:(part + 1) * NK]
                    chain(dve.max(v[:, 0:8], a))
                    dve.max_index(ix[:, 0:8], v[:, 0:8], a)
                    chain(dve.match_replace(z, v[:, 0:8], a, LOWEST))
                    chain(dve.max(v[:, 8:16], z))
                    chain(dve.max_index(ix[:, 8:16], v[:, 8:16], z))
                elif part == 2:
                    chain(dve.tensor_tensor(out=cells[0], in0=bcast(kv[:, 0:TOPK], TOPK),
                                            in1=mid(kv[:, TOPK:2 * TOPK], TOPK), op=ALU.add))
                    chain(dve.max(tops[p][:, 0:8], w1))
                    dve.max_index(pos[:, 0:8], tops[p][:, 0:8], w1)
                    chain(dve.match_replace(w2, tops[p][:, 0:8], w1, LOWEST))
                    chain(dve.max(tops[p][:, 8:16], w2))
                    dve.max_index(pos[:, 8:16], tops[p][:, 8:16], w2)
                    dve.tensor_scalar(gate[p][:, TOPK:TOPK + 1], tops[p][:, 0:1], -1.0, None,
                                      ALU.mult).then_inc(top_ready, 1)
                    chain(dve.tensor_copy(kf[:, :], ki[:, :]))
                else:
                    dve.tensor_scalar(pos[:, 16:32], pos[:, 0:16], 4, None, ALU.logical_shift_right)
                    chain(dve.tensor_scalar(pos[:, 32:48], pos[:, 0:16], 15, None, ALU.bitwise_and))
                    chain(dve.tensor_copy(posf[:, 0:32], pos[:, 16:48]))
                    for s in range(2):
                        chain(dve.tensor_tensor(out=cells[0], in0=bcast(posf[:, s * TOPK:(s + 1) * TOPK], TOPK),
                                                in1=mid(iota16[:, :], TOPK), op=ALU.is_equal))
                        chain(dve.tensor_tensor(out=cells[1], in0=cells[0], in1=mid(kf[:, s * TOPK:(s + 1) * TOPK], TOPK),
                                                op=ALU.mult))
                        chain(dve.tensor_reduce(posf[:, (2 + s) * TOPK:(3 + s) * TOPK], cells[1], AX.X, ALU.add))
                    dve.scalar_tensor_tensor(out=idx_sb[p][:, :], in0=posf[:, 32:48], scalar=float(NK),
                                             in1=posf[:, 48:64], op0=ALU.mult, op1=ALU.add).then_inc(idx_ready, 1)
                    dve.drain()

            def gates(head, p):
                dve.wait_ge(gate_ready, head + 1)
                chain(dve.reciprocal(gate[p][:, TOPK + 2:TOPK + 3], gate[p][:, TOPK + 1:TOPK + 2]))
                dve.tensor_scalar(wts[p][:, :], gate[p][:, 0:TOPK], gate[p][:, TOPK + 2:TOPK + 3], None,
                                  ALU.mult)
                dve.drain()

            def weigh(head, p, k):
                dve.wait_ge(gelu_ready, head * TOPK + (k + 1))
                m = count_pe(head * TOPK + k) if isinstance(head, int) else k
                if not isinstance(head, int):
                    dve.wait_ge(e_free, head * TOPK + (k + 1 - NDG + LATER))
                elif m >= NDG:
                    dve.wait_ge(e_free, m + 1 - NDG)
                dve.tensor_scalar(diag[:, m % NDG, :], ident[:, :], acts[p][:, k:k + 1],
                                  wts[p][:, k:k + 1], ALU.mult, ALU.mult).then_inc(diag_ready, 1)

            def add_up(h, p, k):
                n = h * TOPK + k
                y = vec_sum[h // PH]
                dve.wait_ge(gelu_ready, n + 1)
                link(dve.tensor_tensor(out=acts[p][:, k:k + 1], in0=acts[p][:, k:k + 1], in1=wts[p][:, k:k + 1],
                                       op=ALU.mult))
                slot = n % V_SLOTS[0]
                dve.wait_ge(v_landed[0][slot], 16 * (n // V_SLOTS[0] + 1))
                v = v_slots[0][slot]
                if h % PH == 0 and k == VEC_K[0]:
                    ins = dve.tensor_scalar(y, v, acts[p][:, k:k + 1], None, ALU.mult)
                else:
                    ins = dve.scalar_tensor_tensor(out=y, in0=v, scalar=acts[p][:, k:k + 1], in1=y, op0=ALU.mult,
                                                   op1=ALU.add)
                ins.then_inc(vec_used, 1)
                dve.wait_ge(vec_used, n + 1 - count_pe(n + 1))

            def dot(p, k, rows, h2):
                dve.scalar_tensor_tensor(out=rows, in0=rows, scalar=1.0, in1=h2, op0=ALU.mult,
                                         op1=ALU.mult, accum_out=dots[p][:, k:k + 1]).then_inc(dot_ready, 1)

            def expert(h, k):
                n = h * TOPK + k
                slot = n % U_SLOTS[0]
                dve.wait_ge(u_landed[0][slot], 16 * (n // U_SLOTS[0] + 1))
                dot(h % 2, k, u_slots[0][slot], H2[:, h // PH, :])
                for m in behind(n, LAG[0]):
                    (weigh if added_by_pe(m) else add_up)(m // TOPK, m // TOPK % 2, m % TOPK)

            def choose_first(h, part):
                if part == 0:
                    wait_free(dve, ("sc", h // HEADS, h % PH))
                choose(h // HEADS, h % HEADS, h % 2, part)

            def choose_all(h):
                for part in range(4):
                    choose_first(h, part)

            def finish(t, at_t):
                dve.wait_ge(fss_ready, t + 1)
                chain(dve.reciprocal(stat[:, 44:45], stat[:, 36:37]))
                chain(dve.scalar_tensor_tensor(out=at_t(H2), in0=at_t(H2), scalar=stat[:, 44:45],
                                               in1=mods[:, 3, :], op0=ALU.mult, op1=ALU.mult))
                dve.tensor_tensor(out=at_t(X), in0=at_t(X), in1=at_t(H2), op=ALU.add).then_inc(fin_ready, 1)
                dve.drain()

            follow({
                ("post", "ada_col"): ada_col, ("post", "row"): row, ("post", "norm"): norm, ("post", "small"): small,
                ("post", "small1"): small1, ("post", "small2"): small2,
                ("post", "conv"): conv, ("post", "unit"): unit_norm, ("post", "att"): att, ("post", "spread"): spread,
                ("post", "kv"): kv_, ("post", "kk"): kk_, ("post", "sq4"): add_to("Y1", "Y"),
                ("post", "sq8"): add_to("Y2", "Y"), ("post", "inv"): add_to("Y3", "Y"), ("post", "wmq"): wmq,
                ("post", "c"): add_to("C", "C"), ("post", "ws"): ws, ("post", "os"): os_, ("post", "onorm"): onorm,
                ("post", "yab"): yab, ("post", "added"): added, ("post", "modulated"): modulated,
                "choose_all": choose_all, "choose": choose_first,
                "gates": lambda h: gates(h, h % 2), "expert": expert,
            })
            for j in range(N_Q // 2):
                wait_free(dve, ("sc", 1, j))
            for t in range(HT):
                finish(t, lambda tile: tile[:, t, :])
            with dve.Fori(HT, NT) as t:
                with dve.Fori(0, PH // 2) as b:
                    for p in range(2):
                        head = t * PH + b * 2 + p
                        ahead = t * PH + b * 2 + (p + 1 - HEADS)
                        gates(head, p)
                        h2 = H2[:, bass.ds(t, 1), :].rearrange("p a b -> p (a b)")
                        for k in range(TOPK):
                            slot = k % U_SLOTS[1]
                            dve.wait_ge(u_landed[1][slot],
                                        head * (16 * TOPK // U_SLOTS[1]) + (k // U_SLOTS[1] + 1) * 16
                                        - HEADS * (16 * TOPK // U_SLOTS[1]))
                            dot(p, k, u_slots[1][slot], h2)
                            if k >= LAG[1]:
                                weigh(head, p, k - LAG[1])
                            if k % 3 == 0 and k // 3 < 4:
                                choose(1, ahead % HEADS if p else ahead, 1 - p, k // 3)
                        for k in range(TOPK - LAG[1], TOPK):
                            weigh(head, p, k)
                finish(t, lambda tile: tile[:, bass.ds(t, 1), :].rearrange("p a b -> p (a b)"))

        @block.tensor
        def _(pe):
            n_w = [0]

            def weights(n, u=0):
                use = n_w[0]
                assert USES[use] == n and (use >= N_W) == (u == 1)
                n_w[0] += 1
                pe.wait_ge(w_landed[use % RING], 16 * (use // RING + 1))
                return ring[:, use % RING, :, :]

            def past(ins, first):
                if first and n_w[0] > 1:
                    ins.then_inc(w_used, 1)

            def begin(job):
                b, n = jobs[job]
                if n > 1:
                    pe.wait_ge(free[b], n - 1)
                return PS[:, b, :]

            def done(ins, job):
                ins.then_inc(full[jobs[job][0]], 1)

            def modulation(name, base):
                def stage(c):
                    if name == "ada_col" and c == 0:
                        pe.wait_ge(silub_ready, 1)
                    ps = begin((name, c))
                    for j in range(4):
                        w = weights(base + 4 * c + j)
                        for k in range(KD):
                            ins = pe.matmul(ps[:, j * P:(j + 1) * P], silu_cb[:, k, :], w[:, k, :],
                                            start=(k == 0), stop=(k == KD - 1))
                            past(ins, k == 0)
                    done(ins, (name, c))
                return stage

            def norm(u):
                pe.wait_ge(base_ready, 1)
                ps = begin(("xsq", u))
                for k in range(KD):
                    pe.wait_ge(sq_ready, KD * u + k + 1)
                    ins = pe.matmul(ps[:, 0:HS], ones[:, :], sq[:, k, :], start=(k == 0), stop=(k == KD - 1))
                done(ins, ("xsq", u))

            def small(u):
                pe.wait_ge(consts_ready, 1)
                ps = begin(("small", u))
                for k in range(KD):
                    pe.wait_ge(h_ready, KD * u + k + 1)
                    ins = pe.matmul(ps[0:68, 0:HS], wsm[:, k, :], hT[:, k, :], start=(k == 0), stop=(k == KD - 1))
                done(ins, ("small", u))

            def project(w, dst, src, ks=range(KD), first=True):
                for m, k in enumerate(ks):
                    ins = pe.matmul(dst, w[:, k, :], src[:, m, :], start=(m == 0), stop=(m == len(ks) - 1))
                    past(ins, first and m == 0)
                return ins

            def projection(name, base):
                def stage(u, c):
                    w = weights(base(c), u)
                    ps = begin((name, u, c))
                    done(project(w, ps[:, 0:HS], hT), (name, u, c))
                return stage

            def fv(u, c):
                w = weights(W_F + 8 + c, u)
                ps = begin(("fv", u, c))
                for i in range(HT):
                    for k in range(KD):
                        ins = pe.matmul(ps[:, i * P:(i + 1) * P], hT[:, k, i * P:(i + 1) * P], w[:, k, :],
                                        start=(k == 0), stop=(k == KD - 1))
                        past(ins, i == 0 and k == 0)
                done(ins, ("fv", u, c))

            def unit_norm(u, j):
                ps = begin(("unit", u, j))
                pe.wait_ge(gsq_ready, 4 * u + j + 1)
                done(pe.matmul(ps, ones[:, :], FT[:, j % 2, :], start=True, stop=True), ("unit", u, j))

            def cols(u):
                pe.wait_ge(rows_ready, 3 * (u + 1))
                ps = begin(("cols", u))
                for i in range(HT):
                    ins = pe.transpose(ps[:, i * P:(i + 1) * P], R[:, i * P:(i + 1) * P], ident[:, :])
                done(ins, ("cols", u))

            def att(u, n):
                if n == 0:
                    pe.wait_ge(aug_landed, 2 * 16 * (u + 1))
                    for c in range(4):
                        for which in ("fq", "fk", "fv"):
                            wait_free(pe, (which, u, c))
                if n < FH * HT:
                    h, i = unit(n)
                    t = HT * u + i
                    ps = begin(("S", u, n))
                    w = (t + 1) * P
                    pe.matmul(ps[:, 0:w], qaug[0:66, h, i * P:(i + 1) * P], kaug[0:66, h, 0:w], start=True, stop=False)
                    done(pe.matmul(ps[:, t * P:w], ident[:, :], fox_mask[:, :], start=False, stop=True), ("S", u, n))
                if 2 <= n < FH * HT + 2:
                    t = HT * u + unit(n - 2)[1]
                    pe.wait_ge(pn_ready, FH * HT * u + n - 1)
                    ps = begin(("PT", u, n - 2))
                    for j in range(t + 1):
                        ins = pe.transpose(ps[:, j * P:(j + 1) * P], FT[:, n % 2, j * P:(j + 1) * P], ident[:, :])
                    done(ins, ("PT", u, n - 2))
                if n >= 3:
                    h, i = unit(n - 3)
                    t = HT * u + i
                    wait_free(pe, ("PT", u, n - 3))
                    ps = PS[:, BANK_O, :] if i else begin(("O", u, h))
                    for j in range(t + 1):
                        ins = pe.matmul(ps[0:FDH, i * P:(i + 1) * P], Vr[:, j, h * FDH:(h + 1) * FDH],
                                        FT[:, 2 + (n - 3) % 2, j * P:(j + 1) * P], start=(j == 0), stop=(j == t))
                    if i == HT - 1:
                        done(ins, ("O", u, h))

            def spread(u):
                for job, b0 in (("bg", 0), ("bb", 32)):
                    for j in range(2):
                        ps = begin((job, u, j))
                        for a in range(2):
                            h = 2 * j + a
                            pick = ident[b0:b0 + GH, b0 + h:b0 + h + 1].to_broadcast([GH, P])
                            ins = pe.matmul(ps[:, a * HS:(a + 1) * HS], pick, R[b0:b0 + GH, :], start=True, stop=True)
                        done(ins, (job, u, j))
                pe.wait_ge(qkn_ready, 4 * (u + 1))
                pe.wait_ge(conv_silu, N_CONV * (u + 1))

            def four(job, g, lhs, rhs):
                ps = begin((job, g))
                for h in range(GH):
                    ins = pe.matmul(ps[:, h * P:(h + 1) * P], lhs(h), rhs(h), start=True, stop=True)
                done(ins, (job, g))

            def turn(job, g, src):
                ps = begin((job, g))
                for h in range(GH):
                    ins = pe.transpose(ps[:, h * P:(h + 1) * P], src(h), ident[:, :])
                done(ins, (job, g))

            def of(g, name):
                return lambda h: dn[g // HT][name][:, h * P:(h + 1) * P]

            def at(tile, g):
                i = g % HT
                return lambda h: (tile[h] if isinstance(tile, list) else tile[:, h, :])[:, i * P:(i + 1) * P]

            def kv_(g):
                turn("kt", g, at(kT, g))
                turn("vt", g, at(vT, g))

            def kk_(g):
                u = g // HT
                if g % HT == 0:
                    for j in range(2):
                        wait_free(pe, ("bb", u, j))
                    pe.wait_ge(qd_ready, 2 * (u + 1))
                four("kk", g, at(kT, g), at(kbT[u], g))
                four("qk", g, at(kT, g), at(qT, g))

            def turned(g):
                pe.wait_ge(near_ready, 2 * g + 2)
                turn("D", g, of(g, "N"))
                turn("E", g, of(g, "ET"))

            def sq2(g):
                wait_free(pe, ("D", g))
                four("D2", g, of(g, "N"), of(g, "DD"))
                four("N2", g, of(g, "DD"), of(g, "N"))

            def sq4(g):
                wait_free(pe, ("D2", g))
                pe.wait_ge(y0_ready, g + 1)
                four("Y1", g, of(g, "A"), of(g, "Y"))
                wait_free(pe, ("N2", g))
                four("D4", g, of(g, "B"), of(g, "A"))
                four("N4", g, of(g, "A"), of(g, "B"))

            def sq8(g):
                wait_free(pe, ("D4", g))
                wait_free(pe, ("Y1", g))
                four("Y2", g, of(g, "DD"), of(g, "Y"))
                wait_free(pe, ("N4", g))
                four("D8", g, of(g, "N"), of(g, "DD"))

            def inv(g):
                wait_free(pe, ("D8", g))
                wait_free(pe, ("Y2", g))
                four("Y3", g, of(g, "A"), of(g, "Y"))

            def wmq(g):
                wait_free(pe, ("Y3", g))
                turn("W", g, of(g, "Y"))
                wait_free(pe, ("E", g))
                four("M", g, of(g, "Y"), of(g, "E"))
                four("Q", g, of(g, "E"), of(g, "Y"))

            def m2(g):
                wait_free(pe, ("M", g))
                wait_free(pe, ("Q", g))
                four("M2", g, of(g, "N"), of(g, "DD"))

            def c_(g):
                wait_free(pe, ("M2", g))
                pe.wait_ge(c0_ready, g + 1)
                four("C", g, of(g, "A"), of(g, "C"))

            def tt(g):
                wait_free(pe, ("C", g))
                wait_free(pe, ("W", g))
                four("TT", g, of(g, "B"), of(g, "C"))

            def uw(g):
                for job in ("TT", "vt", "kt"):
                    wait_free(pe, (job, g))
                four("u", g, of(g, "ET"), of(g, "rv"))
                four("wT", g, of(g, "rw"), of(g, "ET"))

            def ws(n):
                g = n // 2
                b0 = CH * (n % 2)
                wait_free(pe, ("wT", g))
                wait_free(pe, ("qk", g))
                if n:
                    wait_free(pe, ("su", n - 1))
                ps = begin(("ws", n))
                for h in range(GH):
                    hs = slice(h * P, (h + 1) * P)
                    ins = pe.matmul(ps[b0:b0 + CH, hs], dn[g // HT]["w"][:, h * P + b0:h * P + b0 + CH], St[:, hs],
                                    start=True, stop=True)
                done(ins, ("ws", n))

            def os_(n):
                g = n // 2
                u = g // HT
                t = dn[u]
                b0 = CH * (n % 2)
                c0 = (n % (2 * HT)) * CH
                rows = slice(b0, b0 + CH)
                wait_free(pe, ("ws", n))
                ps = begin(("o", n))
                for h in range(GH):
                    hs = slice(h * P, (h + 1) * P)
                    dst = ps[:, h * CH:(h + 1) * CH]
                    pe.matmul(dst, St[:, hs], qdT[u][h][:, c0:c0 + CH], start=True, stop=False)
                    ins = pe.matmul(dst, t["vn"][rows, hs], t["a"][rows, h * P + b0:h * P + b0 + CH],
                                    start=False, stop=True)
                done(ins, ("o", n))
                ps = begin(("su", n))
                for h in range(GH):
                    hs = slice(h * P, (h + 1) * P)
                    ins = pe.matmul(ps[:, hs], t["kd"][rows, hs], t["vn"][rows, hs], start=True, stop=True)
                done(ins, ("su", n))

            def onorm(u):
                for j in range(2):
                    pe.wait_ge(osq_ready, 2 * u + j + 1)
                    ps = begin(("oss", u, j))
                    done(pe.matmul(ps, ones[:, :], dn[u][("rv", "rw")[j]], start=True, stop=True), ("oss", u, j))

            def yab(u, c):
                if c == 0:
                    for h in range(FH):
                        wait_free(pe, ("O", u, h))
                    pe.wait_ge(ob_ready, GH * (u + 1))
                w = weights(W_MIX + 3 * c + 2, u)
                ps = begin(("yab", u, c))
                project(w, ps[:, 0:HS], OT, range(4))
                done(project(w, ps[:, HS:S], OBT, range(4, 8), first=False), ("yab", u, c))

            def out_(u, half, c):
                if half == 0 and c == 0:
                    pe.wait_ge(mix_ready, KD * (u + 1))
                w = weights(W_OUT + 4 * half + c, u)
                for i in range(HT):
                    job = ("mix", HT * u + i, half)
                    ps = begin(job) if c == 0 else bank(job)
                    for k in range(KD):
                        ins = pe.matmul(ps[:, c * P:(c + 1) * P], mixT[:, k, i * P:(i + 1) * P], w[:, k, :],
                                        start=(k == 0), stop=(k == KD - 1))
                        past(ins, i == 0 and k == 0)
                    if c == 3:
                        done(ins, job)

            def x1(u, i):
                t = HT * u + i
                pe.wait_ge(h2_ready, t + 1)
                for half in range(2):
                    ps = begin(("h2T", t, half))
                    for k in range(4):
                        ins = pe.transpose(ps[:, k * P:(k + 1) * P],
                                           H2[:, t, half * S + k * P:half * S + (k + 1) * P], ident[:, :])
                    done(ins, ("h2T", t, half))

            def qy(u, j):
                if j == 0:
                    pe.wait_ge(keys_landed, 16)
                    for i in range(HT):
                        for half in range(2):
                            wait_free(pe, ("h2T", HT * u + i, half))
                ps = begin(("qy", u, j))
                for s in range(2):
                    ins = project(weights(W_Q + 2 * j + s, u), ps[:, s * HS:(s + 1) * HS], hT)
                done(ins, ("qy", u, j))

            def sc(u, j):
                wait_free(pe, ("qy", u, j))
                ps = begin(("sc", u, j))
                for i in range(HT):
                    for s in range(2):
                        ins = pe.matmul(ps[:, (2 * i + s) * NK:(2 * i + s + 1) * NK],
                                        FT[:, 2 + j % 2, s * HS + i * P:s * HS + (i + 1) * P], keys[:, s, :],
                                        start=True, stop=True)
                done(ins, ("sc", u, j))

            def weighted(m_done, tile, rows):
                pe.wait_ge(diag_ready, m_done)
                for half in range(2):
                    ins = pe.matmul(PS[:, BANK_Y + half, :], diag[:, tile, :], rows[:, half * S:(half + 1) * S],
                                    start=False, stop=False, skip_group_check=True)
                ins.then_inc(e_free, 1)

            def expert(h, k):
                n = h * TOPK + k
                for m in behind(n, PE_LAG):
                    if m % (PH * TOPK) == 0:
                        pe.wait_ge(y_zero, m // (PH * TOPK) + 1)
                    if added_by_pe(m):
                        slot = m % V_SLOTS[0]
                        pe.wait_ge(v_landed[0][slot], 16 * (m // V_SLOTS[0] + 1))
                        weighted(count_pe(m) + 1, count_pe(m) % NDG, v_slots[0][slot])
                if h % PH == PH - 1 and k == TOPK - 1:
                    pe.wait_ge(vec_used, n + 1 - count_pe(n + 1))
                    for half in range(2):
                        ins = pe.matmul(PS[:, BANK_Y + half, :], ident[:, :],
                                        vec_sum[h // PH][:, half * S:(half + 1) * S],
                                        start=False, stop=False, skip_group_check=True)
                    ins.then_inc(y_whole, 1)

            follow({
                ("pe", "ada_col"): modulation("ada_col", W_COL), ("pe", "row"): modulation("row", W_ROW),
                ("pe", "norm"): norm, ("pe", "small"): small,
                ("pe", "conv"): projection("conv", lambda c: W_CONV + c), ("pe", "gz"): projection("gz", lambda c: W_GZ + c),
                ("pe", "unit"): unit_norm, ("pe", "fq"): projection("fq", lambda c: W_F + c),
                ("pe", "fk"): projection("fk", lambda c: W_F + 4 + c), ("pe", "fv"): fv, ("pe", "cols"): cols,
                ("pe", "att"): att, ("pe", "spread"): spread, ("pe", "kv"): kv_, ("pe", "kk"): kk_,
                ("pe", "turn"): turned, ("pe", "sq2"): sq2, ("pe", "sq4"): sq4, ("pe", "sq8"): sq8, ("pe", "inv"): inv,
                ("pe", "wmq"): wmq, ("pe", "m2"): m2, ("pe", "c"): c_, ("pe", "tt"): tt, ("pe", "uw"): uw,
                ("pe", "ws"): ws, ("pe", "os"): os_, ("pe", "onorm"): onorm,
                ("pe", "ga"): projection("ga", lambda c: W_MIX + 3 * c),
                ("pe", "gb"): projection("gb", lambda c: W_MIX + 3 * c + 1), ("pe", "yab"): yab, ("pe", "out"): out_,
                ("pe", "x1"): x1, ("pe", "qy"): qy, ("pe", "sc"): sc,
                "expert": expert,
            })
            assert n_w[0] == len(USES)
            with pe.Fori(HT, NT) as t:
                pe.wait_ge(y_zero, t + 1)
                pe.sem_inc(seen_pe, 1)
                with pe.Fori(0, PH // 2) as b:
                    for p in range(2):
                        for k in range(TOPK):
                            head = t * PH + b * 2 + p
                            slot = k % V_SLOTS[1]
                            pe.wait_ge(v_landed[1][slot],
                                       head * (16 * TOPK // V_SLOTS[1]) + (k // V_SLOTS[1] + 1) * 16
                                       - HEADS * (16 * TOPK // V_SLOTS[1]))
                            weighted(head * TOPK + (k + 1 + LATER), k % NDG, v_slots[1][slot])


def kernel(x, c, w_ada, b_ada, g_pre_mix, g_post_mix, w_in, b_fgate, fox_w_o, conv_w, a_log, dt_bias,
           gdn_norm_w, gdn_w_o, b_branch_gate, w_out, g_pre_ffn, g_post_ffn, peer_w_query, peer_keys1,
           peer_keys2, peer_u, peer_v):
    import concourse.bacc as bacc
    from concourse.bass_utils import run_bass_kernel_spmd as run

    def tiles(m):
        m = np.asarray(m)
        k, n = m.shape
        return m.reshape(k // P, P, n // P, P).transpose(2, 1, 0, 3).reshape(n // P, P, k)

    def cols(v):
        return np.asarray(v).reshape(-1, P).T

    wi = np.asarray(w_in)[0]
    cut = np.cumsum([0, 512, 512, 512, FH, 512, 512, 512, 512, GH, GH, D, D])
    fq, fk, fv, f, gq, gk, gv, gz, beta, decay, ga, gb = (wi[:, a:b] for a, b in zip(cut[:-1], cut[1:]))
    ada = np.asarray(w_ada)[0]
    mix = np.stack([tiles(ga), tiles(gb), np.concatenate([tiles(fox_w_o[0]), tiles(gdn_w_o[0])], axis=2)], axis=1)
    w_tiles = np.concatenate([
        tiles(ada[:, 0:2 * D]), tiles(gq), tiles(gk), tiles(gv), tiles(gz), tiles(fq), tiles(fk), tiles(fv),
        tiles(ada[:, 2 * D:6 * D]), mix.reshape(3 * KD, P, D), tiles(w_out[0]), tiles(peer_w_query[0])], axis=0)
    small = np.concatenate([f, beta, decay], axis=1).reshape(KD, P, 16).transpose(1, 0, 2).reshape(P, KD * 16)
    bias = np.asarray(b_ada)[0]
    arrays = {
        "x_rows": np.asarray(x)[0].reshape(NT, P, D).transpose(1, 0, 2),
        "x_cols": np.asarray(x)[0].T.reshape(KD, P, 2, HS).transpose(2, 1, 0, 3),
        "c_cols": cols(c),
        "w_tiles": w_tiles,
        "w_small": small,
        "b_small": np.concatenate([np.asarray(b_fgate)[0], np.asarray(dt_bias)[0], np.asarray(a_log)[0]]).reshape(-1, 1),
        "ada_cols": cols(bias[0:2 * D]),
        "ada_rows": bias[2 * D:6 * D],
        "gains_cols": np.concatenate([cols(g_pre_mix), cols(np.asarray(b_branch_gate)[0, 0]),
                                      cols(np.asarray(b_branch_gate)[0, 1]), cols(gdn_norm_w)], axis=1),
        "gain_rows": np.concatenate([np.asarray(g_post_mix)[0], np.asarray(g_pre_ffn)[0], np.asarray(g_post_ffn)[0]]),
        "conv_cols": np.asarray(conv_w)[0].T.reshape(N_CONV, P, CONV).transpose(1, 0, 2),
        "keys_t": np.stack([np.asarray(peer_keys1)[0].T, np.asarray(peer_keys2)[0].T], axis=1),
        "peer_u": np.asarray(peer_u)[0],
        "peer_v": np.asarray(peer_v)[0],
    }
    nc = bacc.Bacc("TRN2", target_bir_lowering=False, num_devices=1)
    fed, args = {}, {}
    for name, a in arrays.items():
        a = np.ascontiguousarray(a)
        fed[f"in_{name}"] = a
        args[name] = nc.dram_tensor(f"in_{name}", a.shape, mybir.dt.from_np(a.dtype), kind="ExternalInput").ap()
    out = nc.dram_tensor("out_x", (NT, P, D), F32, kind="ExternalOutput").ap()
    hybrid_block(nc, out=out, **args)
    return run(nc, [fed], core_ids=[0]).results[0]["out_x"].reshape(1, S, D)
```
